# Optimizing a Trainium2 kernel written in Bass

```python
import math
import jax, jax.numpy as jnp
from jax import lax
import numpy as np
import jax
import jax.numpy as jnp

D_MODEL = 1024
BATCH = 1
SEQ = 256
DEPTH = 1

M_HEADS = 4
M_HEAD_DIM = 128
M_WIDTH = M_HEADS * M_HEAD_DIM
M_CHUNK = 128
CONV_WIDTH = 4
N_HEADS = 8
N_KV_GROUPS = 2
N_REP = N_HEADS // N_KV_GROUPS
N_HEAD_DIM = 64
N_WIDTH = N_HEADS * N_HEAD_DIM
N_KV_WIDTH = N_KV_GROUPS * N_HEAD_DIM
CMP_BLOCK = 32
CMP_STRIDE = 16
CMP_HIDDEN = 2 * N_HEAD_DIM
SEL_BLOCK = 64
SEL_TOPK = 16
WINDOW = 512
NSA_Q_BLOCK = 64
REL_BUCKETS = 32
REL_MAX_DIST = 1024
N_BRANCH = 2
BRANCH_WIDTH = 512
D_FF = -(-8 * D_MODEL // (3 * 256)) * 256
RMS_EPS = 1e-6
BIG = 1e9

IN_SIZES = (M_WIDTH, M_WIDTH, M_WIDTH, M_WIDTH, M_HEADS, M_HEADS,
            N_WIDTH, 6 * N_KV_WIDTH, 3 * N_HEADS, N_BRANCH * D_MODEL)
D_IN_TOTAL = sum(IN_SIZES)


def rms_norm(x, g):
    x32 = x.astype(jnp.float32)
    y = x32 * lax.rsqrt(jnp.mean(x32 * x32, axis=-1, keepdims=True) + RMS_EPS)
    return (y * g.astype(jnp.float32)).astype(x.dtype)

def split_columns(p, sizes):
    out = []
    start = 0
    for s in sizes:
        out.append(p[..., start:start + s])
        start += s
    return out

def causal_depthwise_conv(x, w):
    T = x.shape[1]
    xp = jnp.pad(x, ((0, 0), (CONV_WIDTH - 1, 0), (0, 0)))
    return sum(w[j] * xp[:, j:j + T] for j in range(CONV_WIDTH))

def rel_bucket(dist):
    n = jnp.maximum(dist, 0)
    max_exact = REL_BUCKETS // 2
    nf = jnp.maximum(n, 1).astype(jnp.float32)
    large = max_exact + (jnp.log(nf / max_exact) / math.log(REL_MAX_DIST / max_exact)
                         * (REL_BUCKETS - max_exact)).astype(jnp.int32)
    large = jnp.minimum(large, REL_BUCKETS - 1)
    return jnp.where(n < max_exact, n, large)

def masked_softmax(logits, mask):
    logits = logits.astype(jnp.float32)
    z = jnp.where(mask, logits, -1e30)
    z = z - jnp.max(z, axis=-1, keepdims=True)
    e = jnp.where(mask, jnp.exp(z), 0.0)
    return e / jnp.maximum(jnp.sum(e, axis=-1, keepdims=True), 1e-30)

def mlstm_chunkwise(q, k, v, i_pre, f_pre):
    B, H, T, dk = q.shape
    dv = v.shape[-1]
    L = M_CHUNK
    nc = T // L
    qc = q.reshape(B, H, nc, L, dk)
    kc = k.reshape(B, H, nc, L, dk)
    vc = v.reshape(B, H, nc, L, dv)
    ic = i_pre.reshape(B, H, nc, L)
    bc = jnp.cumsum(jax.nn.log_sigmoid(f_pre).reshape(B, H, nc, L), axis=-1)
    b_last = bc[..., -1]
    a = b_last[..., None] - bc + ic

    def step(carry, inp):
        C, n, m = carry
        k_j, v_j, a_j, bl = inp
        m_new = jnp.maximum(bl + m, jnp.max(a_j, axis=-1))
        decay = jnp.exp(bl + m - m_new)
        w = jnp.exp(a_j - m_new[..., None])
        C_new = decay[..., None, None] * C + jnp.einsum('bhl,bhlk,bhlv->bhkv', w, k_j, v_j)
        n_new = decay[..., None] * n + jnp.einsum('bhl,bhlk->bhk', w, k_j)
        return (C_new, n_new, m_new), (C, n, m)

    init = (jnp.zeros((B, H, dk, dv), jnp.float32), jnp.zeros((B, H, dk), jnp.float32),
            jnp.zeros((B, H), jnp.float32))
    xs = (jnp.moveaxis(kc, 2, 0), jnp.moveaxis(vc, 2, 0), jnp.moveaxis(a, 2, 0), jnp.moveaxis(b_last, 2, 0))
    _, (C_prev, n_prev, m_prev) = lax.scan(step, init, xs)
    C_prev = jnp.moveaxis(C_prev, 0, 2)
    n_prev = jnp.moveaxis(n_prev, 0, 2)
    m_prev = jnp.moveaxis(m_prev, 0, 2)

    causal = jnp.tril(jnp.ones((L, L), dtype=bool))
    log_d = jnp.where(causal, bc[..., :, None] - bc[..., None, :] + ic[..., None, :], -jnp.inf)
    log_inter = bc + m_prev[..., None]
    m_i = jnp.maximum(jnp.max(log_d, axis=-1), log_inter)
    P = jnp.exp(log_d - m_i[..., None]) * jnp.einsum('bhcid,bhcjd->bhcij', qc, kc)
    s_inter = jnp.exp(log_inter - m_i)
    num = (jnp.einsum('bhcij,bhcjv->bhciv', P, vc)
           + s_inter[..., None] * jnp.einsum('bhcid,bhcdv->bhciv', qc, C_prev))
    den = jnp.sum(P, axis=-1) + s_inter * jnp.einsum('bhcid,bhcd->bhci', qc, n_prev)
    h = num / jnp.maximum(jnp.abs(den), jnp.exp(-m_i))[..., None]
    return h.reshape(B, H, T, dv)

def mlstm_mixer(q_pre, k_pre, v, o_pre, i_pre, f_pre, b_fgate, conv_w, g_head):
    B, T, _ = q_pre.shape
    qk = jax.nn.silu(causal_depthwise_conv(jnp.concatenate([q_pre, k_pre], axis=-1), conv_w))
    to_heads = lambda t: t.reshape(B, T, M_HEADS, M_HEAD_DIM).transpose(0, 2, 1, 3).astype(jnp.float32)
    q = to_heads(qk[..., :M_WIDTH])
    k = to_heads(qk[..., M_WIDTH:]) * (M_HEAD_DIM ** -0.5)
    vh = to_heads(v)
    ig = i_pre.astype(jnp.float32).transpose(0, 2, 1)
    fg = (f_pre.astype(jnp.float32) + b_fgate.astype(jnp.float32)).transpose(0, 2, 1)
    hh = mlstm_chunkwise(q, k, vh, ig, fg)
    hh = (hh * lax.rsqrt(jnp.mean(hh * hh, axis=-1, keepdims=True) + RMS_EPS)
          * g_head.astype(jnp.float32).reshape(M_HEADS, 1, M_HEAD_DIM))
    hh = hh.transpose(0, 2, 1, 3).reshape(B, T, M_WIDTH)
    return (jax.nn.sigmoid(o_pre.astype(jnp.float32)) * hh).astype(q_pre.dtype)

def nsa_mixer(q_in, kv_in, gate_in, pe_cmp, w_cmp1, w_cmp2, rel_bias):
    B, T, _ = q_in.shape
    G, R, dh, Q = N_KV_GROUPS, N_REP, N_HEAD_DIM, NSA_Q_BLOCK
    q = q_in.reshape(B, T, G, R, dh).transpose(0, 2, 3, 1, 4) * (dh ** -0.5)
    kv = kv_in.reshape(B, T, 6, G, dh).transpose(2, 0, 3, 1, 4)
    k_c, v_c, k_s, v_s, k_w, v_w = kv[0], kv[1], kv[2], kv[3], kv[4], kv[5]
    gates = jax.nn.sigmoid(gate_in.astype(jnp.float32).reshape(B, T, G, R, 3).transpose(0, 2, 3, 1, 4))

    n_cmp = (T - CMP_BLOCK) // CMP_STRIDE + 1
    cmp_start = jnp.arange(n_cmp) * CMP_STRIDE
    cmp_idx = cmp_start[:, None] + jnp.arange(CMP_BLOCK)[None, :]
    cmp_end = cmp_start + CMP_BLOCK - 1

    def compress(kx, j):
        blk = kx[:, :, cmp_idx] + pe_cmp[j]
        flat = blk.reshape(B, G, n_cmp, CMP_BLOCK * dh)
        return jax.nn.silu(flat @ w_cmp1[j]) @ w_cmp2[j]

    kc_ = compress(k_c, 0)
    vc_ = compress(v_c, 1)

    n_slc = T // SEL_BLOCK
    n_top = min(SEL_TOPK, n_slc)
    k_sb = k_s.reshape(B, G, n_slc, SEL_BLOCK, dh)
    v_sb = v_s.reshape(B, G, n_slc, SEL_BLOCK, dh)
    slc_start = jnp.arange(n_slc) * SEL_BLOCK
    overlap = (jnp.clip(jnp.minimum(cmp_start[:, None] + CMP_BLOCK, slc_start[None, :] + SEL_BLOCK)
                        - jnp.maximum(cmp_start[:, None], slc_start[None, :]), 0)
               / CMP_STRIDE).astype(jnp.float32)

    k_wp = jnp.pad(k_w, ((0, 0), (0, 0), (WINDOW, 0), (0, 0)))
    v_wp = jnp.pad(v_w, ((0, 0), (0, 0), (WINDOW, 0), (0, 0)))

    table = rel_bias.astype(jnp.float32).T.reshape(G, R, REL_BUCKETS)
    g_ix = jnp.arange(G)[None, :, None, None, None]
    r_ix = jnp.arange(R)[None, None, :, None, None]
    gather_blocks = jax.vmap(jax.vmap(lambda blk, ix: blk[ix]))

    def block(i):
        qs = i * Q
        t = qs + jnp.arange(Q)
        qb = lax.dynamic_slice_in_dim(q, qs, Q, axis=3)
        lc = (jnp.einsum('bgrqd,bgcd->bgrqc', qb, kc_).astype(jnp.float32)
              + table[:, :, rel_bucket(t[:, None] - cmp_end[None, :])])
        p_c = masked_softmax(lc, cmp_end[None, :] <= t[:, None])
        o_c = jnp.einsum('bgrqc,bgcd->bgrqd', p_c, vc_.astype(jnp.float32))
        imp = jnp.einsum('bgrqc,cj->bgqj', p_c, overlap)
        cur = t // SEL_BLOCK
        jb = jnp.arange(n_slc)[None, :]
        forced = (jb == 0) | (jb == cur[:, None]) | (jb == cur[:, None] - 1)
        eligible = jb * SEL_BLOCK <= t[:, None]
        score = jnp.where(eligible, jnp.where(forced, BIG, imp), -BIG)
        top_val, top_idx = lax.top_k(score, n_top)
        N = n_top * SEL_BLOCK
        k_g = gather_blocks(k_sb, top_idx).reshape(B, G, Q, N, dh)
        v_g = gather_blocks(v_sb, top_idx).reshape(B, G, Q, N, dh)
        pos_u = top_idx[..., None] * SEL_BLOCK + jnp.arange(SEL_BLOCK)
        mask_u = (top_val > -BIG / 2)[..., None] & (pos_u <= t[:, None, None])
        pos = pos_u.reshape(B, G, Q, N)
        mask_s = mask_u.reshape(B, G, Q, N)
        bias_s = table[g_ix, r_ix, rel_bucket(t[:, None] - pos)[:, :, None]]
        ls = jnp.einsum('bgrqd,bgqnd->bgrqn', qb, k_g).astype(jnp.float32) + bias_s
        p_s = masked_softmax(ls, mask_s[:, :, None])
        o_s = jnp.einsum('bgrqn,bgqnd->bgrqd', p_s, v_g.astype(jnp.float32))
        span = Q + WINDOW
        k_wb = lax.dynamic_slice_in_dim(k_wp, qs, span, axis=2)
        v_wb = lax.dynamic_slice_in_dim(v_wp, qs, span, axis=2)
        pos_w = qs - WINDOW + jnp.arange(span)
        dist = t[:, None] - pos_w[None, :]
        mask_w = (pos_w[None, :] >= 0) & (dist >= 0) & (dist < WINDOW)
        lw = jnp.einsum('bgrqd,bgkd->bgrqk', qb, k_wb).astype(jnp.float32) + table[:, :, rel_bucket(dist)]
        p_w = masked_softmax(lw, mask_w)
        o_w = jnp.einsum('bgrqk,bgkd->bgrqd', p_w, v_wb.astype(jnp.float32))
        gb = lax.dynamic_slice_in_dim(gates, qs, Q, axis=3)
        return gb[..., 0:1] * o_c + gb[..., 1:2] * o_s + gb[..., 2:3] * o_w

    out = lax.map(block, jnp.arange(T // Q))
    out = out.transpose(1, 0, 4, 2, 3, 5).reshape(B, T, N_WIDTH)
    return out.astype(q_in.dtype)

def first_inputs(seed: int = 0) -> dict:
    key = jax.random.key(seed)
    ks = jax.random.split(key, 20)
    nrm = lambda k, shape, scale: jax.random.normal(k, shape, jnp.float32) * scale
    x = nrm(ks[0], (BATCH, SEQ, D_MODEL), 1.0)
    g_norm_mix = 1.0 + nrm(ks[1], (DEPTH, D_MODEL), 0.02)
    w_in = nrm(ks[2], (DEPTH, D_MODEL, D_IN_TOTAL), D_MODEL ** -0.5)
    b_in = nrm(ks[3], (DEPTH, D_IN_TOTAL), 0.02)
    b_fgate = jnp.linspace(3.0, 6.0, M_HEADS, dtype=jnp.float32)[None, :] + nrm(ks[4], (DEPTH, M_HEADS), 0.1)
    conv_qk = nrm(ks[5], (DEPTH, CONV_WIDTH, 2 * M_WIDTH), CONV_WIDTH ** -0.5)
    g_mlstm_head = 1.0 + nrm(ks[6], (DEPTH, M_WIDTH), 0.02)
    pe_cmp = nrm(ks[7], (DEPTH, 2, CMP_BLOCK, N_HEAD_DIM), 0.1)
    w_cmp1 = nrm(ks[8], (DEPTH, 2, CMP_BLOCK * N_HEAD_DIM, CMP_HIDDEN), (CMP_BLOCK * N_HEAD_DIM) ** -0.5)
    w_cmp2 = nrm(ks[9], (DEPTH, 2, CMP_HIDDEN, N_HEAD_DIM), CMP_HIDDEN ** -0.5)
    rel_bias = nrm(ks[10], (REL_BUCKETS, N_HEADS), 0.5)
    w_branch = nrm(ks[11], (DEPTH, N_BRANCH, BRANCH_WIDTH, D_MODEL), BRANCH_WIDTH ** -0.5)
    w_out = nrm(ks[12], (DEPTH, D_MODEL, D_MODEL), D_MODEL ** -0.5)
    g_norm_ffn = 1.0 + nrm(ks[13], (DEPTH, D_MODEL), 0.02)
    w_gate = nrm(ks[14], (DEPTH, D_MODEL, D_FF), D_MODEL ** -0.5)
    w_up = nrm(ks[15], (DEPTH, D_MODEL, D_FF), D_MODEL ** -0.5)
    w_down = nrm(ks[16], (DEPTH, D_FF, D_MODEL), D_FF ** -0.5)
    g_final = 1.0 + nrm(ks[17], (D_MODEL,), 0.02)
    return {'x': x, 'g_norm_mix': g_norm_mix, 'w_in': w_in, 'b_in': b_in, 'b_fgate': b_fgate,
            'conv_qk': conv_qk, 'g_mlstm_head': g_mlstm_head, 'pe_cmp': pe_cmp, 'w_cmp1': w_cmp1,
            'w_cmp2': w_cmp2, 'rel_bias': rel_bias, 'w_branch': w_branch, 'w_out': w_out,
            'g_norm_ffn': g_norm_ffn, 'w_gate': w_gate, 'w_up': w_up, 'w_down': w_down, 'g_final': g_final}

def first_block(x, g_norm_mix, w_in, b_in, b_fgate, conv_qk, g_mlstm_head, pe_cmp, w_cmp1, w_cmp2,
              rel_bias, w_branch, w_out, g_norm_ffn, w_gate, w_up, w_down, g_final):
    B, T, _ = x.shape
    h = x
    for l in range(DEPTH):
        u = rms_norm(h, g_norm_mix[l])
        proj = jnp.einsum('btd,de->bte', u, w_in[l]) + b_in[l]
        mq, mk, mv, mo, mi, mf, nq, nkv, ngate, merge = split_columns(proj, IN_SIZES)
        y_m = mlstm_mixer(mq, mk, mv, mo, mi, mf, b_fgate[l], conv_qk[l], g_mlstm_head[l])
        y_n = nsa_mixer(nq, nkv, ngate, pe_cmp[l], w_cmp1[l], w_cmp2[l], rel_bias)
        ys = jnp.stack([y_m, y_n], axis=2)
        branch = jnp.einsum('btnw,nwd->btnd', ys, w_branch[l])
        gates = jax.nn.sigmoid(merge.reshape(B, T, N_BRANCH, D_MODEL))
        mixed = jnp.sum(gates * branch, axis=2)
        h = h + mixed @ w_out[l]
        f = rms_norm(h, g_norm_ffn[l])
        h = h + (jax.nn.silu(f @ w_gate[l]) * (f @ w_up[l])) @ w_down[l]
    return rms_norm(h, g_final)


MEM_LEN = 256
EPS = 1e-6

GLA_HEADS = 4
GLA_DK = D_MODEL // 8
GLA_DV = D_MODEL // 4
GLA_GATE_RANK = 16
GLA_GATE_TEMP = 16.0
GLA_CHUNK = 64

DSA_HEADS = 8
DSA_KV_HEADS = 2
DSA_HEAD_DIM = 128
IDX_HEADS = 8
IDX_DIM = 64
IDX_TOPK_MAX = 256
Q_BLOCK = 128

MEM_HEADS = 4
MEM_HEAD_DIM = D_MODEL // 4

N_GROUPS = 4
EXPERTS_PER_GROUP = 4
N_EXPERTS = N_GROUPS * EXPERTS_PER_GROUP
EXPERT_TOPK = 2
D_EXPERT = D_MODEL // 4

N_BRANCH_2 = 3
IN_SPLITS = (
    GLA_HEADS * GLA_DK,
    GLA_HEADS * GLA_DK,
    GLA_HEADS * GLA_DV,
    GLA_HEADS * GLA_DV,
    GLA_GATE_RANK,
    DSA_HEADS * DSA_HEAD_DIM,
    DSA_KV_HEADS * DSA_HEAD_DIM,
    DSA_KV_HEADS * DSA_HEAD_DIM,
    IDX_HEADS * IDX_DIM,
    IDX_DIM,
    IDX_HEADS,
    MEM_HEADS * MEM_HEAD_DIM,
    N_BRANCH_2 * D_MODEL,
)
D_IN = sum(IN_SPLITS)


def _rmsnorm(x, g):
    xf = x.astype(jnp.float32)
    y = xf * lax.rsqrt(jnp.mean(xf * xf, axis=-1, keepdims=True) + EPS)
    return y.astype(x.dtype) * g

def _split_in(z):
    offs = []
    acc = 0
    for w in IN_SPLITS[:-1]:
        acc += w
        offs.append(acc)
    return jnp.split(z, offs, axis=-1)

def _gla(q, k, v, g_out, a_low, w_a2, b_a2, norm_g):
    B, T = q.shape[:2]
    C = GLA_CHUNK
    N = T // C
    shp_k = (B, N, C, GLA_HEADS, GLA_DK)
    qf = q.astype(jnp.float32).reshape(shp_k) * GLA_DK ** -0.5
    kf = k.astype(jnp.float32).reshape(shp_k)
    vf = v.astype(jnp.float32).reshape(B, N, C, GLA_HEADS, GLA_DV)
    log_a = jax.nn.log_sigmoid((a_low @ w_a2 + b_a2).astype(jnp.float32)) / GLA_GATE_TEMP
    cum = jnp.cumsum(log_a.reshape(shp_k), axis=2)
    last = cum[:, :, -1:]
    q_dec = qf * jnp.exp(cum)
    k_inv = kf * jnp.exp(-cum)
    k_end = kf * jnp.exp(last - cum)
    causal = jnp.tril(jnp.ones((C, C), dtype=bool))
    att = jnp.where(causal, jnp.einsum('bnihd,bnjhd->bnhij', q_dec, k_inv), 0.0)
    o_intra = jnp.einsum('bnhij,bnjhv->bnihv', att, vf)
    upd = jnp.einsum('bnjhd,bnjhv->nbhdv', k_end, vf)
    decay = jnp.exp(last[:, :, 0]).transpose(1, 0, 2, 3)

    def step(state, inp):
        dec, u = inp
        return dec[..., None] * state + u, state

    s0 = jnp.zeros((B, GLA_HEADS, GLA_DK, GLA_DV), jnp.float32)
    _, s_prev = lax.scan(step, s0, (decay, upd))
    o_inter = jnp.einsum('bnihd,nbhdv->bnihv', q_dec, s_prev)
    o = (o_intra + o_inter).reshape(B, T, GLA_HEADS, GLA_DV)
    o = _rmsnorm(o, norm_g.astype(jnp.float32)).reshape(B, T, GLA_HEADS * GLA_DV)
    return (o * jax.nn.silu(g_out.astype(jnp.float32))).astype(q.dtype)

def _dsa(q, k, v, q_idx, k_idx, w_idx, q_gain, k_gain, kidx_gain):
    B, T = q.shape[:2]
    topk = min(IDX_TOPK_MAX, T // 4)
    grp = DSA_HEADS // DSA_KV_HEADS
    q = _rmsnorm(q.reshape(B, T, DSA_HEADS, DSA_HEAD_DIM), q_gain) * DSA_HEAD_DIM ** -0.5
    k = _rmsnorm(k.reshape(B, T, DSA_KV_HEADS, DSA_HEAD_DIM), k_gain)
    v = v.reshape(B, T, DSA_KV_HEADS, DSA_HEAD_DIM)
    q_idx = q_idx.reshape(B, T, IDX_HEADS, IDX_DIM)
    k_idx = _rmsnorm(k_idx, kidx_gain)
    w_idx = w_idx * (IDX_HEADS ** -0.5 * IDX_DIM ** -0.5)
    key_pos = jnp.arange(T)

    def block(i):
        start = i * Q_BLOCK
        qb = lax.dynamic_slice_in_dim(q, start, Q_BLOCK, axis=1)
        qib = lax.dynamic_slice_in_dim(q_idx, start, Q_BLOCK, axis=1)
        wb = lax.dynamic_slice_in_dim(w_idx, start, Q_BLOCK, axis=1)
        qpos = start + jnp.arange(Q_BLOCK)
        rel = jax.nn.relu(jnp.einsum('bqhd,bsd->bqhs', qib, k_idx).astype(jnp.float32))
        score = jnp.einsum('bqh,bqhs->bqs', wb.astype(jnp.float32), rel)
        allowed = key_pos[None, :] <= qpos[:, None]
        score = jnp.where(allowed, score, -jnp.inf)
        _, idx = lax.top_k(score, topk)
        valid = idx <= qpos[None, :, None]
        kg = jax.vmap(lambda kk, ii: kk[ii])(k, idx)
        vg = jax.vmap(lambda vv, ii: vv[ii])(v, idx)
        qg = qb.reshape(B, Q_BLOCK, DSA_KV_HEADS, grp, DSA_HEAD_DIM)
        logits = jnp.einsum('bqgrd,bqkgd->bqgrk', qg, kg).astype(jnp.float32)
        logits = jnp.where(valid[:, :, None, None, :], logits, -jnp.inf)
        p = jax.nn.softmax(logits, axis=-1).astype(v.dtype)
        o = jnp.einsum('bqgrk,bqkgd->bqgrd', p, vg)
        return o.reshape(B, Q_BLOCK, DSA_HEADS * DSA_HEAD_DIM)

    out = lax.map(block, jnp.arange(T // Q_BLOCK))
    return out.transpose(1, 0, 2, 3).reshape(B, T, DSA_HEADS * DSA_HEAD_DIM)

def _memory_attn(q, mem_h, w_kv, q_gain, k_gain):
    B, T = q.shape[:2]
    M = mem_h.shape[1]
    q = _rmsnorm(q.reshape(B, T, MEM_HEADS, MEM_HEAD_DIM), q_gain) * MEM_HEAD_DIM ** -0.5
    kv = (mem_h @ w_kv).reshape(B, M, 2, MEM_HEADS, MEM_HEAD_DIM)
    k = _rmsnorm(kv[:, :, 0], k_gain)
    v = kv[:, :, 1]
    logits = jnp.einsum('bthd,bmhd->bhtm', q, k).astype(jnp.float32)
    p = jax.nn.softmax(logits, axis=-1).astype(v.dtype)
    o = jnp.einsum('bhtm,bmhd->bthd', p, v)
    return o.reshape(B, T, MEM_HEADS * MEM_HEAD_DIM)

def _hier_moe(h, w_r1, b_r1, w_r2, b_r2, w_gate, w_up, w_down):
    B, T, D = h.shape
    hf = h.reshape(B * T, D)
    g_logits = (hf @ w_r1 + b_r1).astype(jnp.float32)
    g_prob = jax.nn.softmax(g_logits, axis=-1)
    g_sel = jnp.argmax(g_logits, axis=-1)
    g_w = jnp.take_along_axis(g_prob, g_sel[:, None], axis=-1)
    e_logits = (hf @ w_r2 + b_r2).astype(jnp.float32).reshape(-1, N_GROUPS, EXPERTS_PER_GROUP)
    e_logits = jnp.take_along_axis(e_logits, g_sel[:, None, None], axis=1)[:, 0]
    e_prob = jax.nn.softmax(e_logits, axis=-1)
    top_p, top_i = lax.top_k(e_prob, EXPERT_TOPK)
    top_p = top_p / jnp.sum(top_p, axis=-1, keepdims=True)
    expert_id = g_sel[:, None] * EXPERTS_PER_GROUP + top_i
    combine = jnp.sum(jax.nn.one_hot(expert_id, N_EXPERTS, dtype=jnp.float32)
                      * (g_w * top_p)[..., None], axis=1)
    hid = jax.nn.silu(jnp.einsum('nd,edf->nef', hf, w_gate)) * jnp.einsum('nd,edf->nef', hf, w_up)
    hid = hid * combine[..., None].astype(hid.dtype)
    out = jnp.einsum('nef,efd->nd', hid, w_down)
    return out.reshape(B, T, D)

def second_inputs(seed: int = 0) -> dict:
    key = jax.random.key(seed)
    ks = iter(jax.random.split(key, 40))
    L = DEPTH

    def w(shape, fan_in):
        return jax.random.normal(next(ks), shape, jnp.float32) * fan_in ** -0.5

    def gain(shape):
        return 1.0 + 0.02 * jax.random.normal(next(ks), shape, jnp.float32)

    def bias(shape, s=0.01):
        return s * jax.random.normal(next(ks), shape, jnp.float32)

    return {
        'x': jax.random.normal(next(ks), (BATCH, SEQ, D_MODEL), jnp.float32),
        'mem': jax.random.normal(next(ks), (BATCH, MEM_LEN, D_MODEL), jnp.float32),
        'g_mix': gain((L, D_MODEL)),
        'g_mem': gain((L, D_MODEL)),
        'w_in': w((L, D_MODEL, D_IN), D_MODEL),
        'w_gla_a2': w((L, GLA_GATE_RANK, GLA_HEADS * GLA_DK), GLA_GATE_RANK),
        'b_gla_a2': bias((L, GLA_HEADS * GLA_DK), 0.1),
        'gla_norm': gain((L, GLA_DV)),
        'w_mem_kv': w((L, D_MODEL, 2 * MEM_HEADS * MEM_HEAD_DIM), D_MODEL),
        'dsa_q_norm': gain((L, DSA_HEAD_DIM)),
        'dsa_k_norm': gain((L, DSA_HEAD_DIM)),
        'idx_k_norm': gain((L, IDX_DIM)),
        'mem_q_norm': gain((L, MEM_HEAD_DIM)),
        'mem_k_norm': gain((L, MEM_HEAD_DIM)),
        'b_gate': bias((L, N_BRANCH_2 * D_MODEL), 0.1),
        'w_o_gla': w((L, GLA_HEADS * GLA_DV, D_MODEL), GLA_HEADS * GLA_DV),
        'w_o_dsa': w((L, DSA_HEADS * DSA_HEAD_DIM, D_MODEL), DSA_HEADS * DSA_HEAD_DIM),
        'w_o_mem': w((L, MEM_HEADS * MEM_HEAD_DIM, D_MODEL), MEM_HEADS * MEM_HEAD_DIM),
        'w_out': w((L, D_MODEL, D_MODEL), D_MODEL),
        'g_ffn': gain((L, D_MODEL)),
        'w_r1': w((L, D_MODEL, N_GROUPS), D_MODEL),
        'b_r1': bias((L, N_GROUPS)),
        'w_r2': w((L, D_MODEL, N_EXPERTS), D_MODEL),
        'b_r2': bias((L, N_EXPERTS)),
        'w_gate': w((L, N_EXPERTS, D_MODEL, D_EXPERT), D_MODEL),
        'w_up': w((L, N_EXPERTS, D_MODEL, D_EXPERT), D_MODEL),
        'w_down': w((L, N_EXPERTS, D_EXPERT, D_MODEL), D_EXPERT),
    }

def second_block(x, mem, g_mix, g_mem, w_in, w_gla_a2, b_gla_a2, gla_norm, w_mem_kv,
              dsa_q_norm, dsa_k_norm, idx_k_norm, mem_q_norm, mem_k_norm, b_gate,
              w_o_gla, w_o_dsa, w_o_mem, w_out, g_ffn, w_r1, b_r1, w_r2, b_r2,
              w_gate, w_up, w_down):
    B, T, D = x.shape
    for l in range(DEPTH):
        h = _rmsnorm(x, g_mix[l])
        (gq, gk, gv, gg, ga, dq, dk, dv, iq, ik, iw, mq, gates) = _split_in(h @ w_in[l])
        o_gla = _gla(gq, gk, gv, gg, ga, w_gla_a2[l], b_gla_a2[l], gla_norm[l])
        o_dsa = _dsa(dq, dk, dv, iq, ik, iw, dsa_q_norm[l], dsa_k_norm[l], idx_k_norm[l])
        mem_h = _rmsnorm(mem, g_mem[l])
        o_mem = _memory_attn(mq, mem_h, w_mem_kv[l], mem_q_norm[l], mem_k_norm[l])
        gate = jax.nn.sigmoid((gates + b_gate[l]).astype(jnp.float32)).astype(x.dtype)
        gate = gate.reshape(B, T, N_BRANCH_2, D)
        merged = (gate[:, :, 0] * (o_gla @ w_o_gla[l])
                  + gate[:, :, 1] * (o_dsa @ w_o_dsa[l])
                  + gate[:, :, 2] * (o_mem @ w_o_mem[l]))
        x = x + merged @ w_out[l]
        x = x + _hier_moe(_rmsnorm(x, g_ffn[l]), w_r1[l], b_r1[l], w_r2[l], b_r2[l],
                          w_gate[l], w_up[l], w_down[l])
    return x


def setup_inputs(seed=0):
    out = dict(first_inputs(seed))
    for name, value in second_inputs(seed + 1).items():
        if name != "x":
            out[name + "_2"] = value
    return out


def reference(
    x, g_norm_mix, w_in, b_in, b_fgate, conv_qk, g_mlstm_head, pe_cmp, w_cmp1, w_cmp2, rel_bias,
    w_branch, w_out, g_norm_ffn, w_gate, w_up, w_down, g_final, mem_2, g_mix_2, g_mem_2, w_in_2,
    w_gla_a2_2, b_gla_a2_2, gla_norm_2, w_mem_kv_2, dsa_q_norm_2, dsa_k_norm_2, idx_k_norm_2,
    mem_q_norm_2, mem_k_norm_2, b_gate_2, w_o_gla_2, w_o_dsa_2, w_o_mem_2, w_out_2, g_ffn_2,
    w_r1_2, b_r1_2, w_r2_2, b_r2_2, w_gate_2, w_up_2, w_down_2,
):
    x = first_block(
        x, g_norm_mix, w_in, b_in, b_fgate, conv_qk, g_mlstm_head, pe_cmp, w_cmp1, w_cmp2,
        rel_bias, w_branch, w_out, g_norm_ffn, w_gate, w_up, w_down, g_final,
    )
    return second_block(
        x, mem_2, g_mix_2, g_mem_2, w_in_2, w_gla_a2_2, b_gla_a2_2, gla_norm_2, w_mem_kv_2,
        dsa_q_norm_2, dsa_k_norm_2, idx_k_norm_2, mem_q_norm_2, mem_k_norm_2, b_gate_2,
        w_o_gla_2, w_o_dsa_2, w_o_mem_2, w_out_2, g_ffn_2, w_r1_2, b_r1_2, w_r2_2, b_r2_2,
        w_gate_2, w_up_2, w_down_2,
    )


_drawn_inputs = setup_inputs


def setup_inputs(seed=0):
    import zlib

    import numpy as np

    out = dict(_drawn_inputs(seed))
    spreads = {}
    factors = {'g_mlstm_head': 5.229,
     'g_mem_2': 8.0,
     'b_gla_a2_2': 3.368,
     'gla_norm_2': 45.553,
     'dsa_q_norm_2': 38.992,
     'dsa_k_norm_2': 35.07,
     'idx_k_norm_2': 19.335,
     'mem_q_norm_2': 8.0,
     'mem_k_norm_2': 8.0,
     'b_r1_2': 64.0,
     'b_r2_2': 48.096,
     'g_ffn_2': 8.0}
    for name, (base, spread) in spreads.items():
        noise = np.random.default_rng([zlib.crc32(name.encode()), seed]).standard_normal(out[name].shape)
        drawn = base * np.exp(spread * noise) if base else spread * noise
        out[name] = jnp.asarray(drawn.astype(out[name].dtype))
    for name, factor in factors.items():
        out[name] = (out[name] * factor).astype(out[name].dtype)
    return out
```

```python
from contextlib import ExitStack
import math

import numpy as np

import concourse.bass as bass
from concourse import mybir

F32 = mybir.dt.float32
ALU = mybir.AluOpType
ACT = mybir.ActivationFunctionType
AX = mybir.AxisListType

P = 128
T = 256
TT = T // P
D = 1024
KT = D // P
EPS = 1e-6
NEG = -1e30
SW = 256
RING = 3

MH, MD = 4, 128
NH, NG, ND = 8, 2, 64
NREP = NH // NG
CMP_BLOCK, CMP_STRIDE = 32, 16
NCMP = (T - CMP_BLOCK) // CMP_STRIDE + 1
CMP_PAIRS = CMP_BLOCK // 2
BUCKETS, MAX_DIST = 32, 1024
FF = -(-8 * D // (3 * 256)) * 256
M_W, N_W, N_KV = MH * MD, NH * ND, NG * ND
C_MQ = 0
C_MV = 2 * M_W
C_MI = 4 * M_W
C_NQ = C_MI + 2 * MH
C_KV = C_NQ + N_W
C_NGATE = C_KV + 6 * N_KV
C_MERGE = C_NGATE + 3 * NH

GH, GK, GV, GRANK, GCHUNK = 4, 128, 256, 16, 64
GTEMP = 16.0
DH, DG, DD = 8, 2, 128
DREP = DH // DG
IH, IDIM = 8, 64
TOPK = min(256, T // 4)
EH, ED = 4, 256
MEM = 256
NGRP, PERG = 4, 4
NEXP = NGRP * PERG
DEXP = D // 4
B_GQ = 0
B_GV = 2 * GH * GK
B_GA = B_GV + 2 * GH * GV
B_DQ = B_GA + GRANK
B_DKV = B_DQ + DH * DD
B_IQ = B_DKV + 2 * DG * DD
B_IK = B_IQ + IH * IDIM
B_MQ = B_IK + IDIM + IH
B_GATE = B_MQ + EH * ED
MARK = -3e38


def bucket(dist):
    n = np.maximum(dist, 0)
    half = BUCKETS // 2
    nf = np.maximum(n, 1).astype(np.float32)
    large = half + (np.log(nf / np.float32(half)) / np.float32(math.log(MAX_DIST / half))
                    * np.float32(BUCKETS - half)).astype(np.int32)
    return np.where(n < half, n, np.minimum(large, BUCKETS - 1))


def one_hot(dist):
    rows = np.where(dist < 0, BUCKETS, bucket(dist))
    return (np.arange(BUCKETS + 1)[:, None] == rows[None, :]).astype(np.float32)


REV = T + P
OH_CMP0 = T - 1


def constants():
    i = np.arange(P)
    f = np.float32
    le = (i[:, None] <= i[None, :]).astype(f)
    same = (i[:, None] // GCHUNK == i[None, :] // GCHUNK).astype(f)
    after = (i[None, :] > i[:, None]).astype(f)
    t = np.arange(T)
    ends = np.arange(NCMP) * CMP_STRIDE + CMP_BLOCK - 1
    seen = (ends[None, :] <= t[:, None]).astype(f)
    return {
        "c_ident": np.eye(P, dtype=f),
        "c_tri": le,
        "c_tri64": le * same,
        "c_mask_after": after * f(NEG),
        "c_mask_before": after.T * f(-NEG),
        "c_causal": np.concatenate([np.zeros((P, P), f), after * f(NEG)], axis=1),
        "c_seen": seen.reshape(TT, P, NCMP).transpose(1, 0, 2).copy(),
        "c_oh_rev": one_hot(T - 1 - np.arange(REV)),
        "c_oh_cmp": one_hot(np.arange(2 * T) - OH_CMP0),
        "c_neg": np.full((1, NH), NEG, f),
        "c_iota4": np.broadcast_to(np.arange(4, dtype=f), (P, 4)).copy(),
    }


class Count:

    def __init__(self, sem, plan):
        self.sem, self.plan, self.n = sem, plan, 0

    def did(self, *step):
        self.n += 1
        self.plan[step] = self.n
        return self.sem, 1

    def done(self, *step):
        return self.sem, self.plan.get(step, 1)


def program(nc, dram, out, plan):
    ctx = ExitStack()
    first_ctx, second_ctx = ExitStack(), ExitStack()

    def sb(name, shape, dtype=F32, into=None):
        return (into or ctx).enter_context(nc.sbuf_tensor(name, shape, dtype))

    def sem(name):
        return ctx.enter_context(nc.semaphore(name))

    def count(name):
        return Count(sem(name), plan.setdefault(name, {}))

    def spread(ap, *dims):
        return bass.AP(tensor=ap.tensor, offset=ap.offset, ap=[list(ap.ap[0])] + [list(d) for d in dims])

    def along(ap, n):
        return spread(ap, (ap.ap[-1][0], ap.shape[-1]), (0, n))

    ident = sb("ident", [P, P])
    tri = sb("tri", [P, P])
    tri64 = sb("tri64", [P, P])
    mask_after = sb("mask_after", [P, P])
    mask_before = sb("mask_before", [P, P])
    causal = sb("causal", [P, T])
    ones = sb("ones", [P, P])
    minus_half = sb("minus_half", [P, 32])
    rows = sb("rows", [P, 2, P])
    cols = sb("cols", [P, 2, P])
    x = sb("x", [P, TT, D])
    xn = sb("xn", [P, TT, D])
    xT = sb("xT", [P, KT, T])
    ss = sb("ss", [P, 2 * TT])
    ring = sb("ring", [P, RING, KT, SW])
    g_fin = sb("g_fin", [P, D])
    hT = sb("hT", [P, 2, T])
    gated = sb("gated", [P, 2, T])
    small = sb("small", [P, KT, 96])
    bank = [ctx.enter_context(nc.psum_tensor(f"bank{b}", [P, 512], F32)) for b in range(8)]

    VECTORS = [
        [("b_qk", 8), ("b_nq", 4), ("b_merge", 16), ("b_kv", 4), ("g_mix", 8), ("conv", 32),
         ("g_head", 4), ("g_ffn", 8), ("pe", 32)],
        [("g_mix2", 8), ("g_mem", 8), ("g_dq", 1), ("g_dk", 1), ("g_ik", 1), ("g_mq", 2), ("g_mk", 2),
         ("g_gla", 2), ("b_gate", 24), ("g_ffn2", 8)],
    ]
    ROW = {}
    for tile, vectors in enumerate(VECTORS):
        at = 0
        for name, n in vectors:
            ROW[name] = (tile, at)
            at += n
    NROWS = [sum(n for _, n in v) for v in VECTORS]

    def col(name, i=0):
        tile, at = ROW[name]
        return cols[:, tile, at + i:at + i + 1]

    def one(name, shape, dtype=F32):
        return sb(name, shape, dtype, into=first_ctx)

    oh_rev = one("oh_rev", [BUCKETS + 1, REV])
    oh_cmp = one("oh_cmp", [BUCKETS + 1, 2 * T])
    rel = one("rel", [BUCKETS + 1, NH])
    rev = one("rev", [NH, REV])
    strip = one("strip", [P, NH, T])
    cmp_bias = one("cmp_bias", [P, TT, NCMP, NH])
    seen = one("seen", [P, TT, NCMP])
    w_cmp1 = one("w_cmp1_sb", [P, 2, CMP_PAIRS, P])
    w_cmp2k = one("w_cmp2k", [P, 2, ND])
    w_cmp2v = one("w_cmp2v", [P, ND])
    b_vo = one("b_vo", [P, 2 * M_W])
    b_small = one("b_small", [P, 8 + 3 * NH])
    b_vs = one("b_vs", [P, 2, N_KV])
    b_fg = one("b_fg", [P, MH])
    qk_pre = one("qk_pre", [P, 8, 3 + T])
    qk = one("qk", [P, 8, T])
    sig = one("sig", [P, 8, T])
    v1 = one("v1", [P, TT, MH, MD + 1])
    sig_o = one("sig_o", [P, TT, M_W])
    gate_in = one("gate_in", [P, TT, 8 + 3 * NH])
    nsa_gate = one("nsa_gate", [P, TT, 3 * NH])
    nqT = one("nqT", [P, 4, T])
    cmp_in = one("cmp_in", [P, 2, NG, T + 1])
    kT = one("kT", [P, 2, NG, T])
    v_sw = one("v_sw", [P, 2, TT, N_KV])
    mergeT = one("mergeT", [P, 16, T])
    ysT = one("ysT", [P, 8, T])
    mixT = sig
    mix2 = one("mix2", [P, 2, 512])
    fz = one("fz", [P, TT, MH])
    fa = one("fa", [P, TT, MH])
    fe = one("fe", [P, TT, MH])
    lf = one("lf", [P, TT, MH])
    bc = one("bc", [P, 2, TT, MH])
    cc = one("cc", [P, TT, MH])
    cm = one("cm", [P, TT, MH])
    cx = one("cx", [P, MH])
    m1 = one("m1", [P, MH])
    mm = one("mm", [P, TT, MH])
    w_st = one("w_st", [P, 3, MH])
    em = one("em", [P, TT, MH])
    yy = one("yy", [P, TT, MH, P])
    pT = one("pT", [P, TT, MH, P])
    k_tok = one("k_tok", [P, MH, MD])
    wv = one("wv", [P, MH, MD + 1])
    c1 = one("c1", [P, MH, MD + 1])
    hh = one("hh", [P, TT, MH, MD + 1])
    den = one("den", [P, TT, MH])
    hn = one("hn", [P, TT, MH, MD])
    hsq = yy
    blk = one("blk", [P, 2, CMP_PAIRS, NG, NCMP])
    hid = one("hid", [P, 2, NG * NCMP])
    hid_s = one("hid_s", [P, 2, NG * NCMP])
    kcT = one("kcT", [P, NG * NCMP])
    vc = one("vc", [NCMP, NG, ND])
    lc = one("lc", [P, TT, NH, NCMP])
    ec = one("ec", [P, TT, NH, NCMP])
    mc = one("mc", [P, TT, NH])
    sc = one("sc", [P, TT, NH])
    pcT = qk_pre[0:NCMP, :, :].rearrange("p a b -> p (a b)")[:, 0:TT * NH * P]\
        .rearrange("p (t h q) -> p t h q", t=TT, h=NH)
    lg = xn[:, :, :].rearrange("p t (h k) -> p t h k", h=NREP)
    mx = one("mx", [P, 2, NREP])
    sm = one("sm", [P, 2, NREP])
    aT = qk[:, :, :].rearrange("p (b t h) (i q) -> p b t (h i) q", b=2, t=TT, i=2)
    first_ctx.close()

    def two(name, shape, dtype=F32):
        return sb(name, shape, dtype, into=second_ctx)

    gv = two("gv", [P, TT, GH * GV])
    mem = gv
    gqk = two("gqk", [P, 8, T])
    memT = gqk
    o_gT = gqk
    gg = two("gg", [P, TT, GH * GV])
    mk = two("mk", [P, TT, EH * ED])
    mv = two("mv", [P, TT, EH * ED])
    mq = two("mq", [P, TT, EH * ED])
    o_mT = mq[:, :, :].rearrange("p t (k q) -> p (t k) q", q=T)
    mkT = two("mkT", [P, 8, T])
    mergedT = mkT
    mqT = two("mqT", [P, 8, T])
    a_low = two("a_low", [GRANK, T])
    w_a2 = two("w_a2", [GRANK, GH * GK])
    b_a2 = two("b_a2", [P, GH * GK])
    la = two("la", [P, TT, GH * GK])
    lz = two("lz", [P, TT, GH * GK])
    cum = two("cum", [P, GH, T])
    ex = two("ex", [P, GH, T])
    ki = two("ki", [P, GH, T])
    decay = two("decay", [P, GH, T // GCHUNK])
    gla_end = two("gla_end", [P, 2 * T * GH + 3 * GH * GV])
    ke_tok, att = (gla_end[:, n * T * GH:(n + 1) * T * GH].rearrange("p (t h q) -> p t h q", t=TT, h=GH)
                   for n in range(2))
    state = gla_end[:, 2 * T * GH:].rearrange("p (n h v) -> p n h v", n=3, h=GH)
    dq = mk
    o_dT = dq[:, :, :].rearrange("p t (k q) -> p (t k) q", q=T)
    dqT = mqT
    dk = two("dk", [P, TT, DG * DD])
    dv = two("dv", [P, TT, DG * DD])
    dkT = two("dkT", [P, DG, T])
    iqT = two("iqT", [P, 4, T])
    ikw = two("ikw", [P, TT, IDIM + IH])
    ik2 = two("ik2", [P, TT, 2, IDIM])
    ikT = two("ikT", [P, T])
    relu = two("relu", [P, IH, T])
    score = two("score", [P, TT, T])
    best = two("best", [P, TT, 8])
    pick = two("pick", [P, TT, T])
    scaled = two("scaled", [P, 3])
    sq = relu
    s16 = two("s16", [P, TT, 8])
    smx = two("smx", [P, 2, 4])
    ssm = two("ssm", [P, 2, 4])
    probT = two("probT", [P, TT, 4, P])
    b_r = two("b_r", [P, NGRP + NEXP])
    iota4 = two("iota4", [P, 4])
    rl = two("rl", [P, TT, NGRP + NEXP])
    r_tmp = two("r_tmp", [P, TT, NEXP])
    r_key = two("r_key", [P, TT, 4])
    r_one = two("r_one", [P, 3, TT, 4])
    r_el = two("r_el", [P, TT, 4])
    r_s = two("r_s", [P, 8, TT])
    comb = two("comb", [P, TT, NEXP])
    comb_all = gla_end[:, 0:NEXP * T].rearrange("p (e t) -> p e t", e=NEXP)
    second_ctx.close()
    loads = {n: sem("load_" + n) for n in ("x", "const", "rows", "broadcast", "rel", "small", "cmp", "rev", "copies", "strip", "twice", "mem", "second",
                                          "narrow", "router", "g_fin")}
    slab_loaded = [sem(f"slab_loaded{r}") for r in range(RING)]
    slab_used = sem("slab_used")
    bank_read = [sem("bank0_read"), sem("bank1_read")]
    stored = sem("stored")
    setup_pe, setup_vec, setup_act, setup_pool = (count("setup_" + e) for e in ("pe", "vec", "act", "pool"))
    norm_pe, norm_vec, norm_act, norm_pool = (count("norm_" + e) for e in ("pe", "vec", "act", "pool"))
    in1_pe, in1_vec, in1_act = (count("in1_" + e) for e in ("pe", "vec", "act"))
    ml_pe, ml_vec, ml_act, ml_pool = (count("mlstm_" + e) for e in ("pe", "vec", "act", "pool"))
    ns_pe, ns_vec, ns_act = (count("nsa_" + e) for e in ("pe", "vec", "act"))
    mix_vec = count("mix_vec")
    ff_seed = sem("ff_seed")
    ff_up = sem("ff_up")
    ff_silu = sem("ff_silu")
    ff_hidden = sem("ff_hidden")
    ff_shared = sem("ff_shared")
    b2_pe, b2_vec, b2_act, b2_pool = (count("second_" + e) for e in ("pe", "vec", "act", "pool"))

    STREAM = [("qk", "w_in", C_MQ, 4), ("vo", "w_in", C_MV, 4), ("nq", "w_in", C_NQ, 2),
              ("kv", "w_in", C_KV, 3), ("merge", "w_in", C_MERGE, 8),
              ("branch", "w_branch", 0, 4), ("out", "w_out", 0, 4),
              ("ffn", None, 0, 3 * (FF // SW)),
              ("memkv", "w_mem_kv_2", 0, 8), ("mq", "w_in_2", B_MQ, 4), ("gqk", "w_in_2", B_GQ, 4),
              ("gvg", "w_in_2", B_GV, 8), ("dq", "w_in_2", B_DQ, 4), ("dkv", "w_in_2", B_DKV, 2),
              ("iq", "w_in_2", B_IQ, 2)]
    BRANCHES = [("mem", 2, "w_o_mem_2"), ("gla", 0, "w_o_gla_2"), ("dsa", 1, "w_o_dsa_2")]
    for name, z, w_o in BRANCHES:
        for j in range(4):
            STREAM += [(f"gate_{name}{j}", "w_in_2", B_GATE + z * D + j * SW, 1), (f"o_{name}{j}", w_o, j * SW, 1)]
    STREAM += [("out2", "w_out_2", 0, 4), ("moe", None, 0, 3 * NEXP)]
    SLAB, at = {}, 0
    for name, _, _, n in STREAM:
        SLAB[name] = at
        at += n

    def weights(name, c, n):
        m = dram[name]
        m = m[0] if name != "w_branch" else m.rearrange("z n w d -> (z n w) d")
        return m.rearrange("(k p) n -> p k n", p=P)[:, :, c:c + n] if isinstance(c, int) else \
            m.rearrange("(k p) n -> p k n", p=P)[:, :, bass.ds(c, n)]

    BANKED = {}
    for name, _, _, n in STREAM:
        for j in range(n):
            if name not in ("branch", "ffn", "moe"):
                BANKED[SLAB[name] + j] = len(BANKED)

    def half(s, n):
        return bank[BANKED[s] % 2][:, n * T:(n + 1) * T]

    def half_read(s):
        return bank_read[BANKED[s] % 2], 1

    def other_half(eng, s):
        eng.wait_ge(bank_read[BANKED[s] % 2], 2 * (BANKED[s] // 2) + 1)

    def all_out(s):
        return [(bank_read[b], 2 * ((BANKED[s] + 2 - b) // 2)) for b in range(2)]

    def evicted(eng, s):
        for w in all_out(s):
            eng.wait_ge(*w)

    def slab_out(eng, name, j):
        eng.wait_ge(slab_used, SLAB[name] + j + 1)

    def slab_in(pe, s):
        pe.wait_ge(slab_loaded[s % RING], 16 * (s // RING + 1))
        if s in BANKED and BANKED[s] >= 2:
            pe.wait_ge(bank_read[BANKED[s] % 2], 2 * (BANKED[s] // 2))

    def slab_rows(pe, s, operand):
        for n in range(2):
            for k in range(KT):
                ins = pe.matmul(half(s, n), ring[:, s % RING, k, n * P:(n + 1) * P], operand[:, k, :],
                                start=(k == 0), stop=(k == KT - 1))
        return ins

    def slab_tokens(pe, s, operand):
        for t in range(TT):
            for k in range(KT):
                ins = pe.matmul(half(s, t), operand[:, k, t * P:(t + 1) * P], ring[:, s % RING, k, :],
                                start=(k == 0), stop=(k == KT - 1))
        return ins

    def slabs(pe, name, product, operand, start=0, end=4):
        for j in range(start, end):
            slab_in(pe, SLAB[name] + j)
            product(pe, SLAB[name] + j, operand).then_inc(slab_used, 1)

    def norm_square(act, name, src, *ready):
        for w in ready:
            act.wait_ge(*w)
        for t in range(TT):
            act.activation(xn[:, t, :], src[:, t, :], ACT.Square, accum_out=ss[:, t:t + 1])\
               .then_inc(*norm_act.did("square", name, t))

    def norm_scale(vec, name, src, dst=None):
        vec.wait_ge(*norm_act.done("square", name, TT - 1))
        vec.tensor_scalar(ss[:, 2:4], ss[:, 0:2], 1.0 / D, EPS, ALU.mult, ALU.add)\
           .then_inc(*norm_vec.did("mean", name))
        vec.wait_ge(*norm_pool.done("root", name))
        for t in range(TT):
            vec.tensor_scalar((xn if dst is None else dst)[:, t, :], src[:, t, :], ss[:, 2 + t:3 + t], None, ALU.mult)\
               .then_inc(*norm_vec.did("scale", name, t))

    def norm_root(pool, name):
        pool.wait_ge(*norm_vec.done("mean", name))
        pool.tensor_tensor(ss[:, 2:4], ss[:, 2:4], minus_half[:, 0:2], ALU.pow).then_inc(*norm_pool.did("root", name))

    def turn(pe, name, src, n, *ready):
        for w in ready:
            pe.wait_ge(*w)
        for k in range(n):
            for t in range(TT):
                at = (k % 2) * T + t * P
                ins = pe.transpose(bank[4 + k // 2][:, at:at + P], src[:, t, k * P:(k + 1) * P], ident[:, :])
            ins.then_inc(*norm_pe.did("turn", name, k))

    def turned(act, name, n, dst, gain):
        for k in range(n):
            act.wait_ge(*norm_pe.done("turn", name, k | 1 if k | 1 < n else k))
            act.activation(dst[:, k, :], bank[4 + k // 2][:, (k % 2) * T:(k % 2 + 1) * T], ACT.Copy,
                           scale=gain(k)).then_inc(*norm_act.did("gain", name, k))

    def attend(pe, name, logits, values):
        units = [(tt, g) for tt in range(TT) for g in range(1 if name == "mem" else DG)]

        def put_logits(n):
            tt, g = units[n]
            if n:
                pe.wait_ge(*b2_vec.done("lg", name, *units[n - 1]))
            for group in logits(tt, g):
                for dst, parts in group:
                    for i, (a, b) in enumerate(parts):
                        ins = pe.matmul(dst, a, b, start=(i == 0), stop=(i == len(parts) - 1))
            ins.then_inc(*b2_pe.did("lg", name, tt, g))

        put_logits(0)
        for n, (tt, g) in enumerate(units):
            if n + 1 < len(units):
                put_logits(n + 1)
            pe.wait_ge(*b2_vec.done("p", name, tt, g))
            if n:
                pe.wait_ge(*b2_act.done("probT", name, *units[n - 1], 0 if units[n - 1][0] == 0 and name != "mem" else 1))
            tiles = 2 if name == "mem" else tt + 1
            for kt in range(tiles):
                for i in range(4):
                    ins = pe.transpose(bank[6 + kt][:, i * P:(i + 1) * P], lg[:, n % 2, i, kt * P:(kt + 1) * P],
                                       ident[:, :])
                ins.then_inc(*b2_pe.did("probT", name, tt, g, kt))
            pe.wait_ge(*b2_act.done("probT", name, tt, g, tiles - 1))
            if n:
                pe.wait_ge(*b2_act.done("o", name, *units[n - 1]))
            for dst, parts in values(tt, g):
                for i, (a, b) in enumerate(parts):
                    ins = pe.matmul(dst, a, b, start=(i == 0), stop=(i == len(parts) - 1))
            ins.then_inc(*b2_pe.did("o", name, tt, g))

    def attend_vec(vec, name, masked):
        units = [(tt, g) for tt in range(TT) for g in range(1 if name == "mem" else DG)]
        for n, (tt, g) in enumerate(units):
            K = T if name == "mem" else (tt + 1) * P
            hs = 512 // K
            l = lg[:, n % 2, :, 0:K]
            if n >= 2:
                vec.wait_ge(*b2_pe.done("probT", name, *units[n - 2], units[n - 2][0] if name != "mem" else 1))
            vec.wait_ge(*b2_pe.done("lg", name, tt, g))
            for b in range(4 // hs):
                src = bank[4 + b][:, :].rearrange("p (h k) -> p h k", h=hs)
                dst = lg[:, n % 2, b * hs:(b + 1) * hs, 0:K]
                step = b2_vec.did("lg", name, tt, g) if b == 4 // hs - 1 else b2_vec.did("lg_", name, tt, g, b)
                if masked:
                    vec.tensor_tensor(dst, src, spread(pick[:, tt, 0:K], (0, hs), (1, K)), ALU.add).then_inc(*step)
                else:
                    vec.tensor_copy(dst, src).then_inc(*step)
            vec.wait_ge(*b2_vec.done("lg", name, tt, g))
            vec.tensor_reduce(smx[:, n % 2, :], l, AX.X, ALU.max).then_inc(*b2_vec.did("mx", name, tt, g))
            vec.wait_ge(*b2_vec.done("mx", name, tt, g))
            vec.tensor_tensor(l, l, along(smx[:, n % 2, :], K), ALU.subtract).then_inc(*b2_vec.did("shift", name, tt, g))
            vec.wait_ge(*b2_act.done("exp", name, tt, g))
            vec.tensor_reduce(ssm[:, n % 2, :], l, AX.X, ALU.add).then_inc(*b2_vec.did("sum", name, tt, g))
            vec.wait_ge(*b2_vec.done("sum", name, tt, g))
            vec.reciprocal(ssm[:, n % 2, :], ssm[:, n % 2, :]).then_inc(*b2_vec.did("rs", name, tt, g))
            vec.wait_ge(*b2_vec.done("rs", name, tt, g))
            vec.tensor_tensor(l, l, along(ssm[:, n % 2, :], K), ALU.mult).then_inc(*b2_vec.did("p", name, tt, g))

    def attend_act(act, name, store):
        units = [(tt, g) for tt in range(TT) for g in range(1 if name == "mem" else DG)]
        for n, (tt, g) in enumerate(units):
            K = T if name == "mem" else (tt + 1) * P
            act.wait_ge(*b2_vec.done("shift", name, tt, g))
            act.activation(lg[:, n % 2, :, 0:K], lg[:, n % 2, :, 0:K], ACT.Exp).then_inc(*b2_act.did("exp", name, tt, g))
            for kt in range(K // P):
                act.wait_ge(*b2_pe.done("probT", name, tt, g, kt))
                act.activation(probT[:, kt, :, :], bank[6 + kt][:, :].rearrange("p (h q) -> p h q", h=4), ACT.Copy)\
                   .then_inc(*b2_act.did("probT", name, tt, g, kt))
            act.wait_ge(*b2_pe.done("o", name, tt, g))
            store(tt, g)

    def norm_turn(pe, name, *ready):
        turn(pe, name, xn, KT, norm_vec.done("scale", name, TT - 1), *ready)

    def norm_gain(act, name, gain, dst):
        turned(act, name, KT, dst, lambda k: col(gain, k))

    def head_norm(vec, name, src, heads, size):
        flat = src.rearrange("p t n -> p (t n)")
        s2 = sq[:, :, :].rearrange("p a b -> p (a b)")[:, 0:TT * heads * size]
        vec.tensor_tensor(s2, flat, flat, ALU.mult).then_inc(*norm_vec.did("square", name))
        vec.wait_ge(*norm_vec.done("square", name))
        sums = s16[:, :, :].rearrange("p t h -> p (t h)")[:, 0:TT * heads]
        vec.tensor_reduce(sums, s2.rearrange("p (n d) -> p n d", d=size), AX.X, ALU.add)\
           .then_inc(*norm_vec.did("sum", name))
        vec.wait_ge(*norm_vec.done("sum", name))
        vec.tensor_scalar(sums, sums, 1.0 / size, EPS, ALU.mult, ALU.add).then_inc(*norm_vec.did("mean", name))
        vec.wait_ge(*norm_pool.done("root", name))
        grouped = flat.rearrange("p (n d) -> p n d", d=size)
        vec.tensor_tensor(grouped, grouped, along(sums, size), ALU.mult).then_inc(*norm_vec.did("scaled", name))

    def head_root(pool, name, heads):
        sums = s16[:, :, :].rearrange("p t h -> p (t h)")[:, 0:TT * heads]
        pool.wait_ge(*norm_vec.done("mean", name))
        pool.tensor_tensor(sums, sums, minus_half[:, 0:TT * heads], ALU.pow).then_inc(*norm_pool.did("root", name))

    def units_load(sp, first, n, gate, up, down):
        def put(s, turn_, src, i=0):
            sp.wait_ge(slab_used, s + 3 * i - RING + 1)
            dst = ring[:, s % RING, :, :]
            if turn_:
                dst = dst.rearrange("p (n a) c -> p n (a c)", n=2)
            sp.dma_start(dst, src).then_inc(slab_loaded[s % RING], 16)

        put(first, False, gate(0))
        put(first + 1, False, up(0))
        with sp.Fori(0, n - 1) as i:
            put(first + 2, False, gate(i + 1), i)
            put(first + 3, False, up(i + 1), i)
            put(first + 4, True, down(i), i)
        put(first + 3 * n - 1, True, down(n - 1))

    def units_pe(pe, first, n, base):
        def loaded(s, i=0):
            pe.wait_ge(slab_loaded[s % RING], 16 * (s // RING + 1) + 16 * i)

        def rows_(s, b, sem_, least, i=0):
            loaded(s, i)
            if least is not None:
                pe.wait_ge(sem_, least)
            for m in range(2):
                for k in range(KT):
                    ins = pe.matmul(bank[b + m][:, 0:T], ring[:, s % RING, k, m * P:(m + 1) * P], xT[:, k, :],
                                    start=(k == 0), stop=(k == KT - 1))
            ins.then_inc(slab_used, 1)

        def down(s, hidden, i=0, last=False):
            loaded(s, i)
            pe.wait_ge(ff_hidden, hidden)
            w = ring[:, s % RING, :, :].rearrange("p (n a) c -> p n (a c)", n=2)
            for b in range(4):
                for m in range(2):
                    ins = pe.matmul(bank[b][:, :], hT[:, m, (b // 2) * P:(b // 2 + 1) * P],
                                    w[:, m, (b % 2) * 512:(b % 2 + 1) * 512], start=False, stop=(last and m == 1),
                                    skip_group_check=True)
            ins.then_inc(slab_used, 1)

        for b in range(4):
            pe.matmul(bank[b][:, :], ident[:, :], x[:, b // 2, (b % 2) * 512:(b % 2 + 1) * 512],
                      start=True, stop=False, skip_group_check=True)
        rows_(first, 4, ff_silu, 2 * base if base else None)
        rows_(first + 1, 6, ff_hidden, 2 * base if base else None)
        with pe.Fori(0, n - 1) as i:
            rows_(first + 2, 4, ff_silu, 2 * (base + 1) + 2 * i, i)
            rows_(first + 3, 6, ff_hidden, 2 * (base + 1) + 2 * i, i)
            down(first + 4, 2 * (base + 1) + 2 * i, i)
        down(first + 3 * n - 1, 2 * (base + n), last=True)

    def units_act(act, first, n, base):
        def unit(gate_done, before):
            act.wait_ge(slab_used, gate_done)
            if before is not None:
                act.wait_ge(ff_hidden, before)
            for m in range(2):
                act.activation(gated[:, m, :], bank[4 + m][:, 0:T], ACT.Silu).then_inc(ff_silu, 1)

        unit(first + 1, 2 * base if base else None)
        with act.Fori(0, n - 1) as i:
            unit(first + 3 + 3 * i, 2 * (base + 1) + 2 * i)

    def units_vec(vec, first, n, base, share):
        def unit(up_done, turned_down, silu, e):
            vec.wait_ge(slab_used, up_done)
            vec.wait_ge(ff_silu, silu + 2)
            for m in range(2):
                if share is not None:
                    vec.tensor_tensor(gated[:, m, :], gated[:, m, :], share[:, bass.ds(e * T, T)], ALU.mult)\
                       .then_inc(ff_shared, 1)
            if turned_down is not None:
                vec.wait_ge(slab_used, turned_down)
            for m in range(2):
                if share is not None:
                    vec.wait_ge(ff_shared, 2 * e + m + 1)
                vec.tensor_tensor(hT[:, m, :], gated[:, m, :], bank[6 + m][:, 0:T], ALU.mult).then_inc(ff_hidden, 1)

        unit(first + 2, None, 2 * base, 0)
        with vec.Fori(0, n - 1) as i:
            unit(first + 4 + 3 * i, first + 5 + 3 * i, 2 * (base + 1) + 2 * i, i + 1)

    block = ctx.enter_context(nc.Block())

    @block.sync
    def _(sp):
        sp.dma_start(x[:, :, :], dram["x"][0].rearrange("(t p) d -> p t d", p=P)).then_inc(loads["x"], 16)

        def load_slab(s, name, c):
            if s >= RING:
                sp.wait_ge(slab_used, s - RING + 1)
            sp.dma_start(ring[:, s % RING, :, :], weights(name, c, SW)).then_inc(slab_loaded[s % RING], 16)

        for name, matrix, c, n in STREAM:
            if name == "ffn":
                cols_, down = (lambda m: dram[m][0].rearrange("(k p) n -> p k n", p=P)), \
                    dram["w_down"][0].rearrange("(n p) d -> p n d", p=P)
                units_load(sp, SLAB[name], FF // SW, lambda u: cols_("w_gate")[:, :, bass.ds(u * SW, SW)],
                           lambda u: cols_("w_up")[:, :, bass.ds(u * SW, SW)],
                           lambda u: down[:, bass.ds(u * 2, 2), :])
                continue
            if name == "moe":
                up = (lambda m: dram[m][0].rearrange("e (k p) f -> p (e k) f", p=P))
                down2 = dram["w_down_2"][0].rearrange("e (n p) d -> p (e n) d", p=P)
                units_load(sp, SLAB[name], NEXP, lambda u: up("w_gate_2")[:, bass.ds(u * KT, KT), :],
                           lambda u: up("w_up_2")[:, bass.ds(u * KT, KT), :],
                           lambda u: down2[:, bass.ds(u * 2, 2), :])
                continue
            for j in range(n):
                load_slab(SLAB[name] + j, matrix, c + j * SW)
            if name == "kv":
                sp.wait_ge(loads["rev"], 16)
                sp.dma_start(dram["rev_copies"], spread(dram["rev"], (0, P), (1, REV))).then_inc(loads["copies"], 16)
                sp.wait_ge(loads["copies"], 16)
                src = bass.AP(tensor=dram["rev_copies"].tensor, offset=P - 1,
                              ap=[[REV - 1, P], [P * REV, NH], [1, T]])
                sp.dma_start(strip[:, :, :], src).then_inc(loads["strip"], 16)
        sp.wait_ge(*b2_vec.done("y", 1))
        sp.wait_ge(*b2_act.done("y", 1))
        sp.dma_start(out.rearrange("z (t p) d -> p (z t) d", p=P), x[:, :, :]).then_inc(stored, 16)
        sp.wait_ge(stored, 16)

    @block.gpsimd
    def _(pool):
        pool.memset(ones[:, :], 1.0).then_inc(*setup_pool.did("ones"))
        pool.memset(minus_half[:, :], -0.5).then_inc(*setup_pool.did("minus_half"))
        pool.memset(qk_pre[:, :, 0:3], 0.0).then_inc(*setup_pool.did("pad"))
        pool.memset(v1[:, :, :, MD:MD + 1], 1.0).then_inc(*setup_pool.did("ones_v"))
        b_in = dram["b_in"][0]

        def row_load(name, src, lo=0, hi=P):
            tile, at = ROW[name]
            n = src.shape[0]
            pool.dma_start(rows[at:at + n, tile, lo:hi], src).then_inc(loads["rows"], 16)

        def vector_rows(v):
            return v.rearrange("(n p) -> n p", p=P)

        row_load("b_qk", vector_rows(b_in[C_MQ:C_MV]))
        row_load("b_nq", vector_rows(b_in[C_NQ:C_KV]))
        row_load("b_merge", vector_rows(b_in[C_MERGE:C_MERGE + 2 * D]))
        tile, at = ROW["b_kv"]
        pool.dma_start(rows[at:at + 3, tile, :], vector_rows(b_in[C_KV:C_KV + 3 * N_KV])).then_inc(loads["rows"], 16)
        pool.dma_start(rows[at + 3:at + 4, tile, :], vector_rows(b_in[C_KV + 4 * N_KV:C_KV + 5 * N_KV]))\
            .then_inc(loads["rows"], 16)
        row_load("g_mix", vector_rows(dram["g_norm_mix"][0]))
        row_load("conv", dram["conv_qk"][0].rearrange("j (n p) -> (j n) p", p=P))
        row_load("g_head", vector_rows(dram["g_mlstm_head"][0]))
        row_load("g_ffn", vector_rows(dram["g_norm_ffn"][0]))
        row_load("pe", dram["pe_cmp"][0].rearrange("j (n l) d -> (j n) (l d)", l=2))
        row_load("g_mix2", vector_rows(dram["g_mix_2"][0]))
        row_load("g_mem", vector_rows(dram["g_mem_2"][0]))
        row_load("g_dq", vector_rows(dram["dsa_q_norm_2"][0]))
        row_load("g_dk", vector_rows(dram["dsa_k_norm_2"][0]))
        for lo in (0, IDIM):
            row_load("g_ik", dram["idx_k_norm_2"], lo, lo + IDIM)
        row_load("g_mq", vector_rows(dram["mem_q_norm_2"][0]))
        row_load("g_mk", vector_rows(dram["mem_k_norm_2"][0]))
        row_load("g_gla", vector_rows(dram["gla_norm_2"][0]))
        row_load("b_gate", vector_rows(dram["b_gate_2"][0]))
        row_load("g_ffn2", vector_rows(dram["g_ffn_2"][0]))

        pool.wait_ge(*setup_pool.done("minus_half"))
        norm_root(pool, "mix")
        pool.wait_ge(*ml_vec.done("var"))
        pool.tensor_tensor(den[:, :, :].rearrange("p t h -> p (t h)"), den[:, :, :].rearrange("p t h -> p (t h)"),
                           minus_half[:, 0:TT * MH], ALU.pow).then_inc(*ml_pool.did("root"))
        for name in ("ffn", "final", "mix2", "mem"):
            norm_root(pool, name)
        for name, heads in (("mk", EH), ("mq", EH), ("gla", GH), ("dq", DH), ("dk", DG), ("ik", 1)):
            head_root(pool, name, heads)
        norm_root(pool, "ffn2")

    ROW_LOADS = 3 + 2 + 5 + 4 + 2 + 5

    @block.scalar
    def _(act):
        def load(dst, src, name):
            act.dma_start(dst, src).then_inc(loads[name], 16)

        for dst, name in ((ident, "c_ident"), (tri, "c_tri"), (tri64, "c_tri64"), (mask_after, "c_mask_after"),
                          (mask_before, "c_mask_before"), (causal, "c_causal")):
            load(dst[:, :], dram[name], "const")
        load(oh_rev[:, :], dram["c_oh_rev"], "rel")
        load(oh_cmp[:, :], dram["c_oh_cmp"], "rel")
        load(rel[0:BUCKETS, :], dram["rel_bias"], "rel")
        load(rel[BUCKETS:BUCKETS + 1, :], dram["c_neg"], "rel")
        load(seen[:, :, :], dram["c_seen"], "rel")
        b_in = dram["b_in"][0]
        load(small[:, :, 0:8], weights("w_in", C_MI, 8), "small")
        load(small[:, :, 8:32], weights("w_in", C_NGATE, 3 * NH), "small")
        load(g_fin[:, :], dram["g_final"].partition_broadcast(P), "g_fin")
        load(b_vo[:, :], b_in[C_MV:C_MI].partition_broadcast(P), "broadcast")
        load(b_small[:, 0:8], b_in[C_MI:C_NQ].partition_broadcast(P), "broadcast")
        load(b_small[:, 8:32], b_in[C_NGATE:C_MERGE].partition_broadcast(P), "broadcast")
        load(b_vs[:, 0, :], b_in[C_KV + 3 * N_KV:C_KV + 4 * N_KV].partition_broadcast(P), "broadcast")
        load(b_vs[:, 1, :], b_in[C_KV + 5 * N_KV:C_KV + 6 * N_KV].partition_broadcast(P), "broadcast")
        load(b_fg[:, :], dram["b_fgate"][0].partition_broadcast(P), "broadcast")
        for j in range(2):
            load(w_cmp1[:, j, :, :], dram["w_cmp1"][0, j].rearrange("(n p) h -> p n h", p=P), "cmp")
        load(w_cmp2k[:, 0, :], dram["w_cmp2"][0, 0], "cmp")
        load(w_cmp2k[:, 1, :], dram["w_cmp2"][0, 0], "cmp")
        load(w_cmp2v[:, :], dram["w_cmp2"][0, 1], "cmp")

        act.wait_ge(*setup_vec.done("rev"))
        load(dram["rev"], rev[:, :], "rev")

        norm_square(act, "mix", x, (loads["x"], 16))
        norm_gain(act, "mix", "g_mix", xT)

        for j in range(4):
            slab_out(act, "qk", j)
            for n in range(2):
                act.activation(qk_pre[:, 2 * j + n, 3:3 + T], half(SLAB["qk"] + j, n), ACT.Identity,
                               bias=col("b_qk", 2 * j + n)).then_inc(*half_read(SLAB["qk"] + j))
        slab_out(act, "kv", 0)
        s = SLAB["kv"]
        for j in range(2):
            bias = col("b_kv", j)
            act.activation(cmp_in[0:ND, j, 0, 1:T + 1], half(s, j)[0:ND, :], ACT.Identity, bias=bias[0:ND, :])\
               .then_inc(*in1_act.did("cmp0", j))
            act.activation(cmp_in[ND:P, j, 1, 0:T], half(s, j)[ND:P, :], ACT.Identity, bias=bias[ND:P, :])\
               .then_inc(*half_read(s))
        for j in range(2):
            slab_out(act, "kv", 1 + j)
            s = SLAB["kv"] + 1 + j
            bias = col("b_kv", 2 + j)
            act.activation(kT[0:ND, j, 0, :], half(s, 0)[0:ND, :], ACT.Identity, bias=bias[0:ND, :])\
               .then_inc(*in1_act.did("k0", j))
            act.activation(kT[ND:P, j, 1, :], half(s, 0)[ND:P, :], ACT.Identity, bias=bias[ND:P, :])\
               .then_inc(*half_read(s))
        evicted(act, SLAB["kv"] + 2)
        for dst, src in ((cmp_in[ND:P, :, 0, 0:T], cmp_in[0:ND, :, 0, 1:T + 1]),
                         (cmp_in[0:ND, :, 1, 1:T + 1], cmp_in[ND:P, :, 1, 0:T]),
                         (kT[ND:P, :, 0, :], kT[0:ND, :, 0, :]), (kT[0:ND, :, 1, :], kT[ND:P, :, 1, :])):
            act.dma_start(dst, src).then_inc(loads["twice"], 16)

        for n in range(8):
            act.wait_ge(*ml_vec.done("conv", n))
            act.activation(sig[:, n, :], qk[:, n, :], ACT.Sigmoid).then_inc(*ml_act.did("sig", n))
        evicted(act, SLAB["vo"] + 3)
        act.activation(sig_o[:, :, :], sig_o[:, :, :], ACT.Sigmoid).then_inc(*ml_act.did("sig_o"))
        act.wait_ge(*in1_vec.done("gate_in"))
        act.activation(nsa_gate[:, :, :], gate_in[:, :, 8:32], ACT.Sigmoid).then_inc(*ns_act.did("gate"))
        act.wait_ge(*ml_vec.done("fa"))
        act.activation(fe[:, :, :], fa[:, :, :], ACT.Exp, scale=-1.0).then_inc(*ml_act.did("fe"))
        act.wait_ge(*ml_act.done("fe"))
        act.activation(fe[:, :, :], fe[:, :, :], ACT.Ln, bias=1.0).then_inc(*ml_act.did("ln"))

        for j in range(4):
            slab_out(act, "merge", j)
            for n in range(2):
                act.activation(mergeT[:, 2 * j + n, :], half(SLAB["merge"] + j, n), ACT.Sigmoid,
                               bias=col("b_merge", 2 * j + n)).then_inc(*half_read(SLAB["merge"] + j))

        act.wait_ge(*ns_pe.done("hid"))
        act.activation(hid_s[:, :, :], bank[4][:, 0:2 * NG * NCMP].rearrange("p (j n) -> p j n", j=2),
                       ACT.Sigmoid).then_inc(*ns_act.did("hid_s"))
        for j in range(4, 8):
            slab_out(act, "merge", j)
            for n in range(2):
                act.activation(mergeT[:, 2 * j + n, :], half(SLAB["merge"] + j, n), ACT.Sigmoid,
                               bias=col("b_merge", 2 * j + n)).then_inc(*half_read(SLAB["merge"] + j))

        for c in range(TT):
            act.wait_ge(*ml_vec.done("yy", c))
            act.activation(yy[:, c, :, :], yy[:, c, :, :], ACT.Exp, scale=-1.0).then_inc(*ml_act.did("yy", c))
        act.wait_ge(*ml_vec.done("w_st"))
        act.activation(w_st[:, :, :], w_st[:, :, :], ACT.Exp).then_inc(*ml_act.did("w_st"))
        act.wait_ge(*ml_vec.done("em"))
        act.activation(em[:, :, :], em[:, :, :], ACT.Exp, scale=-1.0).then_inc(*ml_act.did("em"))
        act.wait_ge(*ml_pe.done("k_tok"))
        act.activation(k_tok[:, :, :], bank[5][:, :].rearrange("p (h d) -> p h d", h=MH),
                       ACT.Copy).then_inc(*ml_act.did("k_tok"))

        def pair(b):
            return bank[b][:, 0:2 * (MD + 1)].rearrange("p (h d) -> p h d", h=2)

        for n, b in enumerate((6, 4)):
            act.wait_ge(*ml_pe.done("c1", n))
            act.activation(c1[:, 2 * n:2 * n + 2, :], pair(b), ACT.Copy).then_inc(*ml_act.did("c1", n))
        for c, banks in enumerate(((5, 7), (6, 4))):
            for n, b in enumerate(banks):
                act.wait_ge(*ml_pe.done("num", c, n))
                act.activation(hh[:, c, 2 * n:2 * n + 2, :], pair(b), ACT.Copy).then_inc(*ml_act.did("num", c, n))
        for k in range(4):
            act.wait_ge(*ml_pe.done("yT", k // 2))
            act.activation(ysT[:, k, :], bank[(4, 6)[k // 2]][:, (k % 2) * T:(k % 2) * T + T], ACT.Copy,
                           scale=col("g_head", k)).then_inc(*ml_act.did("yT", k))

        act.wait_ge(*ns_vec.done("lc"))
        act.activation(ec[:, :, :, :], lc[:, :, :, :], ACT.Exp).then_inc(*ns_act.did("ec"))
        for n, b in enumerate((7, 4, 5, 6)):
            act.wait_ge(*ns_pe.done("pcT", n))
            act.activation(pcT[:, n // 2, (n % 2) * 4:(n % 2) * 4 + 4, :],
                           bank[b][0:NCMP, :].rearrange("p (h q) -> p h q", h=4),
                           ACT.Copy).then_inc(*ns_act.did("pcT", n))
        for u in range(8):
            tt, g, br = u // 4, u // 2 % 2, u % 2
            K = (tt + 1) * P
            act.wait_ge(*ns_vec.done("shift", u))
            act.activation(lg[:, u % 2, :, 0:K], lg[:, u % 2, :, 0:K], ACT.Exp).then_inc(*ns_act.did("exp", u))
            for kt in range(tt + 1):
                act.wait_ge(*ns_pe.done("aT", u, kt))
                if kt == 0 and u >= 2:
                    act.wait_ge(*ns_pe.done("av", (u - 2) // 2))
                act.activation(aT[:, br, kt, :, :], bank[6 + kt][:, :].rearrange("p (h q) -> p h q", h=NREP),
                               ACT.Copy).then_inc(*ns_act.did("aT", u, kt))
            if br == 1 and g == 1:
                act.wait_ge(*ns_pe.done("av", u // 2))
                act.activation(ysT[:, 4:8, tt * P:tt * P + P],
                               bank[2 + tt][:, :].rearrange("p (h q) -> p h q", h=4),
                               ACT.Copy).then_inc(*ns_act.did("yT", tt))

        norm_square(act, "ffn", x, *all_out(SLAB["out"] + 3))
        load(mem[:, :, :], dram["mem_2"][0].rearrange("(t p) d -> p t d", p=P), "mem")
        load(w_a2[:, :], dram["w_gla_a2_2"][0], "second")
        load(b_a2[:, :], dram["b_gla_a2_2"][0].partition_broadcast(P), "second")
        load(b_r[:, 0:NGRP], dram["b_r1_2"][0].partition_broadcast(P), "second")
        load(b_r[:, NGRP:], dram["b_r2_2"][0].partition_broadcast(P), "second")
        load(iota4[:, :], dram["c_iota4"], "router")
        load(small[:, :, 0:GRANK], weights("w_in_2", B_GA, GRANK), "narrow")
        load(small[:, :, 16:16 + IDIM + IH], weights("w_in_2", B_IK, IDIM + IH), "narrow")
        norm_gain(act, "ffn", "g_ffn", xT)
        units_act(act, SLAB["ffn"], FF // SW, 0)
        for b in (2, 3):
            act.wait_ge(slab_used, SLAB["ffn"] + 3 * (FF // SW))
            act.activation(x[:, 1, (b % 2) * 512:(b % 2 + 1) * 512], bank[b][:, :], ACT.Copy)\
               .then_inc(*b2_act.did("h", b - 2))

        norm_square(act, "final", x, b2_act.done("h", 1), b2_vec.done("h", 1))
        norm_square(act, "mix2", x, b2_vec.done("x2", 1))
        norm_gain(act, "mix2", "g_mix2", xT)
        act.wait_ge(*norm_pe.done("turn", "mix2", KT - 1))
        norm_square(act, "mem", mem, (loads["mem"], 16))
        norm_gain(act, "mem", "g_mem", memT)
        for j in range(8):
            slab_out(act, "memkv", j)
            for t in range(TT):
                act.activation((mk if j < 4 else mv)[:, t, (j % 4) * SW:(j % 4 + 1) * SW], half(SLAB["memkv"] + j, t),
                               ACT.Copy).then_inc(*half_read(SLAB["memkv"] + j))
        turned(act, "mk", 8, mkT, lambda k: col("g_mk", k % 2))
        turned(act, "mq", 8, mqT, lambda k: scaled[:, k % 2:k % 2 + 1])

        def store_mem(tt, g):
            for b in range(2):
                act.activation(o_mT[:, 4 * b:4 * b + 4, tt * P:(tt + 1) * P],
                               bank[2 + b][:, :].rearrange("p (k q) -> p k q", k=4), ACT.Copy)\
                   .then_inc(*(b2_act.did("o", "mem", tt, g) if b else b2_act.did("o_", "mem", tt, g)))

        attend_act(act, "mem", store_mem)
        for j in range(4):
            slab_out(act, "gqk", j)
            for n in range(2):
                act.activation(gqk[:, 2 * j + n, :], half(SLAB["gqk"] + j, n), ACT.Copy)\
                   .then_inc(*half_read(SLAB["gqk"] + j))
        for j in range(8):
            slab_out(act, "gvg", j)
            for t in range(TT):
                act.activation((gv if j < 4 else gg)[:, t, (j % 4) * SW:(j % 4 + 1) * SW],
                               half(SLAB["gvg"] + j, t), ACT.Copy if j < 4 else ACT.Silu)\
                   .then_inc(*half_read(SLAB["gvg"] + j))
        act.wait_ge(*b2_vec.done("lz"))
        act.activation(lz[:, :, :], lz[:, :, :], ACT.Exp, scale=-1.0).then_inc(*b2_act.did("lz"))
        act.wait_ge(*b2_act.done("lz"))
        act.activation(lz[:, :, :], lz[:, :, :], ACT.Ln, bias=1.0).then_inc(*b2_act.did("ln"))
        for t in range(TT):
            act.wait_ge(*b2_pe.done("cum", t))
            act.activation(cum[:, :, t * P:(t + 1) * P], bank[5 + t][:, :].rearrange("p (h q) -> p h q", h=GH),
                           ACT.Copy).then_inc(*b2_act.did("cum", t))
        act.wait_ge(*b2_act.done("cum", 1))
        act.activation(ex[:, :, :], cum[:, :, :], ACT.Exp, scale=1 / GTEMP).then_inc(*b2_act.did("ex", 0))
        act.activation(ki[:, :, :], cum[:, :, :], ACT.Exp, scale=-1 / GTEMP).then_inc(*b2_act.did("ex", 1))
        act.activation(decay[:, :, :], cum[:, :, GCHUNK - 1::GCHUNK], ACT.Exp, scale=1 / GTEMP)\
           .then_inc(*b2_act.did("decay"))
        act.wait_ge(*b2_vec.done("rest"))
        act.activation(ex[:, :, :], cum[:, :, :], ACT.Exp, scale=1 / GTEMP).then_inc(*b2_act.did("ex", 2))
        for t in range(TT):
            act.wait_ge(*b2_pe.done("ke_tok", t))
            act.activation(ke_tok[:, t, :, :], bank[6 + t][:, :].rearrange("p (h q) -> p h q", h=GH), ACT.Copy)\
               .then_inc(*b2_act.did("ke_tok", t))
        turned(act, "gla", 8, o_gT, lambda k: col("g_gla", k % 2))
        for j in range(2):
            slab_out(act, "dkv", j)
            for t in range(TT):
                act.activation((dk, dv)[j][:, t, :], half(SLAB["dkv"] + j, t), ACT.Copy)\
                   .then_inc(*half_read(SLAB["dkv"] + j))
        for j in range(2):
            slab_out(act, "iq", j)
            for n in range(2):
                act.activation(iqT[:, 2 * j + n, :], half(SLAB["iq"] + j, n), ACT.Copy)\
                   .then_inc(*half_read(SLAB["iq"] + j))
        turned(act, "dq", 8, dqT, lambda k: scaled[:, 2:3])
        turned(act, "dk", 2, dkT, lambda k: col("g_dk"))
        turned(act, "ik", 1, ikT[:, :].rearrange("p (a t) -> p a t", a=1), lambda k: col("g_ik"))
        for t in range(TT):
            K = (t + 1) * P
            act.wait_ge(*b2_pe.done("idx", t))
            if t:
                act.wait_ge(*b2_vec.done("idx", 0, IH - 1))
            for b in range(4):
                odd, i = b % 2, 2 * (b // 2)
                src = bank[2 + b][:, :].rearrange("p (h k) -> p h k", h=2)[:, :, 0:K]
                act.activation(relu[:, 2 * i + odd:2 * i + odd + 3:2, 0:K], src, ACT.Relu)\
                   .then_inc(*(b2_act.did("relu", t) if b == 3 else b2_act.did("relu_", t, b)))

        def store_dsa(tt, g):
            act.activation(o_dT[:, g * DREP:(g + 1) * DREP, tt * P:(tt + 1) * P],
                           bank[2][:, :].rearrange("p (h q) -> p h q", h=4), ACT.Copy)\
               .then_inc(*b2_act.did("o", "dsa", tt, g))

        attend_act(act, "dsa", store_dsa)
        for name, z, _ in BRANCHES:
            for j in range(4):
                s = SLAB[f"gate_{name}{j}"]
                slab_out(act, f"gate_{name}{j}", 0)
                m = BANKED[s] - 1
                act.wait_ge(bank_read[m % 2], 2 * (m // 2 + 1))
                for n in range(2):
                    act.activation(gated[:, n, :], half(s, n), ACT.Sigmoid, bias=col("b_gate", z * 8 + 2 * j + n))\
                       .then_inc(*half_read(s))
        norm_square(act, "ffn2", x, *all_out(SLAB["out2"] + 3))
        load(small[:, :, 0:NGRP], dram["w_r1_2"][0].rearrange("(k p) n -> p k n", p=P), "router")
        load(small[:, :, NGRP:NGRP + NEXP], dram["w_r2_2"][0].rearrange("(k p) n -> p k n", p=P), "router")
        norm_gain(act, "ffn2", "g_ffn2", xT)
        act.wait_ge(*b2_vec.done("rl"))
        act.activation(r_tmp[:, :, 0:NGRP], r_tmp[:, :, 0:NGRP], ACT.Exp).then_inc(*b2_act.did("g_exp"))
        act.wait_ge(*b2_vec.done("l2"))
        act.activation(r_s[:, 5, :], r_s[:, 4, :], ACT.Exp).then_inc(*b2_act.did("e_exp"))
        for n in range(8):
            act.wait_ge(*b2_pe.done("comb", n))
            act.activation(comb_all[:, 2 * n:2 * n + 2, :], bank[4 + n % 4][:, :].rearrange("p (e t) -> p e t", e=2),
                           ACT.Copy).then_inc(*b2_act.did("comb", n))
        units_act(act, SLAB["moe"], NEXP, FF // SW)
        for b in (2, 3):
            act.wait_ge(slab_used, SLAB["moe"] + 3 * NEXP)
            act.activation(x[:, 1, (b % 2) * 512:(b % 2 + 1) * 512], bank[b][:, :], ACT.Copy)\
               .then_inc(*b2_act.did("y", b - 2))

    @block.vector
    def _(vec):
        tt_, ts_, stt_ = vec.tensor_tensor, vec.tensor_scalar, vec.scalar_tensor_tensor
        for tile in range(2):
            vec.wait_ge(*setup_pe.done("cols", tile))
            vec.tensor_copy(cols[:, tile, 0:NROWS[tile]], bank[6 + tile][:, 0:NROWS[tile]])\
               .then_inc(*setup_vec.did("cols", tile))
        vec.wait_ge(*setup_pe.done("rev"))
        vec.tensor_copy(rev[:, :], bank[4][0:NH, 0:REV]).then_inc(*setup_vec.did("rev"))
        vec.wait_ge(*setup_pe.done("cmp_bias"))
        vec.tensor_copy(cmp_bias[:, :, :, :],
                        bank[5][:, 0:TT * NCMP * NH].rearrange("p (t c h) -> p t c h", t=TT, c=NCMP))\
           .then_inc(*setup_vec.did("cmp_bias"))

        norm_scale(vec, "mix", x)

        vec.wait_ge(loads["broadcast"], 16 * 6)
        for j in range(4):
            slab_out(vec, "vo", j)
            s = SLAB["vo"] + j
            for t in range(TT):
                if j < 2:
                    dst = v1[:, t, 2 * j:2 * j + 2, 0:MD]
                    src = half(s, t).rearrange("p (h d) -> p h d", h=2)
                    b = b_vo[:, j * SW:(j + 1) * SW].rearrange("p (h d) -> p h d", h=2)
                else:
                    dst, src = sig_o[:, t, (j - 2) * SW:(j - 1) * SW], half(s, t)
                    b = b_vo[:, j * SW:(j + 1) * SW]
                tt_(dst, src, b, ALU.add).then_inc(*half_read(s))
        vec.wait_ge(*in1_pe.done("small"))
        tt_(gate_in[:, :, :], bank[4][:, 0:64].rearrange("p (t n) -> p t n", t=TT),
            spread(b_small[:, :], (0, TT), (1, 32)), ALU.add).then_inc(*in1_vec.did("gate_in"))
        for j in range(2):
            slab_out(vec, "nq", j)
            s = SLAB["nq"] + j
            for n in range(2):
                ts_(nqT[:, 2 * j + n, :], half(s, n), col("b_nq", 2 * j + n), ND ** -0.5,
                    ALU.add, ALU.mult).then_inc(*half_read(s))
        for j in range(2):
            s = SLAB["kv"] + 1 + j
            other_half(vec, s)
            tt_(v_sw[:, j, :, :], half(s, 1).rearrange("p (t n) -> p t n", t=TT),
                spread(b_vs[:, j, :], (0, TT), (1, N_KV)), ALU.add).then_inc(*half_read(s))

        evicted(vec, SLAB["qk"] + 3)
        vec.wait_ge(*setup_pool.done("pad"))
        for j in range(4):
            for n in range(8):
                w = cols[:, ROW["conv"][0], ROW["conv"][1] + 8 * j + n:ROW["conv"][1] + 8 * j + n + 1]
                if j == 0:
                    ts_(qk[:, n, :], qk_pre[:, n, 0:T], w, None, ALU.mult).then_inc(*ml_vec.did("conv0", n))
                    continue
                vec.wait_ge(*ml_vec.done(f"conv{j - 1}", n))
                stt_(qk[:, n, :], qk_pre[:, n, j:j + T], w, qk[:, n, :], ALU.mult, ALU.add)\
                    .then_inc(*ml_vec.did(f"conv{j}" if j < 3 else "conv", n))
        for n in range(8):
            vec.wait_ge(*ml_act.done("sig", n))
            stt_(qk[:, n, :], sig[:, n, :], 1.0 if n < 4 else MD ** -0.5, qk[:, n, :], ALU.mult, ALU.mult)\
                .then_inc(*ml_vec.did("silu", n))
        vec.wait_ge(*in1_vec.done("gate_in"))
        tt_(fz[:, :, :], gate_in[:, :, 4:8], spread(b_fg[:, :], (0, TT), (1, MH)), ALU.add)\
            .then_inc(*ml_vec.did("fz"))
        vec.wait_ge(*ml_vec.done("fz"))
        stt_(fa[:, :, :], fz[:, :, :], -1.0, fz[:, :, :], ALU.mult, ALU.max).then_inc(*ml_vec.did("fa"))
        vec.wait_ge(loads["twice"], 16 * 4)
        for j in range(2):
            for g in range(NG):
                blocks = spread(cmp_in[:, j, g, 1:], (2, CMP_PAIRS), (CMP_STRIDE, NCMP))
                tile, at = ROW["pe"]
                pe_cols = along(cols[:, tile, at + CMP_PAIRS * j:at + CMP_PAIRS * (j + 1)], NCMP)
                tt_(blk[:, j, :, g, :], blocks, pe_cols, ALU.add).then_inc(*ns_vec.did("blk", j, g))
        vec.wait_ge(*ml_act.done("ln"))
        stt_(lf[:, :, :], fz[:, :, :], 0.0, fe[:, :, :], ALU.min, ALU.subtract).then_inc(*ml_vec.did("lf"))
        vec.wait_ge(*ns_act.done("hid_s"))
        tt_(hid[:, :, :], hid_s[:, :, :], bank[4][:, 0:2 * NG * NCMP].rearrange("p (j n) -> p j n", j=2), ALU.mult)\
            .then_inc(*ns_vec.did("hid"))
        vec.wait_ge(*ns_pe.done("kcT"))
        vec.tensor_copy(kcT[:, :], bank[5][:, 0:NG * NCMP]).then_inc(*ns_vec.did("kcT"))
        vec.tensor_copy(vc[:, :, :], bank[5][0:NCMP, 128:128 + NG * ND].rearrange("p (g d) -> p g d", g=NG))\
           .then_inc(*ns_vec.did("vc"))
        vec.wait_ge(*ml_pe.done("bc"))
        vec.tensor_copy(bc[:, :, :, :], bank[4][:, 0:4 * MH].rearrange("p (a t h) -> p a t h", a=2, t=TT))\
           .then_inc(*ml_vec.did("bc"))
        vec.wait_ge(*ml_vec.done("bc"))
        tt_(cc[:, :, :], gate_in[:, :, 0:4], bc[:, 0, :, :], ALU.subtract).then_inc(*ml_vec.did("cc"))
        for c in range(TT):
            vec.wait_ge(*ml_pe.done("crow", c))
            row = bank[5 + c][:, :].rearrange("p (h j) -> p h j", h=MH)
            if c == 0:
                vec.tensor_reduce(cx[:, :], row, AX.X, ALU.max).then_inc(*ml_vec.did("cx"))
            tt_(yy[:, c, :, :], row, spread(mask_after[:, :], (0, MH), (1, P)), ALU.add)\
                .then_inc(*ml_vec.did("masked", c))
        for c in range(TT):
            vec.wait_ge(*ml_vec.done("masked", c))
            vec.tensor_reduce(cm[:, c, :], yy[:, c, :, :], AX.X, ALU.max).then_inc(*ml_vec.did("cm", c))
        vec.wait_ge(*ml_vec.done("cm", 1))
        stt_(m1[:, :], cx[:, :], 0.0, bc[:, 1, 0, :], ALU.max, ALU.add).then_inc(*ml_vec.did("m1"))
        ts_(mm[:, 0, :], cm[:, 0, :], 0.0, None, ALU.max).then_inc(*ml_vec.did("mm", 0))
        vec.wait_ge(*ml_vec.done("m1"))
        tt_(mm[:, 1, :], cm[:, 1, :], m1[:, :], ALU.max).then_inc(*ml_vec.did("mm", 1))
        tt_(w_st[:, 0, :], cc[:, 0, :], bc[:, 1, 0, :], ALU.add).then_inc(*ml_vec.did("a0"))
        vec.wait_ge(*ml_vec.done("a0"))
        tt_(w_st[:, 0, :], w_st[:, 0, :], m1[:, :], ALU.subtract).then_inc(*ml_vec.did("a0m"))
        tt_(w_st[:, 1, :], m1[:, :], mm[:, 1, :], ALU.subtract).then_inc(*ml_vec.did("s_inter"))
        ts_(w_st[:, 2, :], m1[:, :], 0.0, None, ALU.mult).then_inc(*ml_vec.did("w_st"))
        tt_(em[:, :, :], bc[:, 0, :, :], mm[:, :, :], ALU.add).then_inc(*ml_vec.did("em"))
        for c in range(TT):
            vec.wait_ge(*ml_pe.done("mrow", c))
            for h in range(MH):
                ins = stt_(yy[:, c, h, :], bank[5 + c][:, h * P:(h + 1) * P], cc[:, c, h:h + 1], mask_before[:, :],
                           ALU.subtract, ALU.add)
                ins.then_inc(*(ml_vec.did("yy", c) if h == MH - 1 else ml_vec.did("yy_", c, h)))
        for c, b in enumerate((4, 7)):
            vec.wait_ge(*ml_act.done("yy", c))
            vec.wait_ge(*ml_pe.done("st", c))
            tt_(pT[:, c, :, :], yy[:, c, :, :], bank[b][:, :].rearrange("p (h j) -> p h j", h=MH), ALU.mult)\
                .then_inc(*ml_vec.did("pT", c))
        vec.wait_ge(*ml_act.done("w_st"))
        tt_(wv[:, :, :], v1[:, 0, :, :], along(w_st[:, 0, :], MD + 1), ALU.mult).then_inc(*ml_vec.did("wv"))
        for n, b in enumerate((5, 7)):
            vec.wait_ge(*ml_pe.done("inter", n))
            vec.wait_ge(*ml_act.done("num", 1, n))
            for i in range(2):
                h = 2 * n + i
                stt_(hh[:, 1, h, :], bank[b][:, i * (MD + 1):(i + 1) * (MD + 1)], w_st[:, 1, h:h + 1],
                     hh[:, 1, h, :], ALU.mult, ALU.add).then_inc(*ml_vec.did("hh", h))
        vec.wait_ge(*ml_act.done("em"))
        vec.wait_ge(*ml_vec.done("hh", 3))
        for c in range(TT):
            stt_(den[:, c, :], hh[:, c, :, MD], -1.0, hh[:, c, :, MD], ALU.mult, ALU.max).then_inc(*ml_vec.did("abs", c))
        vec.wait_ge(*ml_vec.done("abs", 1))
        tt_(den[:, :, :], den[:, :, :], em[:, :, :], ALU.max).then_inc(*ml_vec.did("den", 1))
        vec.wait_ge(*ml_vec.done("den", 1))
        vec.reciprocal(den[:, :, :], den[:, :, :]).then_inc(*ml_vec.did("rden"))
        vec.wait_ge(*ml_vec.done("rden"))
        for c in range(TT):
            tt_(hn[:, c, :, :], hh[:, c, :, 0:MD], along(den[:, c, :], MD), ALU.mult).then_inc(*ml_vec.did("hn", c))
        for c in range(TT):
            vec.wait_ge(*ml_vec.done("hn", c))
            tt_(hsq[:, c, :, :], hn[:, c, :, :], hn[:, c, :, :], ALU.mult).then_inc(*ml_vec.did("hsq", c))
        for c in range(TT):
            vec.wait_ge(*ml_vec.done("hsq", c))
            vec.tensor_reduce(den[:, c, :], hsq[:, c, :, :], AX.X, ALU.add).then_inc(*ml_vec.did("ssq", c))
        vec.wait_ge(*ml_vec.done("ssq", 1))
        ts_(den[:, :, :], den[:, :, :], 1.0 / MD, EPS, ALU.mult, ALU.add).then_inc(*ml_vec.did("var"))
        vec.wait_ge(*ml_pool.done("root"))
        for c in range(TT):
            tt_(hn[:, c, :, :], hn[:, c, :, :], along(den[:, c, :], MD), ALU.mult).then_inc(*ml_vec.did("hn2", c))
        vec.wait_ge(*ml_act.done("sig_o"))
        for c in range(TT):
            vec.wait_ge(*ml_vec.done("hn2", c))
            tt_(hn[:, c, :, :], hn[:, c, :, :], sig_o[:, c, :].rearrange("p (h d) -> p h d", h=MH), ALU.mult)\
                .then_inc(*ml_vec.did("ym", c))

        vec.wait_ge(*ns_pe.done("lc"))
        for t in range(TT):
            for odd in range(2):
                tt_(lc[:, t, odd::2, :],
                    bank[6 + odd][:, t * NREP * NCMP:(t + 1) * NREP * NCMP].rearrange("p (h c) -> p h c", h=NREP),
                    cmp_bias[:, t, :, odd::2].rearrange("p c h -> p h c"), ALU.add)\
                    .then_inc(*ns_vec.did("lc_", t, odd))
        vec.wait_ge(*ns_vec.done("lc_", 1, 1))
        vec.tensor_reduce(mc[:, :, :], lc[:, :, :, :], AX.X, ALU.max).then_inc(*ns_vec.did("mc"))
        vec.wait_ge(*ns_vec.done("mc"))
        flat = lc[:, :, :, :].rearrange("p t h c -> p (t h) c")
        tt_(flat, flat, along(mc[:, :, :].rearrange("p t h -> p (t h)"), NCMP), ALU.subtract)\
            .then_inc(*ns_vec.did("lc"))
        vec.wait_ge(*ns_act.done("ec"))
        for t in range(TT):
            tt_(ec[:, t, :, :], ec[:, t, :, :], spread(seen[:, t, :], (0, NH), (1, NCMP)), ALU.mult)\
                .then_inc(*ns_vec.did("ec_", t))
        vec.wait_ge(*ns_vec.done("ec_", 1))
        vec.tensor_reduce(sc[:, :, :], ec[:, :, :, :], AX.X, ALU.add).then_inc(*ns_vec.did("sc"))
        vec.wait_ge(*ns_vec.done("sc"))
        ts_(sc[:, :, :], sc[:, :, :], 1e-30, None, ALU.max).then_inc(*ns_vec.did("sc1"))
        vec.wait_ge(*ns_vec.done("sc1"))
        vec.reciprocal(sc[:, :, :], sc[:, :, :]).then_inc(*ns_vec.did("sc2"))
        vec.wait_ge(*ns_vec.done("sc2"))
        vec.wait_ge(*ns_act.done("gate"))
        gates = nsa_gate[:, :, :].rearrange("p t (h b) -> p t h b", b=3)
        tt_(sc[:, :, :], sc[:, :, :], gates[:, :, :, 0], ALU.mult).then_inc(*ns_vec.did("sc3"))
        vec.wait_ge(*ns_vec.done("sc3"))
        flat = ec[:, :, :, :].rearrange("p t h c -> p (t h) c")
        tt_(flat, flat, along(sc[:, :, :].rearrange("p t h -> p (t h)"), NCMP), ALU.mult)\
            .then_inc(*ns_vec.did("pc"))
        vec.wait_ge(loads["strip"], 16)
        for u in range(8):
            tt, g, br = u // 4, u // 2 % 2, u % 2
            K = (tt + 1) * P
            l = lg[:, u % 2, :, 0:K]
            if u >= 2:
                vec.wait_ge(*ns_pe.done("aT", u - 2, (u - 2) // 4))
            for odd in range(2):
                vec.wait_ge(*ns_pe.done("lg", u))
                tt_(lg[:, u % 2, 2 * odd:2 * odd + 2, 0:K],
                    bank[4 + odd][:, 0:2 * K].rearrange("p (h k) -> p h k", h=2),
                    strip[:, g * NREP + odd:(g + 1) * NREP:2, T - K:T], ALU.add)\
                    .then_inc(*ns_vec.did("lg", u, odd))
            vec.wait_ge(*ns_vec.done("lg", u, 1))
            vec.tensor_reduce(mx[:, u % 2, :], l, AX.X, ALU.max).then_inc(*ns_vec.did("mx", u))
            vec.wait_ge(*ns_vec.done("mx", u))
            tt_(l, l, along(mx[:, u % 2, :], K), ALU.subtract).then_inc(*ns_vec.did("shift", u))
            vec.wait_ge(*ns_act.done("exp", u))
            vec.tensor_reduce(sm[:, u % 2, :], l, AX.X, ALU.add).then_inc(*ns_vec.did("sm", u))
            vec.wait_ge(*ns_vec.done("sm", u))
            vec.reciprocal(sm[:, u % 2, :], sm[:, u % 2, :]).then_inc(*ns_vec.did("rs", u))
            vec.wait_ge(*ns_vec.done("rs", u))
            tt_(sm[:, u % 2, :].rearrange("p (o i) -> p o i", o=2), sm[:, u % 2, :].rearrange("p (o i) -> p o i", o=2),
                gates[:, tt, g * NREP:(g + 1) * NREP, 1 + br].rearrange("p (i o) -> p o i", o=2), ALU.mult)\
                .then_inc(*ns_vec.did("gs", u))
            vec.wait_ge(*ns_vec.done("gs", u))
            tt_(l, l, along(sm[:, u % 2, :], K), ALU.mult).then_inc(*ns_vec.did("p", u))

        evicted(vec, SLAB["merge"] + 7)
        for j in range(4):
            slab_out(vec, "branch", j)
            pair_m = mergeT[:, 2 * j:2 * j + 2, :].rearrange("p n t -> p (n t)")
            pair_n = mergeT[:, 8 + 2 * j:10 + 2 * j, :].rearrange("p n t -> p (n t)")
            b = 4 + 2 * (j % 2)
            tt_(mix2[:, 0, :], bank[b][:, :], pair_m, ALU.mult).then_inc(*mix_vec.did("m", j))
            tt_(mix2[:, 1, :], bank[b + 1][:, :], pair_n, ALU.mult).then_inc(*mix_vec.did("n", j))
            vec.wait_ge(*mix_vec.done("n", j))
            tt_(mixT[:, 2 * j:2 * j + 2, :].rearrange("p n t -> p (n t)"), mix2[:, 0, :], mix2[:, 1, :], ALU.add)\
                .then_inc(*mix_vec.did("mix", j))
            vec.wait_ge(*mix_vec.done("mix", j))
        for j in range(4):
            slab_out(vec, "out", j)
            s = SLAB["out"] + j
            for t in range(TT):
                tt_(x[:, t, j * SW:(j + 1) * SW], half(s, t), x[:, t, j * SW:(j + 1) * SW], ALU.add)\
                    .then_inc(*half_read(s))

        norm_scale(vec, "ffn", x)
        units_vec(vec, SLAB["ffn"], FF // SW, 0, None)
        for b in (0, 1):
            vec.wait_ge(slab_used, SLAB["ffn"] + 3 * (FF // SW))
            vec.tensor_copy(x[:, 0, b * 512:(b + 1) * 512], bank[b][:, :]).then_inc(*b2_vec.did("h", b))

        norm_scale(vec, "final", x)
        vec.wait_ge(loads["g_fin"], 16)
        for t in range(TT):
            vec.wait_ge(*norm_vec.done("scale", "final", t))
            tt_(x[:, t, :], xn[:, t, :], g_fin[:, :], ALU.mult).then_inc(*b2_vec.did("x2", t))
        for n in range(3):
            ts_(scaled[:, n:n + 1], col("g_mq", n) if n < 2 else col("g_dq"), (ED if n < 2 else DD) ** -0.5, None,
                ALU.mult).then_inc(*b2_vec.did("scaled", n))
        norm_scale(vec, "mix2", x)
        norm_scale(vec, "mem", mem)
        for j in range(4):
            slab_out(vec, "mq", j)
            for t in range(TT):
                vec.tensor_copy(mq[:, t, j * SW:(j + 1) * SW], half(SLAB["mq"] + j, t))\
                   .then_inc(*half_read(SLAB["mq"] + j))
        evicted(vec, SLAB["memkv"] + 3)
        head_norm(vec, "mk", mk, EH, ED)
        evicted(vec, SLAB["mq"] + 3)
        vec.wait_ge(*norm_vec.done("scaled", "mk"))
        head_norm(vec, "mq", mq, EH, ED)
        attend_vec(vec, "mem", False)
        vec.wait_ge(*b2_pe.done("a_low"))
        vec.tensor_copy(a_low[:, :], bank[4][0:GRANK, 0:T]).then_inc(*b2_vec.did("a_low"))
        vec.wait_ge(loads["second"], 16 * 4)
        for t in range(TT):
            vec.wait_ge(*b2_pe.done("la", t))
            tt_(la[:, t, :], bank[5 + t][:, :], b_a2[:, :], ALU.add).then_inc(*b2_vec.did("z", t))
        vec.wait_ge(*b2_vec.done("z", 1))
        fl, fz_ = la[:, :, :].rearrange("p t n -> p (t n)"), lz[:, :, :].rearrange("p t n -> p (t n)")
        stt_(fz_, fl, -1.0, fl, ALU.mult, ALU.max).then_inc(*b2_vec.did("lz"))
        vec.wait_ge(*b2_act.done("ln"))
        stt_(fl, fl, 0.0, fz_, ALU.min, ALU.subtract).then_inc(*b2_vec.did("la"))
        evicted(vec, SLAB["gqk"] + 3)
        q_, k_ = (gqk[:, n * GH:(n + 1) * GH, :].rearrange("p h t -> p (h t)") for n in range(2))
        ex_, ki_, cum_ = (a[:, :, :].rearrange("p h t -> p (h t)") for a in (ex, ki, cum))
        vec.wait_ge(*b2_act.done("ex", 1))
        stt_(q_, q_, GK ** -0.5, ex_, ALU.mult, ALU.mult).then_inc(*b2_vec.did("qd"))
        tt_(ki_, ki_, k_, ALU.mult).then_inc(*b2_vec.did("ki"))
        vec.wait_ge(*b2_act.done("decay"))
        vec.wait_ge(*b2_vec.done("qd"))
        groups = cum_.rearrange("p (n c) -> p n c", c=GCHUNK)
        tt_(ex_.rearrange("p (n c) -> p n c", c=GCHUNK),
            bass.AP(tensor=groups.tensor, offset=groups.offset + GCHUNK - 1,
                    ap=[list(groups.ap[0]), [GCHUNK, GH * T // GCHUNK], [0, GCHUNK]]), groups, ALU.subtract)\
            .then_inc(*b2_vec.did("rest_"))
        vec.wait_ge(*b2_vec.done("rest_"))
        vec.tensor_copy(cum_, ex_).then_inc(*b2_vec.did("rest"))
        vec.wait_ge(*b2_act.done("ex", 2))
        vec.wait_ge(*b2_vec.done("ki"))
        tt_(k_, k_, ex_, ALU.mult).then_inc(*b2_vec.did("ke"))
        for t in range(TT):
            vec.wait_ge(*b2_pe.done("att", t))
            stt_(att[:, t, :, :], bank[4 + t][:, :].rearrange("p (h q) -> p h q", h=GH), 3e38,
                 spread(tri64[:, :], (0, GH), (1, P)), ALU.min, ALU.mult).then_inc(*b2_vec.did("att", t))
        for n in range(3):
            vec.wait_ge(*b2_pe.done("state", n))
            if n:
                vec.wait_ge(*b2_vec.done("state", n - 1))
            for h in range(GH):
                src = bank[2 + 2 * n + h // 2][:, (h % 2) * GV:(h % 2 + 1) * GV]
                step = b2_vec.did("state", n) if h == GH - 1 else b2_vec.did("state_", n, h)
                if n == 0:
                    vec.tensor_copy(state[:, n, h, :], src).then_inc(*step)
                else:
                    stt_(state[:, n, h, :], state[:, n - 1, h, :], decay[:, h, n:n + 1], src, ALU.mult, ALU.add)\
                        .then_inc(*step)
        for t in range(TT):
            for b in range(2):
                vec.wait_ge(*b2_pe.done("o", t, 2 * b + 1, 1))
                vec.tensor_copy(xn[:, t, b * 512:(b + 1) * 512], bank[4 + 2 * t + b][:, :])\
                   .then_inc(*b2_vec.did("o_raw", t, b))
        vec.wait_ge(*b2_vec.done("o_raw", 1, 1))
        head_norm(vec, "gla", xn, GH, GV)
        evicted(vec, SLAB["gvg"] + 7)
        vec.wait_ge(*norm_vec.done("scaled", "gla"))
        xn_, gg_ = (a[:, :, :].rearrange("p t n -> p (t n)") for a in (xn, gg))
        tt_(xn_, xn_, gg_, ALU.mult).then_inc(*b2_vec.did("gated"))
        for j in range(4):
            slab_out(vec, "dq", j)
            for t in range(TT):
                vec.tensor_copy(dq[:, t, j * SW:(j + 1) * SW], half(SLAB["dq"] + j, t))\
                   .then_inc(*half_read(SLAB["dq"] + j))
        vec.wait_ge(*b2_pe.done("ikw"))
        vec.tensor_copy(ikw[:, :, :], bank[2][:, 0:TT * 72].rearrange("p (t n) -> p t n", t=TT))\
           .then_inc(*b2_vec.did("ikw"))
        evicted(vec, SLAB["dq"] + 3)
        head_norm(vec, "dq", dq, DH, DD)
        evicted(vec, SLAB["dkv"] + 1)
        vec.wait_ge(*norm_vec.done("scaled", "dq"))
        head_norm(vec, "dk", dk, DG, DD)
        vec.wait_ge(*b2_vec.done("ikw"))
        vec.wait_ge(*norm_vec.done("scaled", "dk"))
        for t in range(TT):
            tt_(sq[:, t, 0:IDIM], ikw[:, t, 0:IDIM], ikw[:, t, 0:IDIM], ALU.mult).then_inc(*b2_vec.did("ik_sq", t))
        vec.wait_ge(*b2_vec.done("ik_sq", 1))
        vec.tensor_reduce(s16[:, 0, 0:TT], sq[:, 0:TT, 0:IDIM], AX.X, ALU.add).then_inc(*b2_vec.did("ik_sum"))
        vec.wait_ge(*b2_vec.done("ik_sum"))
        ts_(s16[:, 0, 0:TT], s16[:, 0, 0:TT], 1.0 / IDIM, EPS, ALU.mult, ALU.add).then_inc(*norm_vec.did("mean", "ik"))
        vec.wait_ge(*norm_pool.done("root", "ik"))
        for t in range(TT):
            for a in range(2):
                ts_(ik2[:, t, a, :], ikw[:, t, 0:IDIM], s16[:, 0, t:t + 1], None, ALU.mult)\
                    .then_inc(*(b2_vec.did("ik2") if t and a else b2_vec.did("ik2_", t, a)))
        ts_(ikw[:, :, IDIM:], ikw[:, :, IDIM:], IH ** -0.5 * IDIM ** -0.5, None, ALU.mult).then_inc(*b2_vec.did("iw"))
        vec.wait_ge(*b2_vec.done("iw"))
        for t in range(TT):
            K = (t + 1) * P
            vec.wait_ge(*b2_act.done("relu", t))
            for h in range(IH):
                w = ikw[:, t, IDIM + h:IDIM + h + 1]
                if h == 0:
                    ts_(score[:, t, 0:K], relu[:, h, 0:K], w, None, ALU.mult).then_inc(*b2_vec.did("idx", t, h))
                    continue
                vec.wait_ge(*b2_vec.done("idx", t, h - 1))
                stt_(score[:, t, 0:K], relu[:, h, 0:K], w, score[:, t, 0:K], ALU.mult, ALU.add)\
                    .then_inc(*b2_vec.did("idx", t, h))
        for t in range(TT):
            K = (t + 1) * P
            sc_, mask = score[:, t, 0:K], causal[:, T - K:T]
            vec.wait_ge(*b2_vec.done("idx", t, IH - 1))
            tt_(sc_, sc_, mask, ALU.add).then_inc(*b2_vec.did("allowed", t))
            vec.wait_ge(*b2_vec.done("allowed", t))
            for r in range(TOPK // 8):
                vec.max(best[:, t, :], sc_).then_inc(*b2_vec.did("max", t, r))
                vec.wait_ge(*b2_vec.done("max", t, r))
                vec.match_replace(sc_, best[:, t, :], sc_, MARK).then_inc(*b2_vec.did("match", t, r))
                vec.wait_ge(*b2_vec.done("match", t, r))
            ts_(pick[:, t, 0:K], sc_, MARK, NEG, ALU.not_equal, ALU.mult).then_inc(*b2_vec.did("picked", t))
            vec.wait_ge(*b2_vec.done("picked", t))
            tt_(pick[:, t, 0:K], pick[:, t, 0:K], mask, ALU.min).then_inc(*b2_vec.did("pick", t))
        vec.wait_ge(*b2_vec.done("pick", 1))
        attend_vec(vec, "dsa", True)
        for name, z, _ in BRANCHES:
            for j in range(4):
                g_s, o_s = SLAB[f"gate_{name}{j}"], SLAB[f"o_{name}{j}"]
                vec.wait_ge(bank_read[BANKED[g_s] % 2], 2 * (BANKED[g_s] // 2 + 1))
                slab_out(vec, f"o_{name}{j}", 0)
                first_ = name == BRANCHES[0][0]
                for n in range(2):
                    dst = mergedT[:, 2 * j + n, :]
                    tt_(dst if first_ else hT[:, n, :], half(o_s, n), gated[:, n, :], ALU.mult)\
                        .then_inc(*half_read(o_s))
                if not first_:
                    vec.wait_ge(bank_read[BANKED[o_s] % 2], 2 * (BANKED[o_s] // 2 + 1))
                    for n in range(2):
                        dst = mergedT[:, 2 * j + n, :]
                        tt_(dst, dst, hT[:, n, :], ALU.add)\
                            .then_inc(*(b2_vec.did("merged", name, j) if n else b2_vec.did("merged_", name, j)))
                    vec.wait_ge(*b2_vec.done("merged", name, j))
        for j in range(4):
            s = SLAB["out2"] + j
            slab_out(vec, "out2", j)
            for t in range(TT):
                tt_(x[:, t, j * SW:(j + 1) * SW], half(s, t), x[:, t, j * SW:(j + 1) * SW], ALU.add)\
                    .then_inc(*half_read(s))

        norm_scale(vec, "ffn2", x)
        steps = [0]

        def then(ins):
            steps[0] += 1
            ins.then_inc(*b2_vec.did("route", steps[0]))
            vec.wait_ge(*b2_vec.done("route", steps[0]))

        R_ = NGRP + NEXP
        vec.wait_ge(*b2_pe.done("router"))
        vec.wait_ge(loads["router"], 16 * 3)
        then(tt_(rl[:, :, :], bank[2][:, 0:TT * R_].rearrange("p (t n) -> p t n", t=TT),
                 spread(b_r[:, :], (0, TT), (1, R_)), ALU.add))

        def first_best(value, best_, one):
            then(vec.tensor_reduce(best_, value, AX.X, ALU.max))
            then(tt_(r_key[:, :, :], value, along(best_, 4), ALU.is_equal))
            then(stt_(r_key[:, :, :], r_key[:, :, :], -16.0, spread(iota4[:, :], (0, TT), (1, 4)), ALU.mult, ALU.add))
            then(vec.tensor_reduce(r_s[:, 7, :], r_key[:, :, :], AX.X, ALU.min))
            then(tt_(one, r_key[:, :, :], along(r_s[:, 7, :], 4), ALU.is_equal))

        group = rl[:, :, 0:NGRP]
        first_best(group, r_s[:, 0, :], r_one[:, 0, :, :])
        tt_(r_tmp[:, :, 0:NGRP], group, along(r_s[:, 0, :], NGRP), ALU.subtract).then_inc(*b2_vec.did("rl"))
        vec.wait_ge(*b2_act.done("g_exp"))
        then(vec.tensor_reduce(r_s[:, 1, :], r_tmp[:, :, 0:NGRP], AX.X, ALU.add))
        then(vec.reciprocal(r_s[:, 1, :], r_s[:, 1, :]))
        for t in range(TT):
            then(tt_(r_tmp[:, t, :].rearrange("p (g e) -> p g e", g=NGRP),
                     rl[:, t, NGRP:].rearrange("p (g e) -> p g e", g=NGRP), along(r_one[:, 0, t, :], PERG), ALU.mult))
        then(vec.tensor_reduce(r_el[:, :, :], r_tmp[:, :, :].rearrange("p t (g e) -> p t e g", g=NGRP), AX.X, ALU.add))
        first_best(r_el[:, :, :], r_s[:, 2, :], r_one[:, 1, :, :])
        then(stt_(r_el[:, :, :], r_one[:, 1, :, :], NEG, r_el[:, :, :], ALU.mult, ALU.add))
        first_best(r_el[:, :, :], r_s[:, 3, :], r_one[:, 2, :, :])
        tt_(r_s[:, 4, :], r_s[:, 3, :], r_s[:, 2, :], ALU.subtract).then_inc(*b2_vec.did("l2"))
        vec.wait_ge(*b2_act.done("e_exp"))
        then(ts_(r_s[:, 6, :], r_s[:, 5, :], 1.0, None, ALU.add))
        then(vec.reciprocal(r_s[:, 6, :], r_s[:, 6, :]))
        then(tt_(r_s[:, 6, :], r_s[:, 6, :], r_s[:, 1, :], ALU.mult))
        then(tt_(r_s[:, 5, :], r_s[:, 5, :], r_s[:, 6, :], ALU.mult))
        then(tt_(r_one[:, 1, :, :], r_one[:, 1, :, :], along(r_s[:, 6, :], 4), ALU.mult))
        then(tt_(r_one[:, 2, :, :], r_one[:, 2, :, :], along(r_s[:, 5, :], 4), ALU.mult))
        then(tt_(r_el[:, :, :], r_one[:, 1, :, :], r_one[:, 2, :, :], ALU.add))
        for t in range(TT):
            tt_(comb[:, t, :].rearrange("p (g e) -> p g e", g=NGRP), along(r_one[:, 0, t, :], PERG),
                spread(r_el[:, t, :], (0, NGRP), (1, PERG)), ALU.mult).then_inc(*b2_vec.did("comb", t))
        vec.wait_ge(*b2_act.done("comb", 7))
        units_vec(vec, SLAB["moe"], NEXP, FF // SW, comb_all[:, :, :].rearrange("p e t -> p (e t)"))
        for b in (0, 1):
            vec.wait_ge(slab_used, SLAB["moe"] + 3 * NEXP)
            vec.tensor_copy(x[:, 0, b * 512:(b + 1) * 512], bank[b][:, :]).then_inc(*b2_vec.did("y", b))

    @block.tensor
    def _(pe):
        mm_ = pe.matmul
        pe.wait_ge(loads["const"], 16 * 6)
        pe.wait_ge(loads["rows"], 16 * ROW_LOADS)
        for tile in range(2):
            n = NROWS[tile]
            pe.transpose(bank[6 + tile][:, 0:n], rows[0:n, tile, :], ident[0:n, 0:n])\
              .then_inc(*setup_pe.did("cols", tile))
        pe.wait_ge(loads["rel"], 16 * 5)
        mm_(bank[4][0:NH, 0:REV], rel[:, :], oh_rev[:, :], start=True, stop=True).then_inc(*setup_pe.did("rev"))
        for t in range(TT):
            for c in range(NCMP):
                at = OH_CMP0 + t * P - CMP_STRIDE * c - (CMP_BLOCK - 1)
                n = (t * NCMP + c) * NH
                ins = mm_(bank[5][:, n:n + NH], oh_cmp[:, at:at + P], rel[:, :], start=True, stop=True)
        ins.then_inc(*setup_pe.did("cmp_bias"))

        norm_turn(pe, "mix", setup_vec.done("cmp_bias"), setup_vec.done("cols", 1), setup_vec.done("rev"))

        pe.wait_ge(*norm_act.done("gain", "mix", KT - 1))
        slabs(pe, "qk", slab_rows, xT)
        slabs(pe, "vo", slab_tokens, xT)
        pe.wait_ge(loads["small"], 32)
        for t in range(TT):
            for k in range(KT):
                ins = mm_(bank[4][:, t * 32:(t + 1) * 32], xT[:, k, t * P:(t + 1) * P], small[:, k, 0:32],
                          start=(k == 0), stop=(k == KT - 1))
        ins.then_inc(*in1_pe.did("small"))
        slabs(pe, "nq", slab_rows, xT, 0, 2)
        for j in range(3):
            s = SLAB["kv"] + j
            slab_in(pe, s)
            if j == 0:
                slab_rows(pe, s, xT).then_inc(slab_used, 1)
                continue
            for k in range(KT):
                mm_(half(s, 0), ring[:, s % RING, k, 0:P], xT[:, k, :], start=(k == 0), stop=(k == KT - 1))
            for t in range(TT):
                for k in range(KT):
                    ins = mm_(half(s, 1)[:, t * P:(t + 1) * P], xT[:, k, t * P:(t + 1) * P],
                              ring[:, s % RING, k, P:2 * P], start=(k == 0), stop=(k == KT - 1))
            ins.then_inc(slab_used, 1)
        slabs(pe, "merge", slab_rows, xT, 0, 4)

        pe.wait_ge(loads["cmp"], 16 * 5)
        pe.wait_ge(*ns_vec.done("blk", 1, 1))
        pe.wait_ge(*in1_vec.done("gate_in"))
        for j in range(2):
            for n in range(CMP_PAIRS):
                ins = mm_(bank[4][:, j * NG * NCMP:(j + 1) * NG * NCMP], w_cmp1[:, j, n, :],
                          blk[:, j, n, :, :].rearrange("p g c -> p (g c)"),
                          start=(n == 0), stop=(n == CMP_PAIRS - 1))
        ins.then_inc(*ns_pe.did("hid"))
        pe.wait_ge(*ns_vec.done("hid"))
        mm_(bank[5][:, 0:NG * NCMP], w_cmp2k[:, :, :].rearrange("p a d -> p (a d)"), hid[:, 0, :],
            start=True, stop=True)
        for g in range(NG):
            ins = mm_(bank[5][0:NCMP, 128 + g * ND:128 + (g + 1) * ND], hid[:, 1, g * NCMP:(g + 1) * NCMP],
                      w_cmp2v[:, :], start=True, stop=True)
        ins.then_inc(*ns_pe.did("kcT"))

        slabs(pe, "merge", slab_rows, xT, 4, 8)

        pe.wait_ge(*setup_pool.done("ones"))
        pe.wait_ge(*ml_vec.done("lf"))
        mm_(bank[4][:, 0:8], tri[:, :], lf[:, :, :].rearrange("p t h -> p (t h)"), start=True, stop=True)
        mm_(bank[4][:, 8:16], ones[:, :], lf[:, :, :].rearrange("p t h -> p (t h)"), start=True, stop=True)\
            .then_inc(*ml_pe.did("bc"))
        pe.wait_ge(*ml_vec.done("silu", 7))
        pe.wait_ge(*ml_vec.done("bc"))
        for c, b in enumerate((4, 7)):
            for h in range(MH):
                ins = mm_(bank[b][:, h * P:(h + 1) * P], qk[:, 4 + h, c * P:(c + 1) * P], qk[:, h, c * P:(c + 1) * P],
                          start=True, stop=True)
            ins.then_inc(*ml_pe.did("st", c))
        pe.wait_ge(*ml_vec.done("cc"))
        pe.wait_ge(*ns_vec.done("vc"))
        for c in range(TT):
            for h in range(MH):
                ins = mm_(bank[5 + c][:, h * P:(h + 1) * P], spread(cc[:, c, h:h + 1], (0, P)), ident[:, :],
                          start=True, stop=True)
            ins.then_inc(*ml_pe.did("crow", c))
        pe.wait_ge(*ml_vec.done("mm", 1))
        for c in range(TT):
            pe.wait_ge(*ml_vec.done("masked", c))
            for h in range(MH):
                ins = mm_(bank[5 + c][:, h * P:(h + 1) * P], spread(mm[:, c, h:h + 1], (0, P)), ident[:, :],
                          start=True, stop=True)
            ins.then_inc(*ml_pe.did("mrow", c))
        pe.wait_ge(*ml_vec.done("yy", 0))
        for h in range(MH):
            ins = pe.transpose(bank[5][:, h * P:(h + 1) * P], qk[:, 4 + h, 0:P], ident[:, :])
        ins.then_inc(*ml_pe.did("k_tok"))
        pe.wait_ge(*ml_act.done("k_tok"))
        pe.wait_ge(*ml_vec.done("wv"))
        pe.wait_ge(*ml_vec.done("yy", 1))
        E1 = MD + 1
        for n, b in enumerate((6, 4)):
            if n:
                pe.wait_ge(*ml_vec.done("pT", 0))
            for i in range(2):
                ins = mm_(bank[b][:, i * E1:(i + 1) * E1], k_tok[:, 2 * n + i, :], wv[:, 2 * n + i, :],
                          start=True, stop=True)
            ins.then_inc(*ml_pe.did("c1", n))
        for c, banks in enumerate(((5, 7), (6, 4))):
            pe.wait_ge(*ml_vec.done("pT", 1))
            for n, b in enumerate(banks):
                if c:
                    pe.wait_ge(*ml_act.done("c1", n))
                for i in range(2):
                    h = 2 * n + i
                    ins = mm_(bank[b][:, i * E1:(i + 1) * E1], pT[:, c, h, :], v1[:, c, h, :], start=True, stop=True)
                ins.then_inc(*ml_pe.did("num", c, n))
        for n, b in enumerate((5, 7)):
            pe.wait_ge(*ml_act.done("num", 0, n))
            for i in range(2):
                h = 2 * n + i
                ins = mm_(bank[b][:, i * E1:(i + 1) * E1], qk[:, h, P:T], c1[:, h, :], start=True, stop=True)
            ins.then_inc(*ml_pe.did("inter", n))
        pe.wait_ge(*ml_vec.done("ym", 1))
        pe.wait_ge(*ml_act.done("num", 1, 1))
        for k in range(4):
            for t in range(TT):
                at = (k % 2) * T + t * P
                ins = pe.transpose(bank[(4, 6)[k // 2]][:, at:at + P], hn[:, t, k, :], ident[:, :])
            if k % 2:
                ins.then_inc(*ml_pe.did("yT", k // 2))

        pe.wait_ge(*ml_act.done("yT", 3))
        evicted(pe, SLAB["nq"] + 1)
        pe.wait_ge(*ns_vec.done("vc"))
        for t in range(TT):
            for h in range(NH):
                lo, at = ND * (h % 2), (t * NREP + h // 2) * NCMP
                ins = mm_(bank[6 + h % 2][:, at:at + NCMP], nqT[lo:lo + ND, h // 2, t * P:(t + 1) * P],
                          kcT[lo:lo + ND, (h // NREP) * NCMP:(h // NREP + 1) * NCMP], start=True, stop=True)
        ins.then_inc(*ns_pe.did("lc"))
        pe.wait_ge(*ns_vec.done("pc"))
        pe.wait_ge(*ml_vec.done("hh", 3))
        for n, b in enumerate((7, 4, 5, 6)):
            for i in range(4):
                ins = pe.transpose(bank[b][0:NCMP, i * P:(i + 1) * P], ec[:, n // 2, (n % 2) * 4 + i, :], ident[:, :])
            ins.then_inc(*ns_pe.did("pcT", n))
        pe.wait_ge(*ns_act.done("pcT", 3))
        pe.wait_ge(loads["twice"], 16 * 4)
        evicted(pe, SLAB["kv"] + 2)

        def logits(u):
            tt, g, br = u // 4, u // 2 % 2, u % 2
            K = (tt + 1) * P
            if u:
                pe.wait_ge(*ns_vec.done("lg", u - 1, 1))
            for i in range(2):
                for odd in range(2):
                    h = g * NREP + 2 * i + odd
                    ins = mm_(bank[4 + odd][:, i * K:(i + 1) * K],
                              nqT[odd * ND:(odd + 1) * ND, h // 2, tt * P:(tt + 1) * P],
                              kT[odd * ND:(odd + 1) * ND, br, g, 0:K], start=True, stop=True)
            ins.then_inc(*ns_pe.did("lg", u))

        logits(0)
        for u in range(8):
            tt, g, br = u // 4, u // 2 % 2, u % 2
            if u < 7:
                logits(u + 1)
            pe.wait_ge(*ns_vec.done("p", u))
            for kt in range(tt + 1):
                if u and kt <= (u - 1) // 4:
                    pe.wait_ge(*ns_act.done("aT", u - 1, kt))
                for i in range(NREP):
                    ins = pe.transpose(bank[6 + kt][:, i * P:(i + 1) * P], lg[:, u % 2, i, kt * P:(kt + 1) * P],
                                       ident[:, :])
                ins.then_inc(*ns_pe.did("aT", u, kt))
            if br == 1:
                pe.wait_ge(*ns_act.done("aT", u, tt))
                for odd in range(2):
                    dst = bank[2 + tt][odd * ND:(odd + 1) * ND, g * T:(g + 1) * T]
                    mm_(dst, vc[:, g, :], pcT[:, tt, g * NREP + odd:(g + 1) * NREP:2, :], start=True, stop=False)
                    for b in range(2):
                        for kt in range(tt + 1):
                            ins = mm_(dst, v_sw[:, b, kt, g * ND:(g + 1) * ND], aT[:, b, kt, 2 * odd:2 * odd + 2, :],
                                      start=False, stop=(b == 1 and kt == tt))
                ins.then_inc(*ns_pe.did("av", u // 2))

        pe.wait_ge(*ns_act.done("yT", 1))
        for j in range(4):
            s = SLAB["branch"] + j
            pe.wait_ge(slab_loaded[s % RING], 16 * (s // RING + 1))
            if j >= 2:
                pe.wait_ge(*mix_vec.done("n", j - 2))
            for z in range(2):
                for n in range(2):
                    for k in range(4):
                        ins = mm_(bank[4 + 2 * (j % 2) + z][:, n * T:(n + 1) * T],
                                  ring[:, s % RING, 4 * z + k, n * P:(n + 1) * P], ysT[:, 4 * z + k, :],
                                  start=(k == 0), stop=(k == 3))
            ins.then_inc(slab_used, 1)
        pe.wait_ge(*mix_vec.done("mix", 3))
        slabs(pe, "out", slab_tokens, mixT)

        norm_turn(pe, "ffn")
        pe.wait_ge(*norm_act.done("gain", "ffn", KT - 1))
        units_pe(pe, SLAB["ffn"], FF // SW, 0)

        norm_turn(pe, "mix2")
        pe.wait_ge(*norm_act.done("gain", "mix2", KT - 1))
        norm_turn(pe, "mem")
        pe.wait_ge(*norm_act.done("gain", "mem", KT - 1))
        slabs(pe, "memkv", slab_tokens, memT, 0, 8)
        slabs(pe, "mq", slab_tokens, xT)
        turn(pe, "mk", mk, 8, norm_vec.done("scaled", "mk"))
        pe.wait_ge(*norm_act.done("gain", "mk", 7))
        turn(pe, "mq", mq, 8, norm_vec.done("scaled", "mq"))
        pe.wait_ge(*norm_act.done("gain", "mq", 7))
        evicted(pe, SLAB["memkv"] + 7)
        attend(pe, "mem",
               lambda tt, g: [[(bank[4 + i // 2][:, (i % 2) * T:(i % 2 + 1) * T],
                                [(mqT[:, 2 * i + v, tt * P:(tt + 1) * P], mkT[:, 2 * i + v, :]) for v in range(2)])
                               for i in range(4)]],
               lambda tt, g: [(bank[2 + i // 2][:, (i % 2) * T + v * P:(i % 2) * T + (v + 1) * P],
                               [(mv[:, kt, i * ED + v * P:i * ED + (v + 1) * P], probT[:, kt, i, :])
                                for kt in range(2)]) for i in range(4) for v in range(2)])

        slabs(pe, "gqk", slab_rows, xT)
        slabs(pe, "gvg", slab_tokens, xT, 0, 8)
        pe.wait_ge(loads["narrow"], 16 * 2)
        pe.wait_ge(*b2_act.done("o", "mem", 1, 0))
        for k in range(KT):
            ins = mm_(bank[4][0:GRANK, 0:T], small[:, k, 0:GRANK], xT[:, k, :], start=(k == 0), stop=(k == KT - 1))
        ins.then_inc(*b2_pe.did("a_low"))
        pe.wait_ge(*b2_vec.done("a_low"))
        pe.wait_ge(loads["second"], 16 * 4)
        for t in range(TT):
            mm_(bank[5 + t][:, :], a_low[:, t * P:(t + 1) * P], w_a2[:, :], start=True, stop=True)\
                .then_inc(*b2_pe.did("la", t))
        pe.wait_ge(*b2_vec.done("la"))
        for t in range(TT):
            for h in range(GH):
                ins = mm_(bank[5 + t][:, h * P:(h + 1) * P], la[:, t, h * GK:(h + 1) * GK], tri64[:, :],
                          start=True, stop=True)
            ins.then_inc(*b2_pe.did("cum", t))
        pe.wait_ge(*b2_vec.done("ki"))
        pe.wait_ge(*b2_vec.done("qd"))
        pe.wait_ge(*b2_act.done("cum", 1))
        for t in range(TT):
            for h in range(GH):
                ins = mm_(bank[4 + t][:, h * P:(h + 1) * P], ki[:, h, t * P:(t + 1) * P],
                          gqk[:, h, t * P:(t + 1) * P], start=True, stop=True)
            ins.then_inc(*b2_pe.did("att", t))
        pe.wait_ge(*b2_vec.done("ke"))
        for t in range(TT):
            for h in range(GH):
                ins = pe.transpose(bank[6 + t][:, h * P:(h + 1) * P], gqk[:, GH + h, t * P:(t + 1) * P], ident[:, :])
            ins.then_inc(*b2_pe.did("ke_tok", t))
        pe.wait_ge(*b2_act.done("ke_tok", 1))
        pe.wait_ge(*b2_vec.done("att", 1))
        evicted(pe, SLAB["gvg"] + 7)
        for n in range(3):
            lo = (n % 2) * GCHUNK
            for h in range(GH):
                ins = mm_(bank[2 + 2 * n + h // 2][:, (h % 2) * GV:(h % 2 + 1) * GV],
                          ke_tok[lo:lo + GCHUNK, n // 2, h, :], gv[lo:lo + GCHUNK, n // 2, h * GV:(h + 1) * GV],
                          start=True, stop=True)
            ins.then_inc(*b2_pe.did("state", n))
        pe.wait_ge(*b2_vec.done("state", 2))
        for t in range(TT):
            for h in range(GH):
                dst = bank[4 + 2 * t + h // 2][:, (h % 2) * GV:(h % 2 + 1) * GV]
                mm_(dst, att[:, t, h, :], gv[:, t, h * GV:(h + 1) * GV], start=True, stop=False,
                    skip_group_check=True)
                for c in range(2):
                    n = 2 * t + c
                    if n:
                        mm_(dst[c * GCHUNK:(c + 1) * GCHUNK, :], gqk[:, h, n * GCHUNK:(n + 1) * GCHUNK],
                            state[:, n - 1, h, :], start=False, stop=(c == 1), skip_group_check=True)\
                            .then_inc(*b2_pe.did("o", t, h, c))
        turn(pe, "gla", xn, 8, b2_vec.done("gated"), b2_vec.done("o_raw", 1, 1))
        pe.wait_ge(*norm_act.done("gain", "gla", 7))

        slabs(pe, "dq", slab_tokens, xT)
        slabs(pe, "dkv", slab_tokens, xT, 0, 2)
        slabs(pe, "iq", slab_rows, xT, 0, 2)
        for t in range(TT):
            for k in range(KT):
                ins = mm_(bank[2][:, t * 72:(t + 1) * 72], xT[:, k, t * P:(t + 1) * P], small[:, k, 16:88],
                          start=(k == 0), stop=(k == KT - 1))
        ins.then_inc(*b2_pe.did("ikw"))
        turn(pe, "dq", dq, 8, norm_vec.done("scaled", "dq"))
        pe.wait_ge(*norm_act.done("gain", "dq", 7))
        turn(pe, "dk", dk, 2, norm_vec.done("scaled", "dk"))
        pe.wait_ge(*norm_act.done("gain", "dk", 1))
        turn(pe, "ik", ik2[:, :, :, :].rearrange("p t a d -> p t (a d)"), 1, b2_vec.done("ik2"))
        pe.wait_ge(*norm_act.done("gain", "ik", 0))
        evicted(pe, SLAB["iq"] + 1)
        for t in range(TT):
            K = (t + 1) * P
            if t:
                pe.wait_ge(*b2_act.done("relu", 0))
            for h in range(IH):
                lo, i = (h % 2) * IDIM, h // 2
                ins = mm_(bank[2 + h % 2 + 2 * (i // 2)][:, (i % 2) * T:(i % 2) * T + K],
                          iqT[lo:lo + IDIM, h // 2, t * P:(t + 1) * P], ikT[lo:lo + IDIM, 0:K],
                          start=True, stop=True)
            ins.then_inc(*b2_pe.did("idx", t))
        pe.wait_ge(*b2_act.done("relu", 1))
        attend(pe, "dsa",
               lambda tt, g: [[(bank[4 + i // (4 // (tt + 1))][:, (i % (4 // (tt + 1))) * (tt + 1) * P:
                                                               (i % (4 // (tt + 1)) + 1) * (tt + 1) * P],
                                [(dqT[:, g * DREP + i, tt * P:(tt + 1) * P], dkT[:, g, 0:(tt + 1) * P])])
                               for i in range(4)]],
               lambda tt, g: [(bank[2][:, :], [(dv[:, kt, g * DD:(g + 1) * DD], probT[:, kt, :, :])
                                               for kt in range(tt + 1)])])

        for name, _, _ in BRANCHES:
            src = {"mem": o_mT, "gla": o_gT, "dsa": o_dT}[name]
            for j in range(4):
                slabs(pe, f"gate_{name}{j}", slab_rows, xT, 0, 1)
                slabs(pe, f"o_{name}{j}", slab_rows, src, 0, 1)
        pe.wait_ge(*b2_vec.done("merged", "dsa", 3))
        slabs(pe, "out2", slab_tokens, mergedT)

        norm_turn(pe, "ffn2")
        pe.wait_ge(*norm_act.done("gain", "ffn2", KT - 1))
        pe.wait_ge(loads["router"], 16 * 3)
        R_ = NGRP + NEXP
        for t in range(TT):
            for k in range(KT):
                ins = mm_(bank[2][:, t * R_:(t + 1) * R_], xT[:, k, t * P:(t + 1) * P], small[:, k, 0:R_],
                          start=(k == 0), stop=(k == KT - 1))
        ins.then_inc(*b2_pe.did("router"))
        pe.wait_ge(*b2_vec.done("comb", 1))
        for e in range(NEXP):
            if e >= 8 and e % 2 == 0:
                pe.wait_ge(*b2_act.done("comb", e // 2 - 4))
            for t in range(TT):
                ins = mm_(bank[4 + e // 2 % 4][:, (e % 2) * T + t * P:(e % 2) * T + (t + 1) * P],
                          spread(comb[:, t, e:e + 1], (0, P)), ident[:, :], start=True, stop=True)
            if e % 2:
                ins.then_inc(*b2_pe.did("comb", e // 2))
        pe.wait_ge(*b2_act.done("comb", 7))
        units_pe(pe, SLAB["moe"], NEXP, FF // SW)


def kernel(**inputs):
    import concourse.bacc as bacc
    from concourse.bass_utils import run_bass_kernel_spmd

    arrays = {name: np.ascontiguousarray(a) for name, a in inputs.items()}
    arrays.update(constants())
    plan = {}
    for _ in range(2):
        nc = bacc.Bacc("TRN2", target_bir_lowering=False, num_devices=1)
        dram = {name: nc.dram_tensor("in_" + name, a.shape, mybir.dt.from_np(a.dtype), kind="ExternalInput").ap()
                for name, a in arrays.items()}
        dram["rev"] = nc.dram_tensor("rev_rows", [NH, REV], F32, kind="Internal").ap()
        dram["rev_copies"] = nc.dram_tensor("rev_copies", [NH, P, REV], F32, kind="Internal").ap()
        out = nc.dram_tensor("out_0", [1, T, D], F32, kind="ExternalOutput").ap()
        program(nc, dram, out, plan)
    r = run_bass_kernel_spmd(nc, [{"in_" + name: a for name, a in arrays.items()}], core_ids=[0])
    return r.results[0]["out_0"]
```

```python
from contextlib import ExitStack
import math

import numpy as np

import concourse.bass as bass
from concourse import mybir

F32 = mybir.dt.float32
F32R = mybir.dt.float32r
ALU = mybir.AluOpType
ACT = mybir.ActivationFunctionType
AX = mybir.AxisListType

P = 128
T = 256
TT = T // P
D = 1024
KT = D // P
EPS = 1e-6
NEG = -1e30
SW = 256
RING = 3

MH, MD = 4, 128
NH, NG, ND = 8, 2, 64
NREP = NH // NG
CMP_BLOCK, CMP_STRIDE = 32, 16
NCMP = (T - CMP_BLOCK) // CMP_STRIDE + 1
CMP_PAIRS = CMP_BLOCK // 2
BUCKETS, MAX_DIST = 32, 1024
FF = -(-8 * D // (3 * 256)) * 256
M_W, N_W, N_KV = MH * MD, NH * ND, NG * ND
C_MQ = 0
C_MV = 2 * M_W
C_MI = 4 * M_W
C_NQ = C_MI + 2 * MH
C_KV = C_NQ + N_W
C_NGATE = C_KV + 6 * N_KV
C_MERGE = C_NGATE + 3 * NH

GH, GK, GV, GRANK, GCHUNK = 4, 128, 256, 16, 64
GTEMP = 16.0
DH, DG, DD = 8, 2, 128
DREP = DH // DG
IH, IDIM = 8, 64
TOPK = min(256, T // 4)
EH, ED = 4, 256
MEM = 256
NGRP, PERG = 4, 4
NEXP = NGRP * PERG
DEXP = D // 4
B_GQ = 0
B_GV = 2 * GH * GK
B_GA = B_GV + 2 * GH * GV
B_DQ = B_GA + GRANK
B_DKV = B_DQ + DH * DD
B_IQ = B_DKV + 2 * DG * DD
B_IK = B_IQ + IH * IDIM
B_MQ = B_IK + IDIM + IH
B_GATE = B_MQ + EH * ED
MARK = -3e38


def bucket(dist):
    n = np.maximum(dist, 0)
    half = BUCKETS // 2
    nf = np.maximum(n, 1).astype(np.float32)
    large = half + (np.log(nf / np.float32(half)) / np.float32(math.log(MAX_DIST / half))
                    * np.float32(BUCKETS - half)).astype(np.int32)
    return np.where(n < half, n, np.minimum(large, BUCKETS - 1))


def one_hot(dist):
    rows = np.where(dist < 0, BUCKETS, bucket(dist))
    return (np.arange(BUCKETS + 1)[:, None] == rows[None, :]).astype(np.float32)


REV = T + P
OH_CMP0 = T - 1


def constants():
    i = np.arange(P)
    f = np.float32
    le = (i[:, None] <= i[None, :]).astype(f)
    same = (i[:, None] // GCHUNK == i[None, :] // GCHUNK).astype(f)
    after = (i[None, :] > i[:, None]).astype(f)
    t = np.arange(T)
    ends = np.arange(NCMP) * CMP_STRIDE + CMP_BLOCK - 1
    seen = (ends[None, :] <= t[:, None]).astype(f)
    return {
        "c_ident": np.eye(P, dtype=f),
        "c_tri": le,
        "c_tri64": le * same,
        "c_mask_after": after * f(NEG),
        "c_mask_before": after.T * f(-NEG),
        "c_causal": np.concatenate([np.zeros((P, P), f), after * f(NEG)], axis=1),
        "c_seen": seen.reshape(TT, P, NCMP).transpose(1, 0, 2).copy(),
        "c_oh_rev": one_hot(T - 1 - np.arange(REV)),
        "c_oh_cmp": one_hot(np.arange(2 * T) - OH_CMP0),
        "c_neg": np.full((1, NH), NEG, f),
        "c_iota4": np.broadcast_to(np.arange(4, dtype=f), (P, 4)).copy(),
    }


class Count:

    def __init__(self, sem, plan):
        self.sem, self.plan, self.n = sem, plan, 0

    def did(self, *step):
        self.n += 1
        self.plan[step] = self.n
        return self.sem, 1

    def done(self, *step):
        return self.sem, self.plan.get(step, 1)


def program(nc, dram, out, plan):
    ctx = ExitStack()
    first_ctx, second_ctx = ExitStack(), ExitStack()

    def sb(name, shape, dtype=F32, into=None):
        return (into or ctx).enter_context(nc.sbuf_tensor(name, shape, dtype))

    def sem(name):
        return ctx.enter_context(nc.semaphore(name))

    def count(name):
        return Count(sem(name), plan.setdefault(name, {}))

    def spread(ap, *dims):
        return bass.AP(tensor=ap.tensor, offset=ap.offset, ap=[list(ap.ap[0])] + [list(d) for d in dims])

    def along(ap, n):
        return spread(ap, (ap.ap[-1][0], ap.shape[-1]), (0, n))

    ident = sb("ident", [P, P])
    tri = sb("tri", [P, P])
    tri64 = sb("tri64", [P, P])
    mask_after = sb("mask_after", [P, P])
    mask_before = sb("mask_before", [P, P])
    causal = sb("causal", [P, T])
    ones = sb("ones", [P, P])
    minus_half = sb("minus_half", [P, 32])
    rows = sb("rows", [P, 2, P])
    cols = sb("cols", [P, 2, P])
    x = sb("x", [P, TT, D])
    xn = sb("xn", [P, TT, D])
    xT = sb("xT", [P, KT, T])
    ss = sb("ss", [P, 2 * TT])
    ring = sb("ring", [P, RING, KT, SW])
    g_fin = sb("g_fin", [P, D])
    hT = sb("hT", [P, 2, T])
    gated = sb("gated", [P, 2, T])
    small = sb("small", [P, KT, 96])
    bank = [ctx.enter_context(nc.psum_tensor(f"bank{b}", [P, 512], F32)) for b in range(8)]

    VECTORS = [
        [("b_qk", 8), ("b_nq", 4), ("b_merge", 16), ("b_kv", 4), ("g_mix", 8), ("conv", 32),
         ("g_head", 4), ("g_ffn", 8), ("pe", 32)],
        [("g_mix2", 8), ("g_mem", 8), ("g_dq", 1), ("g_dk", 1), ("g_ik", 1), ("g_mq", 2), ("g_mk", 2),
         ("g_gla", 2), ("b_gate", 24), ("g_ffn2", 8)],
    ]
    ROW = {}
    for tile, vectors in enumerate(VECTORS):
        at = 0
        for name, n in vectors:
            ROW[name] = (tile, at)
            at += n
    NROWS = [sum(n for _, n in v) for v in VECTORS]

    def col(name, i=0):
        tile, at = ROW[name]
        return cols[:, tile, at + i:at + i + 1]

    def one(name, shape, dtype=F32):
        return sb(name, shape, dtype, into=first_ctx)

    oh_rev = one("oh_rev", [BUCKETS + 1, REV])
    oh_cmp = one("oh_cmp", [BUCKETS + 1, 2 * T])
    rel = one("rel", [BUCKETS + 1, NH])
    rev = one("rev", [NH, REV])
    strip = one("strip", [P, NH, T])
    cmp_bias = one("cmp_bias", [P, TT, NCMP, NH])
    seen = one("seen", [P, TT, NCMP])
    w_cmp1 = one("w_cmp1_sb", [P, 2, CMP_PAIRS, P])
    w_cmp2k = one("w_cmp2k", [P, 2, ND])
    w_cmp2v = one("w_cmp2v", [P, ND])
    b_vo = one("b_vo", [P, 2 * M_W])
    b_small = one("b_small", [P, 8 + 3 * NH])
    b_vs = one("b_vs", [P, 2, N_KV])
    b_fg = one("b_fg", [P, MH])
    qk_pre = one("qk_pre", [P, 8, 3 + T])
    qk = one("qk", [P, 8, T])
    sig = one("sig", [P, 8, T])
    v1 = one("v1", [P, TT, MH, MD + 1])
    sig_o = one("sig_o", [P, TT, M_W])
    gate_in = one("gate_in", [P, TT, 8 + 3 * NH])
    nsa_gate = one("nsa_gate", [P, TT, 3 * NH])
    nqT = one("nqT", [P, 4, T])
    cmp_in = one("cmp_in", [P, 2, NG, T + 1])
    kT = one("kT", [P, 2, NG, T])
    v_sw = one("v_sw", [P, 2, TT, N_KV])
    mergeT = one("mergeT", [P, 16, T])
    ysT = one("ysT", [P, 8, T])
    mixT = sig
    mix2 = one("mix2", [P, 2, 512])
    fz = one("fz", [P, TT, MH])
    fa = one("fa", [P, TT, MH])
    fe = one("fe", [P, TT, MH])
    lf = one("lf", [P, TT, MH])
    bc = one("bc", [P, 2, TT, MH])
    cc = one("cc", [P, TT, MH])
    cm = one("cm", [P, TT, MH])
    cx = one("cx", [P, MH])
    m1 = one("m1", [P, MH])
    mm = one("mm", [P, TT, MH])
    w_st = one("w_st", [P, 3, MH])
    em = one("em", [P, TT, MH])
    yy = one("yy", [P, TT, MH, P])
    pT = one("pT", [P, TT, MH, P])
    k_tok = one("k_tok", [P, MH, MD])
    wv = one("wv", [P, MH, MD + 1])
    c1 = one("c1", [P, MH, MD + 1])
    hh = one("hh", [P, TT, MH, MD + 1])
    den = one("den", [P, TT, MH])
    hn = one("hn", [P, TT, MH, MD])
    hsq = yy
    blk = one("blk", [P, 2, CMP_PAIRS, NG, NCMP])
    hid = one("hid", [P, 2, NG * NCMP])
    hid_s = one("hid_s", [P, 2, NG * NCMP])
    kcT = one("kcT", [P, NG * NCMP])
    vc = one("vc", [NCMP, NG, ND])
    lc = one("lc", [P, TT, NH, NCMP])
    ec = one("ec", [P, TT, NH, NCMP])
    mc = one("mc", [P, TT, NH])
    sc = one("sc", [P, TT, NH])
    pcT = qk_pre[0:NCMP, :, :].rearrange("p a b -> p (a b)")[:, 0:TT * NH * P]\
        .rearrange("p (t h q) -> p t h q", t=TT, h=NH)
    lg = xn[:, :, :].rearrange("p t (h k) -> p t h k", h=NREP)
    mx = one("mx", [P, 2, NREP])
    sm = one("sm", [P, 2, NREP])
    aT = qk[:, :, :].rearrange("p (b t h) (i q) -> p b t (h i) q", b=2, t=TT, i=2)
    first_ctx.close()

    def two(name, shape, dtype=F32):
        return sb(name, shape, dtype, into=second_ctx)

    over_ctx = ExitStack()
    memT_hi, memT_lo = (sb("memT_" + n, [P, KT, T], F32R, into=over_ctx) for n in ("hi", "lo"))
    over_ctx.close()
    gla_end = two("gla_end", [P, 2 * T * GH + 3 * GH * GV])
    gv = two("gv", [P, TT, GH * GV])
    b_r = two("b_r", [P, NGRP + NEXP])
    iota4 = two("iota4", [P, 4])
    gqk = two("gqk", [P, 8, T])
    mk = two("mk", [P, TT, EH * ED])
    mv = two("mv", [P, TT, EH * ED])
    h_ctx = ExitStack()
    h_hi, h_lo = (sb("h_" + n, [P, 2, T], F32R, into=h_ctx) for n in ("hi", "lo"))
    h_ctx.close()
    mq = two("mq", [P, TT, EH * ED])
    mkT = two("mkT", [P, 8, T])
    mqT = two("mqT", [P, 8, T])
    scaled = two("scaled", [P, 3])
    s16 = two("s16", [P, TT, 8])

    rl = two("rl", [P, TT, NGRP + NEXP])
    r_tmp = two("r_tmp", [P, TT, NEXP])
    r_key = two("r_key", [P, TT, 4])
    r_one = two("r_one", [P, 3, TT, 4])
    r_el = two("r_el", [P, TT, 4])
    r_s = two("r_s", [P, 8, TT])
    comb = two("comb", [P, TT, NEXP])
    sq = gv
    parts_ctx = ExitStack()
    w_hi, w_lo = (sb("w_" + n, [P, RING, KT, SW], F32R, into=parts_ctx) for n in ("hi", "lo"))
    xT_hi, xT_lo = (sb("xT_" + n, [P, KT, T], F32R, into=parts_ctx) for n in ("hi", "lo"))
    parts_ctx.close()
    w_a2 = two("w_a2", [GRANK, GH * GK])
    b_a2 = two("b_a2", [P, GH * GK])

    mem = gv
    memT = gqk
    o_gT = gqk
    gg = two("gg", [P, TT, GH * GV])
    o_mT = mq[:, :, :].rearrange("p t (k q) -> p (t k) q", q=T)
    mergedT = mkT
    a_low = two("a_low", [GRANK, T])
    la = two("la", [P, TT, GH * GK])
    lz = two("lz", [P, TT, GH * GK])
    cum = two("cum", [P, GH, T])
    ex = two("ex", [P, GH, T])
    ki = two("ki", [P, GH, T])
    decay = two("decay", [P, GH, T // GCHUNK])
    ke_tok, att = (gla_end[:, n * T * GH:(n + 1) * T * GH].rearrange("p (t h q) -> p t h q", t=TT, h=GH)
                   for n in range(2))
    state = gla_end[:, 2 * T * GH:].rearrange("p (n h v) -> p n h v", n=3, h=GH)
    dq = mk
    o_dT = dq[:, :, :].rearrange("p t (k q) -> p (t k) q", q=T)
    dqT = mqT
    dk = two("dk", [P, TT, DG * DD])
    dv = two("dv", [P, TT, DG * DD])
    dkT = two("dkT", [P, DG, T])
    iqT = two("iqT", [P, 4, T])
    ikw = two("ikw", [P, TT, IDIM + IH])
    ik2 = two("ik2", [P, TT, 2, IDIM])
    ikT = two("ikT", [P, T])
    relu = two("relu", [P, IH, T])
    score = two("score", [P, TT, T])
    best = two("best", [P, TT, 8])
    pick = two("pick", [P, TT, T])
    smx = two("smx", [P, 2, 4])
    ssm = two("ssm", [P, 2, 4])
    probT = two("probT", [P, TT, 4, P])
    comb_all = gla_end[:, 0:NEXP * T].rearrange("p (e t) -> p e t", e=NEXP)
    second_ctx.close()
    loads = {n: sem("load_" + n) for n in ("x", "const", "rows", "rows2", "broadcast", "rel", "small", "cmp", "rev", "copies", "strip", "twice", "mem", "second",
                                          "narrow", "router", "g_fin")}
    slab_loaded = [sem(f"slab_loaded{r}") for r in range(RING)]
    slab_used = sem("slab_used")
    bank_read = [sem("bank0_read"), sem("bank1_read")]
    stored = sem("stored")
    setup_pe, setup_vec, setup_act, setup_pool = (count("setup_" + e) for e in ("pe", "vec", "act", "pool"))
    norm_pe, norm_vec, norm_act, norm_pool = (count("norm_" + e) for e in ("pe", "vec", "act", "pool"))
    in1_pe, in1_vec, in1_act = (count("in1_" + e) for e in ("pe", "vec", "act"))
    ml_pe, ml_vec, ml_act, ml_pool = (count("mlstm_" + e) for e in ("pe", "vec", "act", "pool"))
    ns_pe, ns_vec, ns_act = (count("nsa_" + e) for e in ("pe", "vec", "act"))
    mix_vec = count("mix_vec")
    ff_seed = sem("ff_seed")
    ff_up = sem("ff_up")
    ff_silu = sem("ff_silu")
    ff_product = sem("ff_product")
    ff_h_hi = sem("ff_h_hi")
    ff_hidden = sem("ff_hidden")
    w_hi_ready = sem("w_hi_ready")
    w_lo_ready = sem("w_lo_ready")
    xT_hi_ready = sem("xT_hi_ready")
    xT_lo_ready = sem("xT_lo_ready")
    ff_shared = sem("ff_shared")
    b2_pe, b2_vec, b2_act, b2_pool = (count("second_" + e) for e in ("pe", "vec", "act", "pool"))

    STREAM = [("qk", "w_in", C_MQ, 4), ("vo", "w_in", C_MV, 4), ("nq", "w_in", C_NQ, 2),
              ("kv", "w_in", C_KV, 3), ("merge", "w_in", C_MERGE, 8),
              ("branch", "w_branch", 0, 4), ("out", "w_out", 0, 4),
              ("ffn", None, 0, 3 * (FF // SW)),
              ("memkv", "w_mem_kv_2", 0, 8), ("mq", "w_in_2", B_MQ, 4), ("gqk", "w_in_2", B_GQ, 4),
              ("gvg", "w_in_2", B_GV, 8), ("dq", "w_in_2", B_DQ, 4), ("dkv", "w_in_2", B_DKV, 2),
              ("iq", "w_in_2", B_IQ, 2)]
    BRANCHES = [("mem", 2, "w_o_mem_2"), ("gla", 0, "w_o_gla_2"), ("dsa", 1, "w_o_dsa_2")]
    for name, z, w_o in BRANCHES:
        for j in range(4):
            STREAM += [(f"gate_{name}{j}", "w_in_2", B_GATE + z * D + j * SW, 1), (f"o_{name}{j}", w_o, j * SW, 1)]
    STREAM += [("out2", "w_out_2", 0, 4), ("moe", None, 0, 3 * NEXP)]
    SLAB, at = {}, 0
    for name, _, _, n in STREAM:
        SLAB[name] = at
        at += n

    EXTRA = SLAB["gvg"] - SLAB["memkv"]
    SPLIT = [(SLAB["ffn"], 0, 3 * (FF // SW) + EXTRA), (SLAB["moe"], 3 * (FF // SW) + EXTRA, 3 * NEXP)]

    def split_before(base):
        return SPLIT[1][1] if base else 0

    def weights(name, c, n):
        m = dram[name]
        m = m[0] if name != "w_branch" else m.rearrange("z n w d -> (z n w) d")
        return m.rearrange("(k p) n -> p k n", p=P)[:, :, c:c + n] if isinstance(c, int) else \
            m.rearrange("(k p) n -> p k n", p=P)[:, :, bass.ds(c, n)]

    BANKED = {}
    for name, _, _, n in STREAM:
        for j in range(n):
            if name not in ("branch", "ffn", "moe"):
                BANKED[SLAB[name] + j] = len(BANKED)

    def half(s, n):
        return bank[BANKED[s] % 2][:, n * T:(n + 1) * T]

    def half_read(s):
        return bank_read[BANKED[s] % 2], 1

    def other_half(eng, s):
        eng.wait_ge(bank_read[BANKED[s] % 2], 2 * (BANKED[s] // 2) + 1)

    def all_out(s):
        return [(bank_read[b], 2 * ((BANKED[s] + 2 - b) // 2)) for b in range(2)]

    def evicted(eng, s):
        for w in all_out(s):
            eng.wait_ge(*w)

    def slab_out(eng, name, j):
        eng.wait_ge(slab_used, SLAB[name] + j + 1)

    def slab_in(pe, s):
        pe.wait_ge(slab_loaded[s % RING], 16 * (s // RING + 1))
        if s in BANKED and BANKED[s] >= 2:
            pe.wait_ge(bank_read[BANKED[s] % 2], 2 * (BANKED[s] // 2))

    def slab_rows(pe, s, operand):
        for n in range(2):
            for k in range(KT):
                ins = pe.matmul(half(s, n), ring[:, s % RING, k, n * P:(n + 1) * P], operand[:, k, :],
                                start=(k == 0), stop=(k == KT - 1))
        return ins

    def slab_tokens(pe, s, operand):
        for t in range(TT):
            for k in range(KT):
                ins = pe.matmul(half(s, t), operand[:, k, t * P:(t + 1) * P], ring[:, s % RING, k, :],
                                start=(k == 0), stop=(k == KT - 1))
        return ins

    def slabs(pe, name, product, operand, start=0, end=4):
        for j in range(start, end):
            slab_in(pe, SLAB[name] + j)
            product(pe, SLAB[name] + j, operand).then_inc(slab_used, 1)

    def split_slabs(pe, name, tokens, hi, lo, start, end):
        for j in range(start, end):
            sl = SLAB[name] + j
            pe.wait_ge(w_lo_ready, sl - SPLIT[0][0] + 1)
            pe.wait_ge(bank_read[BANKED[sl] % 2], 2 * (BANKED[sl] // 2))
            for n in range(2):
                for k in range(KT):
                    if name == "memkv" and j == 0 and n == 0:
                        x_parts_wait(pe, "mem", k)
                    r, c = sl % RING, slice(n * P, (n + 1) * P)
                    x_ = [v[:, k, c if tokens else slice(0, T)] for v in (hi, lo)]
                    w_ = [v[:, r, k, slice(0, SW) if tokens else c] for v in (w_hi, w_lo)]
                    (ah, al), (bh, bl) = (x_, w_) if tokens else (w_, x_)
                    for m, (a, b) in enumerate(((ah, bh), (ah, bl), (al, bh))):
                        ins = pe.matmul(half(sl, n), a, b, start=(k == 0 and m == 0), stop=(k == KT - 1 and m == 2))
            ins.then_inc(slab_used, 1)

    def norm_square(act, name, src, *ready):
        for w in ready:
            act.wait_ge(*w)
        for t in range(TT):
            act.activation(xn[:, t, :], src[:, t, :], ACT.Square, accum_out=ss[:, t:t + 1])\
               .then_inc(*norm_act.did("square", name, t))

    def norm_scale(vec, name, src, dst=None):
        vec.wait_ge(*norm_act.done("square", name, TT - 1))
        vec.tensor_scalar(ss[:, 2:4], ss[:, 0:2], 1.0 / D, EPS, ALU.mult, ALU.add)\
           .then_inc(*norm_vec.did("mean", name))
        vec.wait_ge(*norm_pool.done("root", name))
        for t in range(TT):
            vec.tensor_scalar((xn if dst is None else dst)[:, t, :], src[:, t, :], ss[:, 2 + t:3 + t], None, ALU.mult)\
               .then_inc(*norm_vec.did("scale", name, t))

    def norm_root(pool, name):
        pool.wait_ge(*norm_vec.done("mean", name))
        pool.tensor_tensor(ss[:, 2:4], ss[:, 2:4], minus_half[:, 0:2], ALU.pow).then_inc(*norm_pool.did("root", name))

    def turn(pe, name, src, n, *ready):
        for w in ready:
            pe.wait_ge(*w)
        for k in range(n):
            for t in range(TT):
                at = (k % 2) * T + t * P
                ins = pe.transpose(bank[4 + k // 2][:, at:at + P], src[:, t, k * P:(k + 1) * P], ident[:, :])
            ins.then_inc(*norm_pe.did("turn", name, k))

    def turned(act, name, n, dst, gain):
        for k in range(n):
            act.wait_ge(*norm_pe.done("turn", name, k | 1 if k | 1 < n else k))
            act.activation(dst[:, k, :], bank[4 + k // 2][:, (k % 2) * T:(k % 2 + 1) * T], ACT.Copy,
                           scale=gain(k)).then_inc(*norm_act.did("gain", name, k))

    def attend(pe, name, logits, values, meanwhile):
        units = [(tt, g) for tt in range(TT) for g in range(1 if name == "mem" else DG)]

        def put_logits(n):
            tt, g = units[n]
            if n:
                pe.wait_ge(*b2_vec.done("lg", name, *units[n - 1]))
            for group in logits(tt, g):
                for dst, parts in group:
                    for i, (a, b) in enumerate(parts):
                        ins = pe.matmul(dst, a, b, start=(i == 0), stop=(i == len(parts) - 1))
            ins.then_inc(*b2_pe.did("lg", name, tt, g))

        put_logits(0)
        for n, (tt, g) in enumerate(units):
            if n + 1 < len(units):
                put_logits(n + 1)
            meanwhile(n)
            pe.wait_ge(*b2_vec.done("p", name, tt, g))
            if n:
                pe.wait_ge(*b2_act.done("probT", name, *units[n - 1], 0 if units[n - 1][0] == 0 and name != "mem" else 1))
            tiles = 2 if name == "mem" else tt + 1
            for kt in range(tiles):
                for i in range(4):
                    ins = pe.transpose(bank[6 + kt][:, i * P:(i + 1) * P], lg[:, n % 2, i, kt * P:(kt + 1) * P],
                                       ident[:, :])
                ins.then_inc(*b2_pe.did("probT", name, tt, g, kt))
            pe.wait_ge(*b2_act.done("probT", name, tt, g, tiles - 1))
            if n:
                pe.wait_ge(*b2_act.done("o", name, *units[n - 1]))
            for dst, parts in values(tt, g):
                for i, (a, b) in enumerate(parts):
                    ins = pe.matmul(dst, a, b, start=(i == 0), stop=(i == len(parts) - 1))
            ins.then_inc(*b2_pe.did("o", name, tt, g))

    def attend_vec(vec, name, masked, meanwhile):
        units = [(tt, g) for tt in range(TT) for g in range(1 if name == "mem" else DG)]
        for n, (tt, g) in enumerate(units):
            K = T if name == "mem" else (tt + 1) * P
            hs = 512 // K
            l = lg[:, n % 2, :, 0:K]
            if n >= 2:
                vec.wait_ge(*b2_pe.done("probT", name, *units[n - 2], units[n - 2][0] if name != "mem" else 1))
            vec.wait_ge(*b2_pe.done("lg", name, tt, g))
            for b in range(4 // hs):
                src = bank[4 + b][:, :].rearrange("p (h k) -> p h k", h=hs)
                dst = lg[:, n % 2, b * hs:(b + 1) * hs, 0:K]
                step = b2_vec.did("lg", name, tt, g) if b == 4 // hs - 1 else b2_vec.did("lg_", name, tt, g, b)
                if masked:
                    vec.tensor_tensor(dst, src, spread(pick[:, tt, 0:K], (0, hs), (1, K)), ALU.add).then_inc(*step)
                else:
                    vec.tensor_copy(dst, src).then_inc(*step)
            vec.wait_ge(*b2_vec.done("lg", name, tt, g))
            vec.tensor_reduce(smx[:, n % 2, :], l, AX.X, ALU.max).then_inc(*b2_vec.did("mx", name, tt, g))
            vec.wait_ge(*b2_vec.done("mx", name, tt, g))
            vec.tensor_tensor(l, l, along(smx[:, n % 2, :], K), ALU.subtract).then_inc(*b2_vec.did("shift", name, tt, g))
            vec.wait_ge(*b2_act.done("exp", name, tt, g))
            vec.tensor_reduce(ssm[:, n % 2, :], l, AX.X, ALU.add).then_inc(*b2_vec.did("sum", name, tt, g))
            vec.wait_ge(*b2_vec.done("sum", name, tt, g))
            vec.reciprocal(ssm[:, n % 2, :], ssm[:, n % 2, :]).then_inc(*b2_vec.did("rs", name, tt, g))
            vec.wait_ge(*b2_vec.done("rs", name, tt, g))
            vec.tensor_tensor(l, l, along(ssm[:, n % 2, :], K), ALU.mult).then_inc(*b2_vec.did("p", name, tt, g))
            meanwhile(n)

    def attend_act(act, name, store, meanwhile):
        units = [(tt, g) for tt in range(TT) for g in range(1 if name == "mem" else DG)]
        for n, (tt, g) in enumerate(units):
            K = T if name == "mem" else (tt + 1) * P
            act.wait_ge(*b2_vec.done("shift", name, tt, g))
            act.activation(lg[:, n % 2, :, 0:K], lg[:, n % 2, :, 0:K], ACT.Exp).then_inc(*b2_act.did("exp", name, tt, g))
            meanwhile(n)
            for kt in range(K // P):
                act.wait_ge(*b2_pe.done("probT", name, tt, g, kt))
                act.activation(probT[:, kt, :, :], bank[6 + kt][:, :].rearrange("p (h q) -> p h q", h=4), ACT.Copy)\
                   .then_inc(*b2_act.did("probT", name, tt, g, kt))
            act.wait_ge(*b2_pe.done("o", name, tt, g))
            store(tt, g)

    def norm_turn(pe, name, *ready):
        turn(pe, name, xn, KT, norm_vec.done("scale", name, TT - 1), *ready)

    def norm_gain(act, name, gain, dst):
        act.wait_ge(*setup_vec.done("cols", ROW[gain][0]))
        turned(act, name, KT, dst, lambda k: col(gain, k))

    def head_norm(vec, name, src, heads, size):
        flat = src.rearrange("p t n -> p (t n)")
        s2 = sq[:, :, :].rearrange("p a b -> p (a b)")[:, 0:TT * heads * size]
        vec.tensor_tensor(s2, flat, flat, ALU.mult).then_inc(*norm_vec.did("square", name))
        vec.wait_ge(*norm_vec.done("square", name))
        sums = s16[:, :, :].rearrange("p t h -> p (t h)")[:, 0:TT * heads]
        vec.tensor_reduce(sums, s2.rearrange("p (n d) -> p n d", d=size), AX.X, ALU.add)\
           .then_inc(*norm_vec.did("sum", name))
        vec.wait_ge(*norm_vec.done("sum", name))
        vec.tensor_scalar(sums, sums, 1.0 / size, EPS, ALU.mult, ALU.add).then_inc(*norm_vec.did("mean", name))
        vec.wait_ge(*norm_pool.done("root", name))
        grouped = flat.rearrange("p (n d) -> p n d", d=size)
        vec.tensor_tensor(grouped, grouped, along(sums, size), ALU.mult).then_inc(*norm_vec.did("scaled", name))

    def head_root(pool, name, heads):
        sums = s16[:, :, :].rearrange("p t h -> p (t h)")[:, 0:TT * heads]
        pool.wait_ge(*norm_vec.done("mean", name))
        pool.tensor_tensor(sums, sums, minus_half[:, 0:TT * heads], ALU.pow).then_inc(*norm_pool.did("root", name))

    def units_load(sp, first, n, base, gate, up, down):
        def put(q, turn_, src, i=0):
            s = first + q
            if q < RING:
                sp.wait_ge(slab_used, s - RING + 1)
            else:
                sp.wait_ge(w_lo_ready, split_before(base) + q - RING + 1 + 3 * i)
            dst = ring[:, s % RING, :, :]
            if turn_:
                dst = dst.rearrange("p (n a) c -> p n (a c)", n=2)
            sp.dma_start(dst, src).then_inc(slab_loaded[s % RING], 16)

        for q, src in enumerate((gate(0), up(0), gate(1))):
            put(q, False, src)
        with sp.Fori(0, n - 2) as i:
            put(3, False, up(i + 1), i)
            put(4, True, down(i), i)
            put(5, False, gate(i + 2), i)
        put(3 * n - 3, False, up(n - 1))
        put(3 * n - 2, True, down(n - 2))
        put(3 * n - 1, True, down(n - 1))

    def units_pe(pe, first, n, base, shares=None):
        def split_(q, i=0):
            pe.wait_ge(w_lo_ready, split_before(base) + q + 1 + 3 * i)
            return (first + q) % RING

        def product(dst, pairs, start, stop, **kw):
            for j, ((ah, al), (bh, bl)) in enumerate(pairs):
                for m, (a, b) in enumerate(((ah, bh), (ah, bl), (al, bh))):
                    ins = pe.matmul(dst, a, b, start=(start and j + m == 0),
                                    stop=(stop and j == len(pairs) - 1 and m == 2), **kw)
            return ins

        def rows_(q, b, sem_, least, i=0, x_parts=False):
            r = split_(q, i)
            if least is not None:
                pe.wait_ge(sem_, least)
            for m in range(2):
                for k in range(KT):
                    if x_parts and m == 0:
                        x_parts_wait(pe, "ffn2" if base else "ffn", k)
                    ins = product(bank[b + m][:, 0:T], [([w[:, r, k, m * P:(m + 1) * P] for w in (w_hi, w_lo)],
                                                         [v[:, k, :] for v in (xT_hi, xT_lo)])],
                                  k == 0, k == KT - 1)
            ins.then_inc(slab_used, 1)

        def down(q, hidden, i=0, last=False):
            r = split_(q, i)
            pe.wait_ge(ff_hidden, hidden)
            wh, wl = (w[:, r, :, :].rearrange("p (n a) c -> p n (a c)", n=2) for w in (w_hi, w_lo))
            for b in range(4):
                t, c = b // 2, (b % 2) * 512
                ins = product(bank[b][:, :],
                              [([h[:, m, t * P:(t + 1) * P] for h in (h_hi, h_lo)],
                                [w[:, m, c:c + 512] for w in (wh, wl)]) for m in range(2)], False, last,
                              skip_group_check=True)
            ins.then_inc(slab_used, 1)

        def seed(start, end):
            for b in range(start, end):
                pe.matmul(bank[b][:, :], ident[:, :], x[:, b // 2, (b % 2) * 512:(b % 2 + 1) * 512],
                          start=True, stop=False, skip_group_check=True)

        seed(0, 4 if shares is None else 2)
        rows_(0, 4, ff_silu, 2 * base if base else None, x_parts=True)
        rows_(1, 6, ff_product, 2 * base if base else None)
        if shares is not None:
            shares()
            seed(2, 4)
        with pe.Fori(0, n - 1) as i:
            rows_(2, 4, ff_silu, 2 * (base + 1) + 2 * i, i)
            rows_(3, 6, ff_product, 2 * (base + 1) + 2 * i, i)
            down(4, base + 1 + i, i)
        down(3 * n - 1, base + n, last=True)

    PARTED = {name: KT * n for n, name in enumerate(("ffn", "mem", "mix2", "ffn2"))}

    def x_parts_wait(pe, name, k=KT - 1):
        pe.wait_ge(xT_lo_ready, PARTED[name] + k + 1)

    def x_parts(vec, name, src, hi, lo):
        for k in range(KT):
            vec.wait_ge(*norm_act.done("gain", name, k))
            vec.tensor_copy(hi[:, k, :], src[:, k, :]).then_inc(xT_hi_ready, 1)
            vec.wait_ge(xT_hi_ready, PARTED[name] + k + 1)
            vec.tensor_tensor(lo[:, k, :], src[:, k, :], hi[:, k, :].bitcast(F32), ALU.subtract)\
               .then_inc(xT_lo_ready, 1)

    def unit_hi(act, first, base, q, i=0):
        s = first + q
        act.wait_ge(slab_loaded[s % RING], 16 * (s // RING + 1) + 16 * i)
        if q >= RING:
            act.wait_ge(slab_used, s - RING + 1 + 3 * i)
        act.activation(w_hi[:, s % RING, :, :], ring[:, s % RING, :, :], ACT.Copy).then_inc(w_hi_ready, 1)

    def unit_lo(vec, first, base, q, i=0):
        s = first + q
        vec.wait_ge(w_hi_ready, split_before(base) + q + 1 + 3 * i)
        if q >= RING:
            vec.wait_ge(slab_used, s - RING + 1 + 3 * i)
        vec.tensor_tensor(w_lo[:, s % RING, :, :], ring[:, s % RING, :, :], w_hi[:, s % RING, :, :].bitcast(F32),
                          ALU.subtract).then_inc(w_lo_ready, 1)

    def units_act(act, first, n, base, shares=None):
        def silu(gate_done, before):
            act.wait_ge(slab_used, gate_done)
            if before is not None:
                act.wait_ge(ff_hidden, before)
            for m in range(2):
                act.activation(gated[:, m, :], bank[4 + m][:, 0:T], ACT.Silu).then_inc(ff_silu, 1)

        silu(first + 1, base if base else None)
        if shares is not None:
            shares()
        with act.Fori(0, n - 1) as i:
            unit_hi(act, first, base, 3, i)
            unit_hi(act, first, base, 4, i)
            silu(first + 3 + 3 * i, base + 1 + i)
            unit_hi(act, first, base, 5, i)

    def units_vec(vec, first, n, base, share):
        def product(e):
            vec.wait_ge(ff_silu, 2 * base + 2 + 2 * e)
            if share is not None:
                for m in range(2):
                    vec.tensor_tensor(gated[:, m, :], gated[:, m, :], share[:, bass.ds(e * T, T)], ALU.mult)\
                       .then_inc(ff_shared, 1)
            vec.wait_ge(slab_used, first + 2 if isinstance(e, int) and e == 0 else first + 1 + 3 * e)
            for m in range(2):
                if share is not None:
                    vec.wait_ge(ff_shared, 2 * e + m + 1)
                vec.tensor_tensor(gated[:, m, :], gated[:, m, :], bank[6 + m][:, 0:T], ALU.mult).then_inc(ff_product, 1)

        def parts(e):
            vec.wait_ge(ff_product, 2 * base + 2 + 2 * e)
            vec.wait_ge(slab_used, first + 2 + 3 * e)
            vec.tensor_copy(h_hi[:, :, :], gated[:, :, :]).then_inc(ff_h_hi, 1)
            vec.wait_ge(ff_h_hi, base + 1 + e)
            vec.tensor_tensor(h_lo[:, :, :], gated[:, :, :], h_hi[:, :, :].bitcast(F32), ALU.subtract)\
               .then_inc(ff_hidden, 1)

        vec.wait_ge(slab_used, first + 2)
        with vec.Fori(0, n - 1) as i:
            product(i)
            unit_lo(vec, first, base, 3, i)
            parts(i)
            unit_lo(vec, first, base, 4, i)
            unit_lo(vec, first, base, 5, i)
        product(n - 1)
        parts(n - 1)

    def row_load(eng, name, src, lo=0, hi=P):
        tile, at = ROW[name]
        n = src.shape[0]
        eng.dma_start(rows[at:at + n, tile, lo:hi], src).then_inc(loads["rows2" if tile else "rows"], 16)

    def vector_rows(v):
        return v.rearrange("(n p) -> n p", p=P)

    block = ctx.enter_context(nc.Block())

    @block.sync
    def _(sp):
        sp.dma_start(x[:, :, :], dram["x"][0].rearrange("(t p) d -> p t d", p=P)).then_inc(loads["x"], 16)

        def load_slab(s, name, c):
            before = [(f, b) for f, b, n in SPLIT if f <= s - RING < f + n]
            if before:
                f, b = before[0]
                sp.wait_ge(w_lo_ready, b + s - RING - f + 1)
            elif s >= RING:
                sp.wait_ge(slab_used, s - RING + 1)
            sp.dma_start(ring[:, s % RING, :, :], weights(name, c, SW)).then_inc(slab_loaded[s % RING], 16)

        b_in = dram["b_in"][0]
        row_load(sp, "g_mix", vector_rows(dram["g_norm_mix"][0]))
        row_load(sp, "b_qk", vector_rows(b_in[C_MQ:C_MV]))
        row_load(sp, "b_nq", vector_rows(b_in[C_NQ:C_KV]))
        row_load(sp, "b_merge", vector_rows(b_in[C_MERGE:C_MERGE + 2 * D]))
        tile, at = ROW["b_kv"]
        sp.dma_start(rows[at:at + 3, tile, :], vector_rows(b_in[C_KV:C_KV + 3 * N_KV])).then_inc(loads["rows"], 16)
        sp.dma_start(rows[at + 3:at + 4, tile, :], vector_rows(b_in[C_KV + 4 * N_KV:C_KV + 5 * N_KV]))\
            .then_inc(loads["rows"], 16)
        row_load(sp, "conv", dram["conv_qk"][0].rearrange("j (n p) -> (j n) p", p=P))
        row_load(sp, "g_head", vector_rows(dram["g_mlstm_head"][0]))
        row_load(sp, "g_ffn", vector_rows(dram["g_norm_ffn"][0]))
        row_load(sp, "pe", dram["pe_cmp"][0].rearrange("j (n l) d -> (j n) (l d)", l=2))

        for name, matrix, c, n in STREAM:
            if name == "ffn":
                cols_, down = (lambda m: dram[m][0].rearrange("(k p) n -> p k n", p=P)), \
                    dram["w_down"][0].rearrange("(n p) d -> p n d", p=P)
                units_load(sp, SLAB[name], FF // SW, 0, lambda u: cols_("w_gate")[:, :, bass.ds(u * SW, SW)],
                           lambda u: cols_("w_up")[:, :, bass.ds(u * SW, SW)],
                           lambda u: down[:, bass.ds(u * 2, 2), :])
                continue
            if name == "moe":
                up = (lambda m: dram[m][0].rearrange("e (k p) f -> p (e k) f", p=P))
                down2 = dram["w_down_2"][0].rearrange("e (n p) d -> p (e n) d", p=P)
                units_load(sp, SLAB[name], NEXP, FF // SW, lambda u: up("w_gate_2")[:, bass.ds(u * KT, KT), :],
                           lambda u: up("w_up_2")[:, bass.ds(u * KT, KT), :],
                           lambda u: down2[:, bass.ds(u * 2, 2), :])
                continue
            for j in range(n):
                load_slab(SLAB[name] + j, matrix, c + j * SW)
            if name == "kv":
                sp.wait_ge(loads["rev"], 16)
                sp.dma_start(dram["rev_copies"], spread(dram["rev"], (0, P), (1, REV))).then_inc(loads["copies"], 16)
                sp.wait_ge(loads["copies"], 16)
                src = bass.AP(tensor=dram["rev_copies"].tensor, offset=P - 1,
                              ap=[[REV - 1, P], [P * REV, NH], [1, T]])
                sp.dma_start(strip[:, :, :], src).then_inc(loads["strip"], 16)
        sp.wait_ge(*b2_vec.done("y", 1))
        sp.wait_ge(*b2_act.done("y", 1))
        sp.dma_start(out.rearrange("z (t p) d -> p (z t) d", p=P), x[:, :, :]).then_inc(stored, 16)
        sp.wait_ge(stored, 16)

    @block.gpsimd
    def _(pool):
        pool.memset(ones[:, :], 1.0).then_inc(*setup_pool.did("ones"))
        pool.memset(minus_half[:, :], -0.5).then_inc(*setup_pool.did("minus_half"))
        pool.memset(qk_pre[:, :, 0:3], 0.0).then_inc(*setup_pool.did("pad"))
        pool.memset(v1[:, :, :, MD:MD + 1], 1.0).then_inc(*setup_pool.did("ones_v"))
        row_load(pool, "g_mix2", vector_rows(dram["g_mix_2"][0]))
        row_load(pool, "g_mem", vector_rows(dram["g_mem_2"][0]))
        row_load(pool, "g_dq", vector_rows(dram["dsa_q_norm_2"][0]))
        row_load(pool, "g_dk", vector_rows(dram["dsa_k_norm_2"][0]))
        for lo in (0, IDIM):
            row_load(pool, "g_ik", dram["idx_k_norm_2"], lo, lo + IDIM)
        row_load(pool, "g_mq", vector_rows(dram["mem_q_norm_2"][0]))
        row_load(pool, "g_mk", vector_rows(dram["mem_k_norm_2"][0]))
        row_load(pool, "g_gla", vector_rows(dram["gla_norm_2"][0]))
        row_load(pool, "b_gate", vector_rows(dram["b_gate_2"][0]))
        row_load(pool, "g_ffn2", vector_rows(dram["g_ffn_2"][0]))

        pool.wait_ge(*setup_pool.done("minus_half"))
        norm_root(pool, "mix")
        pool.wait_ge(*ml_vec.done("var"))
        pool.tensor_tensor(den[:, :, :].rearrange("p t h -> p (t h)"), den[:, :, :].rearrange("p t h -> p (t h)"),
                           minus_half[:, 0:TT * MH], ALU.pow).then_inc(*ml_pool.did("root"))
        for name in ("ffn", "mem", "final", "mix2"):
            norm_root(pool, name)
        for name, heads in (("mk", EH), ("mq", EH), ("gla", GH), ("dq", DH), ("dk", DG), ("ik", 1)):
            head_root(pool, name, heads)
        norm_root(pool, "ffn2")

    ROW_LOADS = (10, 11)

    @block.scalar
    def _(act):
        def load(dst, src, name):
            act.dma_start(dst, src).then_inc(loads[name], 16)

        for dst, name in ((ident, "c_ident"), (tri, "c_tri"), (tri64, "c_tri64"), (mask_after, "c_mask_after"),
                          (mask_before, "c_mask_before"), (causal, "c_causal")):
            load(dst[:, :], dram[name], "const")
        norm_square(act, "mix", x, (loads["x"], 16))
        load(oh_rev[:, :], dram["c_oh_rev"], "rel")
        load(oh_cmp[:, :], dram["c_oh_cmp"], "rel")
        load(rel[0:BUCKETS, :], dram["rel_bias"], "rel")
        load(rel[BUCKETS:BUCKETS + 1, :], dram["c_neg"], "rel")
        load(seen[:, :, :], dram["c_seen"], "rel")
        b_in = dram["b_in"][0]
        load(small[:, :, 0:8], weights("w_in", C_MI, 8), "small")
        load(small[:, :, 8:32], weights("w_in", C_NGATE, 3 * NH), "small")
        norm_gain(act, "mix", "g_mix", xT)
        load(g_fin[:, :], dram["g_final"].partition_broadcast(P), "g_fin")
        load(b_vo[:, :], b_in[C_MV:C_MI].partition_broadcast(P), "broadcast")
        load(b_small[:, 0:8], b_in[C_MI:C_NQ].partition_broadcast(P), "broadcast")
        load(b_small[:, 8:32], b_in[C_NGATE:C_MERGE].partition_broadcast(P), "broadcast")
        load(b_vs[:, 0, :], b_in[C_KV + 3 * N_KV:C_KV + 4 * N_KV].partition_broadcast(P), "broadcast")
        load(b_vs[:, 1, :], b_in[C_KV + 5 * N_KV:C_KV + 6 * N_KV].partition_broadcast(P), "broadcast")
        load(b_fg[:, :], dram["b_fgate"][0].partition_broadcast(P), "broadcast")
        for j in range(2):
            load(w_cmp1[:, j, :, :], dram["w_cmp1"][0, j].rearrange("(n p) h -> p n h", p=P), "cmp")
        load(w_cmp2k[:, 0, :], dram["w_cmp2"][0, 0], "cmp")
        load(w_cmp2k[:, 1, :], dram["w_cmp2"][0, 0], "cmp")
        load(w_cmp2v[:, :], dram["w_cmp2"][0, 1], "cmp")
        act.wait_ge(*setup_vec.done("rev"))
        load(dram["rev"], rev[:, :], "rev")

        for j in range(4):
            slab_out(act, "qk", j)
            for n in range(2):
                act.activation(qk_pre[:, 2 * j + n, 3:3 + T], half(SLAB["qk"] + j, n), ACT.Identity,
                               bias=col("b_qk", 2 * j + n)).then_inc(*half_read(SLAB["qk"] + j))
        for n in range(8):
            act.wait_ge(*ml_vec.done("conv", n))
            act.activation(sig[:, n, :], qk[:, n, :], ACT.Sigmoid).then_inc(*ml_act.did("sig", n))
        slab_out(act, "kv", 0)
        s = SLAB["kv"]
        for j in range(2):
            bias = col("b_kv", j)
            act.activation(cmp_in[0:ND, j, 0, 1:T + 1], half(s, j)[0:ND, :], ACT.Identity, bias=bias[0:ND, :])\
               .then_inc(*in1_act.did("cmp0", j))
            act.activation(cmp_in[ND:P, j, 1, 0:T], half(s, j)[ND:P, :], ACT.Identity, bias=bias[ND:P, :])\
               .then_inc(*half_read(s))
        for j in range(2):
            slab_out(act, "kv", 1 + j)
            s = SLAB["kv"] + 1 + j
            bias = col("b_kv", 2 + j)
            act.activation(kT[0:ND, j, 0, :], half(s, 0)[0:ND, :], ACT.Identity, bias=bias[0:ND, :])\
               .then_inc(*in1_act.did("k0", j))
            act.activation(kT[ND:P, j, 1, :], half(s, 0)[ND:P, :], ACT.Identity, bias=bias[ND:P, :])\
               .then_inc(*half_read(s))
        evicted(act, SLAB["kv"] + 2)
        for dst, src in ((cmp_in[ND:P, :, 0, 0:T], cmp_in[0:ND, :, 0, 1:T + 1]),
                         (cmp_in[0:ND, :, 1, 1:T + 1], cmp_in[ND:P, :, 1, 0:T]),
                         (kT[ND:P, :, 0, :], kT[0:ND, :, 0, :]), (kT[0:ND, :, 1, :], kT[ND:P, :, 1, :])):
            act.dma_start(dst, src).then_inc(loads["twice"], 16)

        evicted(act, SLAB["vo"] + 3)
        act.activation(sig_o[:, :, :], sig_o[:, :, :], ACT.Sigmoid).then_inc(*ml_act.did("sig_o"))
        act.wait_ge(*in1_vec.done("gate_in"))
        act.activation(nsa_gate[:, :, :], gate_in[:, :, 8:32], ACT.Sigmoid).then_inc(*ns_act.did("gate"))
        act.wait_ge(*ml_vec.done("fa"))
        act.activation(fe[:, :, :], fa[:, :, :], ACT.Exp, scale=-1.0).then_inc(*ml_act.did("fe"))
        act.wait_ge(*ml_act.done("fe"))
        act.activation(fe[:, :, :], fe[:, :, :], ACT.Ln, bias=1.0).then_inc(*ml_act.did("ln"))

        def merge_gate(j):
            slab_out(act, "merge", j)
            for n in range(2):
                act.activation(mergeT[:, 2 * j + n, :], half(SLAB["merge"] + j, n), ACT.Sigmoid,
                               bias=col("b_merge", 2 * j + n)).then_inc(*half_read(SLAB["merge"] + j))

        merge_gate(0)
        merge_gate(1)

        act.wait_ge(*ns_pe.done("hid"))
        act.activation(hid_s[:, :, :], bank[4][:, 0:2 * NG * NCMP].rearrange("p (j n) -> p j n", j=2),
                       ACT.Sigmoid).then_inc(*ns_act.did("hid_s"))
        merge_gate(2)
        merge_gate(3)

        for c in range(TT):
            act.wait_ge(*ml_vec.done("yy", c))
            act.activation(yy[:, c, :, :], yy[:, c, :, :], ACT.Exp, scale=-1.0).then_inc(*ml_act.did("yy", c))
        act.wait_ge(*ml_vec.done("w_st"))
        act.activation(w_st[:, :, :], w_st[:, :, :], ACT.Exp).then_inc(*ml_act.did("w_st"))
        act.wait_ge(*ml_vec.done("em"))
        act.activation(em[:, :, :], em[:, :, :], ACT.Exp, scale=-1.0).then_inc(*ml_act.did("em"))
        merge_gate(4)
        act.wait_ge(*ml_pe.done("k_tok"))
        act.activation(k_tok[:, :, :], bank[5][:, :].rearrange("p (h d) -> p h d", h=MH),
                       ACT.Copy).then_inc(*ml_act.did("k_tok"))

        def pair(b):
            return bank[b][:, 0:2 * (MD + 1)].rearrange("p (h d) -> p h d", h=2)

        for n, b in enumerate((6, 4)):
            act.wait_ge(*ml_pe.done("c1", n))
            act.activation(c1[:, 2 * n:2 * n + 2, :], pair(b), ACT.Copy).then_inc(*ml_act.did("c1", n))
        for c, banks in enumerate(((5, 7), (6, 4))):
            for n, b in enumerate(banks):
                act.wait_ge(*ml_pe.done("num", c, n))
                act.activation(hh[:, c, 2 * n:2 * n + 2, :], pair(b), ACT.Copy).then_inc(*ml_act.did("num", c, n))
        merge_gate(5)
        merge_gate(6)
        for k in range(4):
            act.wait_ge(*ml_pe.done("yT", k // 2))
            act.activation(ysT[:, k, :], bank[(4, 6)[k // 2]][:, (k % 2) * T:(k % 2) * T + T], ACT.Copy,
                           scale=col("g_head", k)).then_inc(*ml_act.did("yT", k))

        act.wait_ge(*ns_vec.done("lc"))
        act.activation(ec[:, :, :, :], lc[:, :, :, :], ACT.Exp).then_inc(*ns_act.did("ec"))
        merge_gate(7)
        for n, b in enumerate((7, 4, 5, 6)):
            act.wait_ge(*ns_pe.done("pcT", n))
            act.activation(pcT[:, n // 2, (n % 2) * 4:(n % 2) * 4 + 4, :],
                           bank[b][0:NCMP, :].rearrange("p (h q) -> p h q", h=4),
                           ACT.Copy).then_inc(*ns_act.did("pcT", n))
        for u in range(8):
            tt, g, br = u // 4, u // 2 % 2, u % 2
            K = (tt + 1) * P
            act.wait_ge(*ns_vec.done("shift", u))
            act.activation(lg[:, u % 2, :, 0:K], lg[:, u % 2, :, 0:K], ACT.Exp).then_inc(*ns_act.did("exp", u))
            for kt in range(tt + 1):
                act.wait_ge(*ns_pe.done("aT", u, kt))
                if kt == 0 and u >= 2:
                    act.wait_ge(*ns_pe.done("av", (u - 2) // 2))
                act.activation(aT[:, br, kt, :, :], bank[6 + kt][:, :].rearrange("p (h q) -> p h q", h=NREP),
                               ACT.Copy).then_inc(*ns_act.did("aT", u, kt))
            if br == 1 and g == 1:
                act.wait_ge(*ns_pe.done("av", u // 2))
                act.activation(ysT[:, 4:8, tt * P:tt * P + P],
                               bank[2 + tt][:, :].rearrange("p (h q) -> p h q", h=4),
                               ACT.Copy).then_inc(*ns_act.did("yT", tt))

        norm_square(act, "ffn", x, *all_out(SLAB["out"] + 3))
        load(mem[:, :, :], dram["mem_2"][0].rearrange("(t p) d -> p t d", p=P), "mem")
        load(b_r[:, 0:NGRP], dram["b_r1_2"][0].partition_broadcast(P), "second")
        load(b_r[:, NGRP:], dram["b_r2_2"][0].partition_broadcast(P), "second")
        load(iota4[:, :], dram["c_iota4"], "router")
        load(small[:, :, 0:GRANK], weights("w_in_2", B_GA, GRANK), "narrow")
        load(small[:, :, 16:16 + IDIM + IH], weights("w_in_2", B_IK, IDIM + IH), "narrow")
        for q in range(2):
            unit_hi(act, SLAB["ffn"], 0, q)
        norm_gain(act, "ffn", "g_ffn", xT)
        unit_hi(act, SLAB["ffn"], 0, 2)
        units_act(act, SLAB["ffn"], FF // SW, 0)
        U = 3 * (FF // SW)
        norm_square(act, "mem", mem, (loads["mem"], 16))
        unit_hi(act, SLAB["ffn"], 0, U)
        unit_hi(act, SLAB["ffn"], 0, U + 1)
        for b in (2, 3):
            act.wait_ge(slab_used, SLAB["ffn"] + 3 * (FF // SW))
            act.activation(x[:, 1, (b % 2) * 512:(b % 2 + 1) * 512], bank[b][:, :], ACT.Copy)\
               .then_inc(*b2_act.did("h", b - 2))

        def extra_hi(start, end):
            for n in range(start, end):
                unit_hi(act, SLAB["ffn"], 0, U + n)

        def mem_out(start, end):
            for j in range(start, end):
                slab_out(act, "memkv", j)
                for t in range(TT):
                    act.activation((mk if j < 4 else mv)[:, t, (j % 4) * SW:(j % 4 + 1) * SW],
                                   half(SLAB["memkv"] + j, t), ACT.Copy).then_inc(*half_read(SLAB["memkv"] + j))
                extra_hi(j + RING, j + RING + 1)

        def gqk_out(start, end):
            for j in range(start, end):
                slab_out(act, "gqk", j)
                for n in range(2):
                    act.activation(gqk[:, 2 * j + n, :], half(SLAB["gqk"] + j, n), ACT.Copy)\
                       .then_inc(*half_read(SLAB["gqk"] + j))

        def gvg_out(start, end):
            for j in range(start, end):
                slab_out(act, "gvg", j)
                for t in range(TT):
                    act.activation((gv if j < 4 else gg)[:, t, (j % 4) * SW:(j % 4 + 1) * SW],
                                   half(SLAB["gvg"] + j, t), ACT.Copy if j < 4 else ACT.Silu)\
                       .then_inc(*half_read(SLAB["gvg"] + j))

        def dkv_out(j):
            slab_out(act, "dkv", j)
            for t in range(TT):
                act.activation((dk, dv)[j][:, t, :], half(SLAB["dkv"] + j, t), ACT.Copy)\
                   .then_inc(*half_read(SLAB["dkv"] + j))

        def iq_out(j):
            slab_out(act, "iq", j)
            for n in range(2):
                act.activation(iqT[:, 2 * j + n, :], half(SLAB["iq"] + j, n), ACT.Copy)\
                   .then_inc(*half_read(SLAB["iq"] + j))

        def branch_gate(branch, j):
            name, z, _ = BRANCHES[branch]
            s = SLAB[f"gate_{name}{j}"]
            slab_out(act, f"gate_{name}{j}", 0)
            m = BANKED[s] - 1
            act.wait_ge(bank_read[m % 2], 2 * (m // 2 + 1))
            for n in range(2):
                act.activation(gated[:, n, :], half(s, n), ACT.Sigmoid, bias=col("b_gate", z * 8 + 2 * j + n))\
                   .then_inc(*half_read(s))

        extra_hi(2, 3)
        norm_gain(act, "mem", "g_mem", memT)
        norm_square(act, "final", x, b2_act.done("h", 1), b2_vec.done("h", 1))
        mem_out(0, 2)
        norm_square(act, "mix2", x, b2_vec.done("x2", 1))
        mem_out(2, 4)
        norm_gain(act, "mix2", "g_mix2", xT)
        mem_out(4, 8)
        turned(act, "mk", 8, mkT, lambda k: col("g_mk", k % 2))
        extra_hi(11, 15)
        gqk_out(0, 1)
        extra_hi(15, 16)
        gqk_out(1, 3)
        turned(act, "mq", 8, mqT, lambda k: scaled[:, k % 2:k % 2 + 1])

        def store_mem(tt, g):
            for b in range(2):
                act.activation(o_mT[:, 4 * b:4 * b + 4, tt * P:(tt + 1) * P],
                               bank[2 + b][:, :].rearrange("p (k q) -> p k q", k=4), ACT.Copy)\
                   .then_inc(*(b2_act.did("o", "mem", tt, g) if b else b2_act.did("o_", "mem", tt, g)))

        gqk_out(3, 4)
        load(w_a2[:, :], dram["w_gla_a2_2"][0], "second")
        load(b_a2[:, :], dram["b_gla_a2_2"][0].partition_broadcast(P), "second")
        attend_act(act, "mem", store_mem, lambda n: gvg_out(2 * n, 2 * n + 2))
        gvg_out(4, 7)
        act.wait_ge(*b2_vec.done("lz"))
        act.activation(lz[:, :, :], lz[:, :, :], ACT.Exp, scale=-1.0).then_inc(*b2_act.did("lz"))
        act.wait_ge(*b2_act.done("lz"))
        act.activation(lz[:, :, :], lz[:, :, :], ACT.Ln, bias=1.0).then_inc(*b2_act.did("ln"))
        gvg_out(7, 8)
        for t in range(TT):
            act.wait_ge(*b2_pe.done("cum", t))
            act.activation(cum[:, :, t * P:(t + 1) * P], bank[5 + t][:, :].rearrange("p (h q) -> p h q", h=GH),
                           ACT.Copy).then_inc(*b2_act.did("cum", t))
        act.wait_ge(*b2_act.done("cum", 1))
        act.activation(ex[:, :, :], cum[:, :, :], ACT.Exp, scale=1 / GTEMP).then_inc(*b2_act.did("ex", 0))
        act.activation(ki[:, :, :], cum[:, :, :], ACT.Exp, scale=-1 / GTEMP).then_inc(*b2_act.did("ex", 1))
        act.activation(decay[:, :, :], cum[:, :, GCHUNK - 1::GCHUNK], ACT.Exp, scale=1 / GTEMP)\
           .then_inc(*b2_act.did("decay"))
        act.wait_ge(*b2_vec.done("rest"))
        act.activation(ex[:, :, :], cum[:, :, :], ACT.Exp, scale=1 / GTEMP).then_inc(*b2_act.did("ex", 2))
        for t in range(TT):
            act.wait_ge(*b2_pe.done("ke_tok", t))
            act.activation(ke_tok[:, t, :, :], bank[6 + t][:, :].rearrange("p (h q) -> p h q", h=GH), ACT.Copy)\
               .then_inc(*b2_act.did("ke_tok", t))
        dkv_out(0)
        dkv_out(1)
        iq_out(0)
        iq_out(1)
        branch_gate(0, 0)
        turned(act, "gla", 8, o_gT, lambda k: col("g_gla", k % 2))
        branch_gate(0, 1)
        turned(act, "dq", 8, dqT, lambda k: scaled[:, 2:3])
        turned(act, "dk", 2, dkT, lambda k: col("g_dk"))
        turned(act, "ik", 1, ikT[:, :].rearrange("p (a t) -> p a t", a=1), lambda k: col("g_ik"))
        for t in range(TT):
            K = (t + 1) * P
            act.wait_ge(*b2_pe.done("idx", t))
            if t:
                act.wait_ge(*b2_vec.done("idx", 0, IH - 1))
            for b in range(4):
                odd, i = b % 2, 2 * (b // 2)
                src = bank[2 + b][:, :].rearrange("p (h k) -> p h k", h=2)[:, :, 0:K]
                act.activation(relu[:, 2 * i + odd:2 * i + odd + 3:2, 0:K], src, ACT.Relu)\
                   .then_inc(*(b2_act.did("relu", t) if b == 3 else b2_act.did("relu_", t, b)))

        def store_dsa(tt, g):
            act.activation(o_dT[:, g * DREP:(g + 1) * DREP, tt * P:(tt + 1) * P],
                           bank[2][:, :].rearrange("p (h q) -> p h q", h=4), ACT.Copy)\
               .then_inc(*b2_act.did("o", "dsa", tt, g))

        branch_gate(0, 2)
        branch_gate(0, 3)
        attend_act(act, "dsa", store_dsa, lambda n: branch_gate(1, n))
        for j in range(4):
            branch_gate(2, j)
        norm_square(act, "ffn2", x, *all_out(SLAB["out2"] + 3))
        load(small[:, :, 0:NGRP], dram["w_r1_2"][0].rearrange("(k p) n -> p k n", p=P), "router")
        load(small[:, :, NGRP:NGRP + NEXP], dram["w_r2_2"][0].rearrange("(k p) n -> p k n", p=P), "router")
        for q in range(2):
            unit_hi(act, SLAB["moe"], FF // SW, q)
        norm_gain(act, "ffn2", "g_ffn2", xT)
        unit_hi(act, SLAB["moe"], FF // SW, 2)
        act.wait_ge(*b2_vec.done("rl"))
        act.activation(r_tmp[:, :, 0:NGRP], r_tmp[:, :, 0:NGRP], ACT.Exp).then_inc(*b2_act.did("g_exp"))
        act.wait_ge(*b2_vec.done("l2"))
        act.activation(r_s[:, 5, :], r_s[:, 4, :], ACT.Exp).then_inc(*b2_act.did("e_exp"))

        def shares():
            for n in range(8):
                act.wait_ge(*b2_pe.done("comb", n))
                act.activation(comb_all[:, 2 * n:2 * n + 2, :],
                               bank[2 + n % 2][:, :].rearrange("p (e t) -> p e t", e=2), ACT.Copy)\
                   .then_inc(*b2_act.did("comb", n))

        units_act(act, SLAB["moe"], NEXP, FF // SW, shares)
        for b in (2, 3):
            act.wait_ge(slab_used, SLAB["moe"] + 3 * NEXP)
            act.activation(x[:, 1, (b % 2) * 512:(b % 2 + 1) * 512], bank[b][:, :], ACT.Copy)\
               .then_inc(*b2_act.did("y", b - 2))

    @block.vector
    def _(vec):
        tt_, ts_, stt_ = vec.tensor_tensor, vec.tensor_scalar, vec.scalar_tensor_tensor
        def columns(tile):
            vec.wait_ge(*setup_pe.done("cols", tile))
            vec.tensor_copy(cols[:, tile, 0:NROWS[tile]], bank[2 + tile][:, 0:NROWS[tile]])\
               .then_inc(*setup_vec.did("cols", tile))

        norm_scale(vec, "mix", x)
        columns(0)
        vec.wait_ge(*setup_pe.done("rev"))
        vec.tensor_copy(rev[:, :], bank[3][0:NH, 0:REV]).then_inc(*setup_vec.did("rev"))
        vec.wait_ge(*setup_pe.done("cmp_bias"))
        vec.tensor_copy(cmp_bias[:, :, :, :],
                        bank[2][:, 0:TT * NCMP * NH].rearrange("p (t c h) -> p t c h", t=TT, c=NCMP))\
           .then_inc(*setup_vec.did("cmp_bias"))
        columns(1)

        def conv_tap(j):
            evicted(vec, SLAB["qk"] + 3)
            vec.wait_ge(*setup_pool.done("pad"))
            for n in range(8):
                w = cols[:, ROW["conv"][0], ROW["conv"][1] + 8 * j + n:ROW["conv"][1] + 8 * j + n + 1]
                if j == 0:
                    ts_(qk[:, n, :], qk_pre[:, n, 0:T], w, None, ALU.mult).then_inc(*ml_vec.did("conv0", n))
                    continue
                vec.wait_ge(*ml_vec.done(f"conv{j - 1}", n))
                stt_(qk[:, n, :], qk_pre[:, n, j:j + T], w, qk[:, n, :], ALU.mult, ALU.add)\
                    .then_inc(*ml_vec.did(f"conv{j}" if j < 3 else "conv", n))

        vec.wait_ge(loads["broadcast"], 16 * 6)
        for j in range(4):
            slab_out(vec, "vo", j)
            s = SLAB["vo"] + j
            for t in range(TT):
                if j < 2:
                    dst = v1[:, t, 2 * j:2 * j + 2, 0:MD]
                    src = half(s, t).rearrange("p (h d) -> p h d", h=2)
                    b = b_vo[:, j * SW:(j + 1) * SW].rearrange("p (h d) -> p h d", h=2)
                else:
                    dst, src = sig_o[:, t, (j - 2) * SW:(j - 1) * SW], half(s, t)
                    b = b_vo[:, j * SW:(j + 1) * SW]
                tt_(dst, src, b, ALU.add).then_inc(*half_read(s))
            conv_tap(j)
        vec.wait_ge(*in1_pe.done("small"))
        tt_(gate_in[:, :, :], bank[4][:, 0:64].rearrange("p (t n) -> p t n", t=TT),
            spread(b_small[:, :], (0, TT), (1, 32)), ALU.add).then_inc(*in1_vec.did("gate_in"))
        for n in range(8):
            vec.wait_ge(*ml_act.done("sig", n))
            stt_(qk[:, n, :], sig[:, n, :], 1.0 if n < 4 else MD ** -0.5, qk[:, n, :], ALU.mult, ALU.mult)\
                .then_inc(*ml_vec.did("silu", n))
        for j in range(2):
            slab_out(vec, "nq", j)
            s = SLAB["nq"] + j
            for n in range(2):
                ts_(nqT[:, 2 * j + n, :], half(s, n), col("b_nq", 2 * j + n), ND ** -0.5,
                    ALU.add, ALU.mult).then_inc(*half_read(s))
        for j in range(2):
            s = SLAB["kv"] + 1 + j
            other_half(vec, s)
            tt_(v_sw[:, j, :, :], half(s, 1).rearrange("p (t n) -> p t n", t=TT),
                spread(b_vs[:, j, :], (0, TT), (1, N_KV)), ALU.add).then_inc(*half_read(s))

        vec.wait_ge(*in1_vec.done("gate_in"))
        tt_(fz[:, :, :], gate_in[:, :, 4:8], spread(b_fg[:, :], (0, TT), (1, MH)), ALU.add)\
            .then_inc(*ml_vec.did("fz"))
        vec.wait_ge(*ml_vec.done("fz"))
        stt_(fa[:, :, :], fz[:, :, :], -1.0, fz[:, :, :], ALU.mult, ALU.max).then_inc(*ml_vec.did("fa"))
        vec.wait_ge(loads["twice"], 16 * 4)
        for j in range(2):
            for g in range(NG):
                blocks = spread(cmp_in[:, j, g, 1:], (2, CMP_PAIRS), (CMP_STRIDE, NCMP))
                tile, at = ROW["pe"]
                pe_cols = along(cols[:, tile, at + CMP_PAIRS * j:at + CMP_PAIRS * (j + 1)], NCMP)
                tt_(blk[:, j, :, g, :], blocks, pe_cols, ALU.add).then_inc(*ns_vec.did("blk", j, g))
        vec.wait_ge(*ml_act.done("ln"))
        stt_(lf[:, :, :], fz[:, :, :], 0.0, fe[:, :, :], ALU.min, ALU.subtract).then_inc(*ml_vec.did("lf"))
        vec.wait_ge(*ns_act.done("hid_s"))
        tt_(hid[:, :, :], hid_s[:, :, :], bank[4][:, 0:2 * NG * NCMP].rearrange("p (j n) -> p j n", j=2), ALU.mult)\
            .then_inc(*ns_vec.did("hid"))
        vec.wait_ge(*ns_pe.done("kcT"))
        vec.tensor_copy(kcT[:, :], bank[5][:, 0:NG * NCMP]).then_inc(*ns_vec.did("kcT"))
        vec.tensor_copy(vc[:, :, :], bank[5][0:NCMP, 128:128 + NG * ND].rearrange("p (g d) -> p g d", g=NG))\
           .then_inc(*ns_vec.did("vc"))
        vec.wait_ge(*ml_pe.done("bc"))
        vec.tensor_copy(bc[:, :, :, :], bank[4][:, 0:4 * MH].rearrange("p (a t h) -> p a t h", a=2, t=TT))\
           .then_inc(*ml_vec.did("bc"))
        vec.wait_ge(*ml_vec.done("bc"))
        tt_(cc[:, :, :], gate_in[:, :, 0:4], bc[:, 0, :, :], ALU.subtract).then_inc(*ml_vec.did("cc"))
        for c in range(TT):
            vec.wait_ge(*ml_pe.done("crow", c))
            row = bank[5 + c][:, :].rearrange("p (h j) -> p h j", h=MH)
            if c == 0:
                vec.tensor_reduce(cx[:, :], row, AX.X, ALU.max).then_inc(*ml_vec.did("cx"))
            tt_(yy[:, c, :, :], row, spread(mask_after[:, :], (0, MH), (1, P)), ALU.add)\
                .then_inc(*ml_vec.did("masked", c))
        for c in range(TT):
            vec.wait_ge(*ml_vec.done("masked", c))
            vec.tensor_reduce(cm[:, c, :], yy[:, c, :, :], AX.X, ALU.max).then_inc(*ml_vec.did("cm", c))
        vec.wait_ge(*ml_vec.done("cm", 1))
        stt_(m1[:, :], cx[:, :], 0.0, bc[:, 1, 0, :], ALU.max, ALU.add).then_inc(*ml_vec.did("m1"))
        ts_(mm[:, 0, :], cm[:, 0, :], 0.0, None, ALU.max).then_inc(*ml_vec.did("mm", 0))
        vec.wait_ge(*ml_vec.done("m1"))
        tt_(mm[:, 1, :], cm[:, 1, :], m1[:, :], ALU.max).then_inc(*ml_vec.did("mm", 1))
        tt_(w_st[:, 0, :], cc[:, 0, :], bc[:, 1, 0, :], ALU.add).then_inc(*ml_vec.did("a0"))
        vec.wait_ge(*ml_vec.done("a0"))
        tt_(w_st[:, 0, :], w_st[:, 0, :], m1[:, :], ALU.subtract).then_inc(*ml_vec.did("a0m"))
        tt_(w_st[:, 1, :], m1[:, :], mm[:, 1, :], ALU.subtract).then_inc(*ml_vec.did("s_inter"))
        ts_(w_st[:, 2, :], m1[:, :], 0.0, None, ALU.mult).then_inc(*ml_vec.did("w_st"))
        tt_(em[:, :, :], bc[:, 0, :, :], mm[:, :, :], ALU.add).then_inc(*ml_vec.did("em"))
        for c in range(TT):
            vec.wait_ge(*ml_pe.done("mrow", c))
            for h in range(MH):
                ins = stt_(yy[:, c, h, :], bank[5 + c][:, h * P:(h + 1) * P], cc[:, c, h:h + 1], mask_before[:, :],
                           ALU.subtract, ALU.add)
                ins.then_inc(*(ml_vec.did("yy", c) if h == MH - 1 else ml_vec.did("yy_", c, h)))
        for c, b in enumerate((4, 7)):
            vec.wait_ge(*ml_act.done("yy", c))
            vec.wait_ge(*ml_pe.done("st", c))
            tt_(pT[:, c, :, :], yy[:, c, :, :], bank[b][:, :].rearrange("p (h j) -> p h j", h=MH), ALU.mult)\
                .then_inc(*ml_vec.did("pT", c))
        vec.wait_ge(*ml_act.done("w_st"))
        tt_(wv[:, :, :], v1[:, 0, :, :], along(w_st[:, 0, :], MD + 1), ALU.mult).then_inc(*ml_vec.did("wv"))
        for n, b in enumerate((5, 7)):
            vec.wait_ge(*ml_pe.done("inter", n))
            vec.wait_ge(*ml_act.done("num", 1, n))
            for i in range(2):
                h = 2 * n + i
                stt_(hh[:, 1, h, :], bank[b][:, i * (MD + 1):(i + 1) * (MD + 1)], w_st[:, 1, h:h + 1],
                     hh[:, 1, h, :], ALU.mult, ALU.add).then_inc(*ml_vec.did("hh", h))
        vec.wait_ge(*ml_act.done("em"))
        vec.wait_ge(*ml_vec.done("hh", 3))
        for c in range(TT):
            stt_(den[:, c, :], hh[:, c, :, MD], -1.0, hh[:, c, :, MD], ALU.mult, ALU.max).then_inc(*ml_vec.did("abs", c))
        vec.wait_ge(*ml_vec.done("abs", 1))
        tt_(den[:, :, :], den[:, :, :], em[:, :, :], ALU.max).then_inc(*ml_vec.did("den", 1))
        vec.wait_ge(*ml_vec.done("den", 1))
        vec.reciprocal(den[:, :, :], den[:, :, :]).then_inc(*ml_vec.did("rden"))
        vec.wait_ge(*ml_vec.done("rden"))
        for c in range(TT):
            tt_(hn[:, c, :, :], hh[:, c, :, 0:MD], along(den[:, c, :], MD), ALU.mult).then_inc(*ml_vec.did("hn", c))
        for c in range(TT):
            vec.wait_ge(*ml_vec.done("hn", c))
            tt_(hsq[:, c, :, :], hn[:, c, :, :], hn[:, c, :, :], ALU.mult).then_inc(*ml_vec.did("hsq", c))
        for c in range(TT):
            vec.wait_ge(*ml_vec.done("hsq", c))
            vec.tensor_reduce(den[:, c, :], hsq[:, c, :, :], AX.X, ALU.add).then_inc(*ml_vec.did("ssq", c))
        vec.wait_ge(*ml_vec.done("ssq", 1))
        ts_(den[:, :, :], den[:, :, :], 1.0 / MD, EPS, ALU.mult, ALU.add).then_inc(*ml_vec.did("var"))
        vec.wait_ge(*ml_pool.done("root"))
        for c in range(TT):
            tt_(hn[:, c, :, :], hn[:, c, :, :], along(den[:, c, :], MD), ALU.mult).then_inc(*ml_vec.did("hn2", c))
        vec.wait_ge(*ml_act.done("sig_o"))
        for c in range(TT):
            vec.wait_ge(*ml_vec.done("hn2", c))
            tt_(hn[:, c, :, :], hn[:, c, :, :], sig_o[:, c, :].rearrange("p (h d) -> p h d", h=MH), ALU.mult)\
                .then_inc(*ml_vec.did("ym", c))

        vec.wait_ge(*ns_pe.done("lc"))
        for t in range(TT):
            for odd in range(2):
                tt_(lc[:, t, odd::2, :],
                    bank[6 + odd][:, t * NREP * NCMP:(t + 1) * NREP * NCMP].rearrange("p (h c) -> p h c", h=NREP),
                    cmp_bias[:, t, :, odd::2].rearrange("p c h -> p h c"), ALU.add)\
                    .then_inc(*ns_vec.did("lc_", t, odd))
        vec.wait_ge(*ns_vec.done("lc_", 1, 1))
        vec.tensor_reduce(mc[:, :, :], lc[:, :, :, :], AX.X, ALU.max).then_inc(*ns_vec.did("mc"))
        vec.wait_ge(*ns_vec.done("mc"))
        flat = lc[:, :, :, :].rearrange("p t h c -> p (t h) c")
        tt_(flat, flat, along(mc[:, :, :].rearrange("p t h -> p (t h)"), NCMP), ALU.subtract)\
            .then_inc(*ns_vec.did("lc"))
        vec.wait_ge(*ns_act.done("ec"))
        for t in range(TT):
            tt_(ec[:, t, :, :], ec[:, t, :, :], spread(seen[:, t, :], (0, NH), (1, NCMP)), ALU.mult)\
                .then_inc(*ns_vec.did("ec_", t))
        vec.wait_ge(*ns_vec.done("ec_", 1))
        vec.tensor_reduce(sc[:, :, :], ec[:, :, :, :], AX.X, ALU.add).then_inc(*ns_vec.did("sc"))
        vec.wait_ge(*ns_vec.done("sc"))
        ts_(sc[:, :, :], sc[:, :, :], 1e-30, None, ALU.max).then_inc(*ns_vec.did("sc1"))
        vec.wait_ge(*ns_vec.done("sc1"))
        vec.reciprocal(sc[:, :, :], sc[:, :, :]).then_inc(*ns_vec.did("sc2"))
        vec.wait_ge(*ns_vec.done("sc2"))
        vec.wait_ge(*ns_act.done("gate"))
        gates = nsa_gate[:, :, :].rearrange("p t (h b) -> p t h b", b=3)
        tt_(sc[:, :, :], sc[:, :, :], gates[:, :, :, 0], ALU.mult).then_inc(*ns_vec.did("sc3"))
        vec.wait_ge(*ns_vec.done("sc3"))
        flat = ec[:, :, :, :].rearrange("p t h c -> p (t h) c")
        tt_(flat, flat, along(sc[:, :, :].rearrange("p t h -> p (t h)"), NCMP), ALU.mult)\
            .then_inc(*ns_vec.did("pc"))
        vec.wait_ge(loads["strip"], 16)
        for u in range(8):
            tt, g, br = u // 4, u // 2 % 2, u % 2
            K = (tt + 1) * P
            l = lg[:, u % 2, :, 0:K]
            if u >= 2:
                vec.wait_ge(*ns_pe.done("aT", u - 2, (u - 2) // 4))
            for odd in range(2):
                vec.wait_ge(*ns_pe.done("lg", u))
                tt_(lg[:, u % 2, 2 * odd:2 * odd + 2, 0:K],
                    bank[4 + odd][:, 0:2 * K].rearrange("p (h k) -> p h k", h=2),
                    strip[:, g * NREP + odd:(g + 1) * NREP:2, T - K:T], ALU.add)\
                    .then_inc(*ns_vec.did("lg", u, odd))
            vec.wait_ge(*ns_vec.done("lg", u, 1))
            vec.tensor_reduce(mx[:, u % 2, :], l, AX.X, ALU.max).then_inc(*ns_vec.did("mx", u))
            vec.wait_ge(*ns_vec.done("mx", u))
            tt_(l, l, along(mx[:, u % 2, :], K), ALU.subtract).then_inc(*ns_vec.did("shift", u))
            vec.wait_ge(*ns_act.done("exp", u))
            vec.tensor_reduce(sm[:, u % 2, :], l, AX.X, ALU.add).then_inc(*ns_vec.did("sm", u))
            vec.wait_ge(*ns_vec.done("sm", u))
            vec.reciprocal(sm[:, u % 2, :], sm[:, u % 2, :]).then_inc(*ns_vec.did("rs", u))
            vec.wait_ge(*ns_vec.done("rs", u))
            tt_(sm[:, u % 2, :].rearrange("p (o i) -> p o i", o=2), sm[:, u % 2, :].rearrange("p (o i) -> p o i", o=2),
                gates[:, tt, g * NREP:(g + 1) * NREP, 1 + br].rearrange("p (i o) -> p o i", o=2), ALU.mult)\
                .then_inc(*ns_vec.did("gs", u))
            vec.wait_ge(*ns_vec.done("gs", u))
            tt_(l, l, along(sm[:, u % 2, :], K), ALU.mult).then_inc(*ns_vec.did("p", u))

        evicted(vec, SLAB["merge"] + 7)
        for j in range(4):
            slab_out(vec, "branch", j)
            pair_m = mergeT[:, 2 * j:2 * j + 2, :].rearrange("p n t -> p (n t)")
            pair_n = mergeT[:, 8 + 2 * j:10 + 2 * j, :].rearrange("p n t -> p (n t)")
            b = 4 + 2 * (j % 2)
            tt_(mix2[:, 0, :], bank[b][:, :], pair_m, ALU.mult).then_inc(*mix_vec.did("m", j))
            tt_(mix2[:, 1, :], bank[b + 1][:, :], pair_n, ALU.mult).then_inc(*mix_vec.did("n", j))
            vec.wait_ge(*mix_vec.done("n", j))
            tt_(mixT[:, 2 * j:2 * j + 2, :].rearrange("p n t -> p (n t)"), mix2[:, 0, :], mix2[:, 1, :], ALU.add)\
                .then_inc(*mix_vec.did("mix", j))
            vec.wait_ge(*mix_vec.done("mix", j))
        for j in range(4):
            slab_out(vec, "out", j)
            s = SLAB["out"] + j
            for t in range(TT):
                tt_(x[:, t, j * SW:(j + 1) * SW], half(s, t), x[:, t, j * SW:(j + 1) * SW], ALU.add)\
                    .then_inc(*half_read(s))

        norm_scale(vec, "ffn", x)
        unit_lo(vec, SLAB["ffn"], 0, 0)
        x_parts(vec, "ffn", xT, xT_hi, xT_lo)
        for q in (1, 2):
            unit_lo(vec, SLAB["ffn"], 0, q)
        units_vec(vec, SLAB["ffn"], FF // SW, 0, None)
        norm_scale(vec, "mem", mem, mem)

        def extra_lo(start, end):
            for n in range(start, end):
                unit_lo(vec, SLAB["ffn"], 0, 3 * (FF // SW) + n)

        extra_lo(0, 1)
        for b in (0, 1):
            vec.wait_ge(slab_used, SLAB["ffn"] + 3 * (FF // SW))
            vec.tensor_copy(x[:, 0, b * 512:(b + 1) * 512], bank[b][:, :]).then_inc(*b2_vec.did("h", b))

        x_parts(vec, "mem", memT, memT_hi, memT_lo)
        extra_lo(1, 3)
        norm_scale(vec, "final", x)
        vec.wait_ge(loads["g_fin"], 16)
        for t in range(TT):
            vec.wait_ge(*norm_vec.done("scale", "final", t))
            tt_(x[:, t, :], xn[:, t, :], g_fin[:, :], ALU.mult).then_inc(*b2_vec.did("x2", t))
        for n in range(3):
            ts_(scaled[:, n:n + 1], col("g_mq", n) if n < 2 else col("g_dq"), (ED if n < 2 else DD) ** -0.5, None,
                ALU.mult).then_inc(*b2_vec.did("scaled", n))
        extra_lo(3, 5)
        norm_scale(vec, "mix2", x)
        extra_lo(5, 7)
        x_parts(vec, "mix2", xT, xT_hi, xT_lo)
        extra_lo(7, 10)
        evicted(vec, SLAB["memkv"] + 3)
        head_norm(vec, "mk", mk, EH, ED)
        extra_lo(10, 11)
        for j in range(4):
            slab_out(vec, "mq", j)
            for t in range(TT):
                vec.tensor_copy(mq[:, t, j * SW:(j + 1) * SW], half(SLAB["mq"] + j, t))\
                   .then_inc(*half_read(SLAB["mq"] + j))
            extra_lo(11 + j, 12 + j)
        evicted(vec, SLAB["mq"] + 3)
        vec.wait_ge(*norm_vec.done("scaled", "mk"))
        head_norm(vec, "mq", mq, EH, ED)
        extra_lo(15, 16)
        attend_vec(vec, "mem", False, lambda n: None)
        def dq_out(j):
            slab_out(vec, "dq", j)
            for t in range(TT):
                vec.tensor_copy(dq[:, t, j * SW:(j + 1) * SW], half(SLAB["dq"] + j, t))\
                   .then_inc(*half_read(SLAB["dq"] + j))

        def branch_out(branch, j):
            name, z, _ = BRANCHES[branch]
            g_s, o_s = SLAB[f"gate_{name}{j}"], SLAB[f"o_{name}{j}"]
            vec.wait_ge(bank_read[BANKED[g_s] % 2], 2 * (BANKED[g_s] // 2 + 1))
            slab_out(vec, f"o_{name}{j}", 0)
            for n in range(2):
                dst = hT[:, n, :] if branch else mergedT[:, 2 * j + n, :]
                tt_(dst, half(o_s, n), gated[:, n, :], ALU.mult).then_inc(*half_read(o_s))
            if branch:
                vec.wait_ge(bank_read[BANKED[o_s] % 2], 2 * (BANKED[o_s] // 2 + 1))
                for n in range(2):
                    dst = mergedT[:, 2 * j + n, :]
                    tt_(dst, dst, hT[:, n, :], ALU.add)\
                        .then_inc(*(b2_vec.did("merged", name, j) if n else b2_vec.did("merged_", name, j)))
                vec.wait_ge(*b2_vec.done("merged", name, j))

        vec.wait_ge(*b2_pe.done("a_low"))
        vec.tensor_copy(a_low[:, :], bank[4][0:GRANK, 0:T]).then_inc(*b2_vec.did("a_low"))
        vec.wait_ge(loads["second"], 16 * 4)
        for t in range(TT):
            vec.wait_ge(*b2_pe.done("la", t))
            tt_(la[:, t, :], bank[5 + t][:, :], b_a2[:, :], ALU.add).then_inc(*b2_vec.did("z", t))
        vec.wait_ge(*b2_vec.done("z", 1))
        fl, fz_ = la[:, :, :].rearrange("p t n -> p (t n)"), lz[:, :, :].rearrange("p t n -> p (t n)")
        stt_(fz_, fl, -1.0, fl, ALU.mult, ALU.max).then_inc(*b2_vec.did("lz"))
        vec.wait_ge(*b2_act.done("ln"))
        stt_(fl, fl, 0.0, fz_, ALU.min, ALU.subtract).then_inc(*b2_vec.did("la"))
        evicted(vec, SLAB["gqk"] + 3)
        dq_out(0)
        q_, k_ = (gqk[:, n * GH:(n + 1) * GH, :].rearrange("p h t -> p (h t)") for n in range(2))
        ex_, ki_, cum_ = (a[:, :, :].rearrange("p h t -> p (h t)") for a in (ex, ki, cum))
        vec.wait_ge(*b2_act.done("ex", 1))
        stt_(q_, q_, GK ** -0.5, ex_, ALU.mult, ALU.mult).then_inc(*b2_vec.did("qd"))
        tt_(ki_, ki_, k_, ALU.mult).then_inc(*b2_vec.did("ki"))
        dq_out(1)
        vec.wait_ge(*b2_act.done("decay"))
        vec.wait_ge(*b2_vec.done("qd"))
        groups = cum_.rearrange("p (n c) -> p n c", c=GCHUNK)
        tt_(ex_.rearrange("p (n c) -> p n c", c=GCHUNK),
            bass.AP(tensor=groups.tensor, offset=groups.offset + GCHUNK - 1,
                    ap=[list(groups.ap[0]), [GCHUNK, GH * T // GCHUNK], [0, GCHUNK]]), groups, ALU.subtract)\
            .then_inc(*b2_vec.did("rest_"))
        vec.wait_ge(*b2_vec.done("rest_"))
        vec.tensor_copy(cum_, ex_).then_inc(*b2_vec.did("rest"))
        vec.wait_ge(*b2_act.done("ex", 2))
        vec.wait_ge(*b2_vec.done("ki"))
        tt_(k_, k_, ex_, ALU.mult).then_inc(*b2_vec.did("ke"))
        for t in range(TT):
            vec.wait_ge(*b2_pe.done("att", t))
            stt_(att[:, t, :, :], bank[4 + t][:, :].rearrange("p (h q) -> p h q", h=GH), 3e38,
                 spread(tri64[:, :], (0, GH), (1, P)), ALU.min, ALU.mult).then_inc(*b2_vec.did("att", t))
        dq_out(2)
        dq_out(3)
        for n in range(3):
            vec.wait_ge(*b2_pe.done("state", n))
            if n:
                vec.wait_ge(*b2_vec.done("state", n - 1))
            for h in range(GH):
                src = bank[2 + 2 * n + h // 2][:, (h % 2) * GV:(h % 2 + 1) * GV]
                step = b2_vec.did("state", n) if h == GH - 1 else b2_vec.did("state_", n, h)
                if n == 0:
                    vec.tensor_copy(state[:, n, h, :], src).then_inc(*step)
                else:
                    stt_(state[:, n, h, :], state[:, n - 1, h, :], decay[:, h, n:n + 1], src, ALU.mult, ALU.add)\
                        .then_inc(*step)
        for t in range(TT):
            for b in range(2):
                vec.wait_ge(*b2_pe.done("o", t, 2 * b + 1, 1))
                vec.tensor_copy(xn[:, t, b * 512:(b + 1) * 512], bank[4 + 2 * t + b][:, :])\
                   .then_inc(*b2_vec.did("o_raw", t, b))
        vec.wait_ge(*b2_vec.done("o_raw", 1, 1))
        head_norm(vec, "gla", xn, GH, GV)
        evicted(vec, SLAB["gvg"] + 7)
        vec.wait_ge(*norm_vec.done("scaled", "gla"))
        xn_, gg_ = (a[:, :, :].rearrange("p t n -> p (t n)") for a in (xn, gg))
        tt_(xn_, xn_, gg_, ALU.mult).then_inc(*b2_vec.did("gated"))
        vec.wait_ge(*b2_pe.done("ikw"))
        vec.tensor_copy(ikw[:, :, :], bank[2][:, 0:TT * 72].rearrange("p (t n) -> p t n", t=TT))\
           .then_inc(*b2_vec.did("ikw"))
        branch_out(0, 0)
        evicted(vec, SLAB["dq"] + 3)
        head_norm(vec, "dq", dq, DH, DD)
        branch_out(0, 1)
        evicted(vec, SLAB["dkv"] + 1)
        vec.wait_ge(*norm_vec.done("scaled", "dq"))
        head_norm(vec, "dk", dk, DG, DD)
        vec.wait_ge(*b2_vec.done("ikw"))
        vec.wait_ge(*norm_vec.done("scaled", "dk"))
        for t in range(TT):
            tt_(sq[:, t, 0:IDIM], ikw[:, t, 0:IDIM], ikw[:, t, 0:IDIM], ALU.mult).then_inc(*b2_vec.did("ik_sq", t))
        vec.wait_ge(*b2_vec.done("ik_sq", 1))
        vec.tensor_reduce(s16[:, 0, 0:TT], sq[:, 0:TT, 0:IDIM], AX.X, ALU.add).then_inc(*b2_vec.did("ik_sum"))
        vec.wait_ge(*b2_vec.done("ik_sum"))
        ts_(s16[:, 0, 0:TT], s16[:, 0, 0:TT], 1.0 / IDIM, EPS, ALU.mult, ALU.add).then_inc(*norm_vec.did("mean", "ik"))
        vec.wait_ge(*norm_pool.done("root", "ik"))
        for t in range(TT):
            for a in range(2):
                ts_(ik2[:, t, a, :], ikw[:, t, 0:IDIM], s16[:, 0, t:t + 1], None, ALU.mult)\
                    .then_inc(*(b2_vec.did("ik2") if t and a else b2_vec.did("ik2_", t, a)))
        ts_(ikw[:, :, IDIM:], ikw[:, :, IDIM:], IH ** -0.5 * IDIM ** -0.5, None, ALU.mult).then_inc(*b2_vec.did("iw"))
        vec.wait_ge(*b2_vec.done("iw"))
        for t in range(TT):
            K = (t + 1) * P
            vec.wait_ge(*b2_act.done("relu", t))
            for h in range(IH):
                w = ikw[:, t, IDIM + h:IDIM + h + 1]
                if h == 0:
                    ts_(score[:, t, 0:K], relu[:, h, 0:K], w, None, ALU.mult).then_inc(*b2_vec.did("idx", t, h))
                    continue
                vec.wait_ge(*b2_vec.done("idx", t, h - 1))
                stt_(score[:, t, 0:K], relu[:, h, 0:K], w, score[:, t, 0:K], ALU.mult, ALU.add)\
                    .then_inc(*b2_vec.did("idx", t, h))
        for t in range(TT):
            K = (t + 1) * P
            sc_, mask = score[:, t, 0:K], causal[:, T - K:T]
            vec.wait_ge(*b2_vec.done("idx", t, IH - 1))
            tt_(sc_, sc_, mask, ALU.add).then_inc(*b2_vec.did("allowed", t))
            vec.wait_ge(*b2_vec.done("allowed", t))
            for r in range(TOPK // 8):
                vec.max(best[:, t, :], sc_).then_inc(*b2_vec.did("max", t, r))
                vec.wait_ge(*b2_vec.done("max", t, r))
                vec.match_replace(sc_, best[:, t, :], sc_, MARK).then_inc(*b2_vec.did("match", t, r))
                vec.wait_ge(*b2_vec.done("match", t, r))
            ts_(pick[:, t, 0:K], sc_, MARK, NEG, ALU.not_equal, ALU.mult).then_inc(*b2_vec.did("picked", t))
            vec.wait_ge(*b2_vec.done("picked", t))
            tt_(pick[:, t, 0:K], pick[:, t, 0:K], mask, ALU.min).then_inc(*b2_vec.did("pick", t))
            branch_out(0, 2 + t)
        vec.wait_ge(*b2_vec.done("pick", 1))
        attend_vec(vec, "dsa", True, lambda n: branch_out(1, n))
        for j in range(4):
            branch_out(2, j)
        for j in range(4):
            s = SLAB["out2"] + j
            slab_out(vec, "out2", j)
            for t in range(TT):
                tt_(x[:, t, j * SW:(j + 1) * SW], half(s, t), x[:, t, j * SW:(j + 1) * SW], ALU.add)\
                    .then_inc(*half_read(s))

        norm_scale(vec, "ffn2", x)
        unit_lo(vec, SLAB["moe"], FF // SW, 0)
        x_parts(vec, "ffn2", xT, xT_hi, xT_lo)
        for q in (1, 2):
            unit_lo(vec, SLAB["moe"], FF // SW, q)
        steps = [0]

        def then(ins):
            steps[0] += 1
            ins.then_inc(*b2_vec.did("route", steps[0]))
            vec.wait_ge(*b2_vec.done("route", steps[0]))

        R_ = NGRP + NEXP
        vec.wait_ge(*b2_pe.done("router"))
        vec.wait_ge(loads["router"], 16 * 3)
        then(tt_(rl[:, :, :], bank[2][:, 0:TT * R_].rearrange("p (t n) -> p t n", t=TT),
                 spread(b_r[:, :], (0, TT), (1, R_)), ALU.add))

        def first_best(value, best_, one):
            then(vec.tensor_reduce(best_, value, AX.X, ALU.max))
            then(tt_(r_key[:, :, :], value, along(best_, 4), ALU.is_equal))
            then(stt_(r_key[:, :, :], r_key[:, :, :], -16.0, spread(iota4[:, :], (0, TT), (1, 4)), ALU.mult, ALU.add))
            then(vec.tensor_reduce(r_s[:, 7, :], r_key[:, :, :], AX.X, ALU.min))
            then(tt_(one, r_key[:, :, :], along(r_s[:, 7, :], 4), ALU.is_equal))

        group = rl[:, :, 0:NGRP]
        first_best(group, r_s[:, 0, :], r_one[:, 0, :, :])
        tt_(r_tmp[:, :, 0:NGRP], group, along(r_s[:, 0, :], NGRP), ALU.subtract).then_inc(*b2_vec.did("rl"))
        vec.wait_ge(*b2_act.done("g_exp"))
        then(vec.tensor_reduce(r_s[:, 1, :], r_tmp[:, :, 0:NGRP], AX.X, ALU.add))
        then(vec.reciprocal(r_s[:, 1, :], r_s[:, 1, :]))
        for t in range(TT):
            then(tt_(r_tmp[:, t, :].rearrange("p (g e) -> p g e", g=NGRP),
                     rl[:, t, NGRP:].rearrange("p (g e) -> p g e", g=NGRP), along(r_one[:, 0, t, :], PERG), ALU.mult))
        then(vec.tensor_reduce(r_el[:, :, :], r_tmp[:, :, :].rearrange("p t (g e) -> p t e g", g=NGRP), AX.X, ALU.add))
        first_best(r_el[:, :, :], r_s[:, 2, :], r_one[:, 1, :, :])
        then(stt_(r_el[:, :, :], r_one[:, 1, :, :], NEG, r_el[:, :, :], ALU.mult, ALU.add))
        first_best(r_el[:, :, :], r_s[:, 3, :], r_one[:, 2, :, :])
        tt_(r_s[:, 4, :], r_s[:, 3, :], r_s[:, 2, :], ALU.subtract).then_inc(*b2_vec.did("l2"))
        vec.wait_ge(*b2_act.done("e_exp"))
        then(ts_(r_s[:, 6, :], r_s[:, 5, :], 1.0, None, ALU.add))
        then(vec.reciprocal(r_s[:, 6, :], r_s[:, 6, :]))
        then(tt_(r_s[:, 6, :], r_s[:, 6, :], r_s[:, 1, :], ALU.mult))
        then(tt_(r_s[:, 5, :], r_s[:, 5, :], r_s[:, 6, :], ALU.mult))
        then(tt_(r_one[:, 1, :, :], r_one[:, 1, :, :], along(r_s[:, 6, :], 4), ALU.mult))
        then(tt_(r_one[:, 2, :, :], r_one[:, 2, :, :], along(r_s[:, 5, :], 4), ALU.mult))
        then(tt_(r_el[:, :, :], r_one[:, 1, :, :], r_one[:, 2, :, :], ALU.add))
        for t in range(TT):
            tt_(comb[:, t, :].rearrange("p (g e) -> p g e", g=NGRP), along(r_one[:, 0, t, :], PERG),
                spread(r_el[:, t, :], (0, NGRP), (1, PERG)), ALU.mult).then_inc(*b2_vec.did("comb", t))
        vec.wait_ge(*b2_act.done("comb", 7))
        units_vec(vec, SLAB["moe"], NEXP, FF // SW, comb_all[:, :, :].rearrange("p e t -> p (e t)"))
        for b in (0, 1):
            vec.wait_ge(slab_used, SLAB["moe"] + 3 * NEXP)
            vec.tensor_copy(x[:, 0, b * 512:(b + 1) * 512], bank[b][:, :]).then_inc(*b2_vec.did("y", b))

    @block.tensor
    def _(pe):
        mm_ = pe.matmul
        pe.wait_ge(loads["const"], 16 * 6)

        def columns(tile):
            n = NROWS[tile]
            pe.wait_ge(loads["rows2" if tile else "rows"], 16 * ROW_LOADS[tile])
            pe.transpose(bank[2 + tile][:, 0:n], rows[0:n, tile, :], ident[0:n, 0:n])\
              .then_inc(*setup_pe.did("cols", tile))

        columns(0)
        norm_turn(pe, "mix")
        pe.wait_ge(loads["rel"], 16 * 5)
        mm_(bank[3][0:NH, 0:REV], rel[:, :], oh_rev[:, :], start=True, stop=True).then_inc(*setup_pe.did("rev"))
        pe.wait_ge(*setup_vec.done("cols", 0))
        for t in range(TT):
            for c in range(NCMP):
                at = OH_CMP0 + t * P - CMP_STRIDE * c - (CMP_BLOCK - 1)
                n = (t * NCMP + c) * NH
                ins = mm_(bank[2][:, n:n + NH], oh_cmp[:, at:at + P], rel[:, :], start=True, stop=True)
        ins.then_inc(*setup_pe.did("cmp_bias"))
        pe.wait_ge(*setup_vec.done("rev"))
        columns(1)
        pe.wait_ge(*norm_act.done("gain", "mix", KT - 1))
        slabs(pe, "qk", slab_rows, xT)
        slabs(pe, "vo", slab_tokens, xT)
        pe.wait_ge(loads["small"], 32)
        for t in range(TT):
            for k in range(KT):
                ins = mm_(bank[4][:, t * 32:(t + 1) * 32], xT[:, k, t * P:(t + 1) * P], small[:, k, 0:32],
                          start=(k == 0), stop=(k == KT - 1))
        ins.then_inc(*in1_pe.did("small"))
        slabs(pe, "nq", slab_rows, xT, 0, 2)
        for j in range(3):
            s = SLAB["kv"] + j
            slab_in(pe, s)
            if j == 0:
                slab_rows(pe, s, xT).then_inc(slab_used, 1)
                continue
            for k in range(KT):
                mm_(half(s, 0), ring[:, s % RING, k, 0:P], xT[:, k, :], start=(k == 0), stop=(k == KT - 1))
            for t in range(TT):
                for k in range(KT):
                    ins = mm_(half(s, 1)[:, t * P:(t + 1) * P], xT[:, k, t * P:(t + 1) * P],
                              ring[:, s % RING, k, P:2 * P], start=(k == 0), stop=(k == KT - 1))
            ins.then_inc(slab_used, 1)
        slabs(pe, "merge", slab_rows, xT, 0, 2)

        pe.wait_ge(loads["cmp"], 16 * 5)
        pe.wait_ge(*ns_vec.done("blk", 1, 1))
        pe.wait_ge(*in1_vec.done("gate_in"))
        for j in range(2):
            for n in range(CMP_PAIRS):
                ins = mm_(bank[4][:, j * NG * NCMP:(j + 1) * NG * NCMP], w_cmp1[:, j, n, :],
                          blk[:, j, n, :, :].rearrange("p g c -> p (g c)"),
                          start=(n == 0), stop=(n == CMP_PAIRS - 1))
        ins.then_inc(*ns_pe.did("hid"))
        slabs(pe, "merge", slab_rows, xT, 2, 3)
        pe.wait_ge(*ns_vec.done("hid"))
        mm_(bank[5][:, 0:NG * NCMP], w_cmp2k[:, :, :].rearrange("p a d -> p (a d)"), hid[:, 0, :],
            start=True, stop=True)
        for g in range(NG):
            ins = mm_(bank[5][0:NCMP, 128 + g * ND:128 + (g + 1) * ND], hid[:, 1, g * NCMP:(g + 1) * NCMP],
                      w_cmp2v[:, :], start=True, stop=True)
        ins.then_inc(*ns_pe.did("kcT"))

        pe.wait_ge(*setup_pool.done("ones"))
        pe.wait_ge(*ml_vec.done("lf"))
        mm_(bank[4][:, 0:8], tri[:, :], lf[:, :, :].rearrange("p t h -> p (t h)"), start=True, stop=True)
        mm_(bank[4][:, 8:16], ones[:, :], lf[:, :, :].rearrange("p t h -> p (t h)"), start=True, stop=True)\
            .then_inc(*ml_pe.did("bc"))
        pe.wait_ge(*ml_vec.done("silu", 7))
        pe.wait_ge(*ml_vec.done("bc"))
        for c, b in enumerate((4, 7)):
            for h in range(MH):
                ins = mm_(bank[b][:, h * P:(h + 1) * P], qk[:, 4 + h, c * P:(c + 1) * P], qk[:, h, c * P:(c + 1) * P],
                          start=True, stop=True)
            ins.then_inc(*ml_pe.did("st", c))
        pe.wait_ge(*ml_vec.done("cc"))
        pe.wait_ge(*ns_vec.done("vc"))
        for c in range(TT):
            for h in range(MH):
                ins = mm_(bank[5 + c][:, h * P:(h + 1) * P], spread(cc[:, c, h:h + 1], (0, P)), ident[:, :],
                          start=True, stop=True)
            ins.then_inc(*ml_pe.did("crow", c))
        slabs(pe, "merge", slab_rows, xT, 3, 4)
        pe.wait_ge(*ml_vec.done("mm", 1))
        for c in range(TT):
            pe.wait_ge(*ml_vec.done("masked", c))
            for h in range(MH):
                ins = mm_(bank[5 + c][:, h * P:(h + 1) * P], spread(mm[:, c, h:h + 1], (0, P)), ident[:, :],
                          start=True, stop=True)
            ins.then_inc(*ml_pe.did("mrow", c))
        slabs(pe, "merge", slab_rows, xT, 4, 5)
        pe.wait_ge(*ml_vec.done("yy", 0))
        for h in range(MH):
            ins = pe.transpose(bank[5][:, h * P:(h + 1) * P], qk[:, 4 + h, 0:P], ident[:, :])
        ins.then_inc(*ml_pe.did("k_tok"))
        pe.wait_ge(*ml_act.done("k_tok"))
        pe.wait_ge(*ml_vec.done("wv"))
        pe.wait_ge(*ml_vec.done("yy", 1))
        E1 = MD + 1
        for n, b in enumerate((6, 4)):
            if n:
                pe.wait_ge(*ml_vec.done("pT", 0))
            for i in range(2):
                ins = mm_(bank[b][:, i * E1:(i + 1) * E1], k_tok[:, 2 * n + i, :], wv[:, 2 * n + i, :],
                          start=True, stop=True)
            ins.then_inc(*ml_pe.did("c1", n))
        for c, banks in enumerate(((5, 7), (6, 4))):
            pe.wait_ge(*ml_vec.done("pT", 1))
            for n, b in enumerate(banks):
                if c:
                    pe.wait_ge(*ml_act.done("c1", n))
                for i in range(2):
                    h = 2 * n + i
                    ins = mm_(bank[b][:, i * E1:(i + 1) * E1], pT[:, c, h, :], v1[:, c, h, :], start=True, stop=True)
                ins.then_inc(*ml_pe.did("num", c, n))
        for n, b in enumerate((5, 7)):
            pe.wait_ge(*ml_act.done("num", 0, n))
            for i in range(2):
                h = 2 * n + i
                ins = mm_(bank[b][:, i * E1:(i + 1) * E1], qk[:, h, P:T], c1[:, h, :], start=True, stop=True)
            ins.then_inc(*ml_pe.did("inter", n))
        slabs(pe, "merge", slab_rows, xT, 5, 7)
        pe.wait_ge(*ml_vec.done("ym", 1))
        pe.wait_ge(*ml_act.done("num", 1, 1))
        for k in range(4):
            for t in range(TT):
                at = (k % 2) * T + t * P
                ins = pe.transpose(bank[(4, 6)[k // 2]][:, at:at + P], hn[:, t, k, :], ident[:, :])
            if k % 2:
                ins.then_inc(*ml_pe.did("yT", k // 2))

        pe.wait_ge(*ml_act.done("yT", 3))
        evicted(pe, SLAB["nq"] + 1)
        pe.wait_ge(*ns_vec.done("vc"))
        for t in range(TT):
            for h in range(NH):
                lo, at = ND * (h % 2), (t * NREP + h // 2) * NCMP
                ins = mm_(bank[6 + h % 2][:, at:at + NCMP], nqT[lo:lo + ND, h // 2, t * P:(t + 1) * P],
                          kcT[lo:lo + ND, (h // NREP) * NCMP:(h // NREP + 1) * NCMP], start=True, stop=True)
        ins.then_inc(*ns_pe.did("lc"))
        slabs(pe, "merge", slab_rows, xT, 7, 8)
        pe.wait_ge(*ns_vec.done("pc"))
        pe.wait_ge(*ml_vec.done("hh", 3))
        for n, b in enumerate((7, 4, 5, 6)):
            for i in range(4):
                ins = pe.transpose(bank[b][0:NCMP, i * P:(i + 1) * P], ec[:, n // 2, (n % 2) * 4 + i, :], ident[:, :])
            ins.then_inc(*ns_pe.did("pcT", n))
        pe.wait_ge(*ns_act.done("pcT", 3))
        pe.wait_ge(loads["twice"], 16 * 4)
        evicted(pe, SLAB["kv"] + 2)

        def logits(u):
            tt, g, br = u // 4, u // 2 % 2, u % 2
            K = (tt + 1) * P
            if u:
                pe.wait_ge(*ns_vec.done("lg", u - 1, 1))
            for i in range(2):
                for odd in range(2):
                    h = g * NREP + 2 * i + odd
                    ins = mm_(bank[4 + odd][:, i * K:(i + 1) * K],
                              nqT[odd * ND:(odd + 1) * ND, h // 2, tt * P:(tt + 1) * P],
                              kT[odd * ND:(odd + 1) * ND, br, g, 0:K], start=True, stop=True)
            ins.then_inc(*ns_pe.did("lg", u))

        logits(0)
        for u in range(8):
            tt, g, br = u // 4, u // 2 % 2, u % 2
            if u < 7:
                logits(u + 1)
            pe.wait_ge(*ns_vec.done("p", u))
            for kt in range(tt + 1):
                if u and kt <= (u - 1) // 4:
                    pe.wait_ge(*ns_act.done("aT", u - 1, kt))
                for i in range(NREP):
                    ins = pe.transpose(bank[6 + kt][:, i * P:(i + 1) * P], lg[:, u % 2, i, kt * P:(kt + 1) * P],
                                       ident[:, :])
                ins.then_inc(*ns_pe.did("aT", u, kt))
            if br == 1:
                pe.wait_ge(*ns_act.done("aT", u, tt))
                for odd in range(2):
                    dst = bank[2 + tt][odd * ND:(odd + 1) * ND, g * T:(g + 1) * T]
                    mm_(dst, vc[:, g, :], pcT[:, tt, g * NREP + odd:(g + 1) * NREP:2, :], start=True, stop=False)
                    for b in range(2):
                        for kt in range(tt + 1):
                            ins = mm_(dst, v_sw[:, b, kt, g * ND:(g + 1) * ND], aT[:, b, kt, 2 * odd:2 * odd + 2, :],
                                      start=False, stop=(b == 1 and kt == tt))
                ins.then_inc(*ns_pe.did("av", u // 2))

        pe.wait_ge(*ns_act.done("yT", 1))
        for j in range(4):
            s = SLAB["branch"] + j
            pe.wait_ge(slab_loaded[s % RING], 16 * (s // RING + 1))
            if j >= 2:
                pe.wait_ge(*mix_vec.done("n", j - 2))
            for z in range(2):
                for n in range(2):
                    for k in range(4):
                        ins = mm_(bank[4 + 2 * (j % 2) + z][:, n * T:(n + 1) * T],
                                  ring[:, s % RING, 4 * z + k, n * P:(n + 1) * P], ysT[:, 4 * z + k, :],
                                  start=(k == 0), stop=(k == 3))
            ins.then_inc(slab_used, 1)
        pe.wait_ge(*mix_vec.done("mix", 3))
        slabs(pe, "out", slab_tokens, mixT)

        norm_turn(pe, "ffn")
        pe.wait_ge(*norm_act.done("gain", "ffn", KT - 1))
        units_pe(pe, SLAB["ffn"], FF // SW, 0)

        turn(pe, "mem", mem, KT, norm_vec.done("scale", "mem", TT - 1))
        pe.wait_ge(*b2_vec.done("h", 1))
        split_slabs(pe, "memkv", True, memT_hi, memT_lo, 0, 4)
        norm_turn(pe, "mix2")
        split_slabs(pe, "memkv", True, memT_hi, memT_lo, 4, 8)
        pe.wait_ge(*norm_act.done("gain", "mix2", KT - 1))
        x_parts_wait(pe, "mix2")
        split_slabs(pe, "mq", True, xT_hi, xT_lo, 0, 1)
        turn(pe, "mk", mk, 8, norm_vec.done("scaled", "mk"))
        split_slabs(pe, "mq", True, xT_hi, xT_lo, 1, 4)
        split_slabs(pe, "gqk", False, xT_hi, xT_lo, 0, 3)
        pe.wait_ge(*norm_act.done("gain", "mk", 7))
        turn(pe, "mq", mq, 8, norm_vec.done("scaled", "mq"))
        split_slabs(pe, "gqk", False, xT_hi, xT_lo, 3, 4)
        pe.wait_ge(*norm_act.done("gain", "mq", 7))
        evicted(pe, SLAB["memkv"] + 7)
        attend(pe, "mem",
               lambda tt, g: [[(bank[4 + i // 2][:, (i % 2) * T:(i % 2 + 1) * T],
                                [(mqT[:, 2 * i + v, tt * P:(tt + 1) * P], mkT[:, 2 * i + v, :]) for v in range(2)])
                               for i in range(4)]],
               lambda tt, g: [(bank[2 + i // 2][:, (i % 2) * T + v * P:(i % 2) * T + (v + 1) * P],
                               [(mv[:, kt, i * ED + v * P:i * ED + (v + 1) * P], probT[:, kt, i, :])
                                for kt in range(2)]) for i in range(4) for v in range(2)],
               lambda n: slabs(pe, "gvg", slab_tokens, xT, 2 * n, 2 * n + 2))

        slabs(pe, "gvg", slab_tokens, xT, 4, 6)
        pe.wait_ge(loads["narrow"], 16 * 2)
        pe.wait_ge(*b2_act.done("o", "mem", 1, 0))
        for k in range(KT):
            ins = mm_(bank[4][0:GRANK, 0:T], small[:, k, 0:GRANK], xT[:, k, :], start=(k == 0), stop=(k == KT - 1))
        ins.then_inc(*b2_pe.did("a_low"))
        slabs(pe, "gvg", slab_tokens, xT, 6, 7)
        pe.wait_ge(*b2_vec.done("a_low"))
        pe.wait_ge(loads["second"], 16 * 4)
        for t in range(TT):
            mm_(bank[5 + t][:, :], a_low[:, t * P:(t + 1) * P], w_a2[:, :], start=True, stop=True)\
                .then_inc(*b2_pe.did("la", t))
        slabs(pe, "gvg", slab_tokens, xT, 7, 8)
        pe.wait_ge(*b2_vec.done("la"))
        for t in range(TT):
            for h in range(GH):
                ins = mm_(bank[5 + t][:, h * P:(h + 1) * P], la[:, t, h * GK:(h + 1) * GK], tri64[:, :],
                          start=True, stop=True)
            ins.then_inc(*b2_pe.did("cum", t))
        slabs(pe, "dq", slab_tokens, xT, 0, 2)
        pe.wait_ge(*b2_vec.done("ki"))
        pe.wait_ge(*b2_vec.done("qd"))
        pe.wait_ge(*b2_act.done("cum", 1))
        for t in range(TT):
            for h in range(GH):
                ins = mm_(bank[4 + t][:, h * P:(h + 1) * P], ki[:, h, t * P:(t + 1) * P],
                          gqk[:, h, t * P:(t + 1) * P], start=True, stop=True)
            ins.then_inc(*b2_pe.did("att", t))
        slabs(pe, "dq", slab_tokens, xT, 2, 3)
        pe.wait_ge(*b2_vec.done("ke"))
        for t in range(TT):
            for h in range(GH):
                ins = pe.transpose(bank[6 + t][:, h * P:(h + 1) * P], gqk[:, GH + h, t * P:(t + 1) * P], ident[:, :])
            ins.then_inc(*b2_pe.did("ke_tok", t))
        slabs(pe, "dq", slab_tokens, xT, 3, 4)
        pe.wait_ge(*b2_act.done("ke_tok", 1))
        pe.wait_ge(*b2_vec.done("att", 1))
        evicted(pe, SLAB["gvg"] + 7)
        for n in range(3):
            lo = (n % 2) * GCHUNK
            for h in range(GH):
                ins = mm_(bank[2 + 2 * n + h // 2][:, (h % 2) * GV:(h % 2 + 1) * GV],
                          ke_tok[lo:lo + GCHUNK, n // 2, h, :], gv[lo:lo + GCHUNK, n // 2, h * GV:(h + 1) * GV],
                          start=True, stop=True)
            ins.then_inc(*b2_pe.did("state", n))
        slabs(pe, "dkv", slab_tokens, xT, 0, 1)
        pe.wait_ge(*b2_vec.done("state", 2))
        for t in range(TT):
            for h in range(GH):
                dst = bank[4 + 2 * t + h // 2][:, (h % 2) * GV:(h % 2 + 1) * GV]
                mm_(dst, att[:, t, h, :], gv[:, t, h * GV:(h + 1) * GV], start=True, stop=False,
                    skip_group_check=True)
                for c in range(2):
                    n = 2 * t + c
                    if n:
                        mm_(dst[c * GCHUNK:(c + 1) * GCHUNK, :], gqk[:, h, n * GCHUNK:(n + 1) * GCHUNK],
                            state[:, n - 1, h, :], start=False, stop=(c == 1), skip_group_check=True)\
                            .then_inc(*b2_pe.did("o", t, h, c))
        slabs(pe, "dkv", slab_tokens, xT, 1, 2)
        slabs(pe, "iq", slab_rows, xT, 0, 2)

        def gate_and_out(branch, j):
            name = BRANCHES[branch][0]
            slabs(pe, f"gate_{name}{j}", slab_rows, xT, 0, 1)
            slabs(pe, f"o_{name}{j}", slab_rows, (o_mT, o_gT, o_dT)[branch], 0, 1)

        for t in range(TT):
            for k in range(KT):
                ins = mm_(bank[2][:, t * 72:(t + 1) * 72], xT[:, k, t * P:(t + 1) * P], small[:, k, 16:88],
                          start=(k == 0), stop=(k == KT - 1))
        ins.then_inc(*b2_pe.did("ikw"))
        gate_and_out(0, 0)
        turn(pe, "gla", xn, 8, b2_vec.done("gated"), b2_vec.done("o_raw", 1, 1))
        gate_and_out(0, 1)
        pe.wait_ge(*norm_act.done("gain", "gla", 7))
        turn(pe, "dq", dq, 8, norm_vec.done("scaled", "dq"))
        pe.wait_ge(*norm_act.done("gain", "dq", 7))
        turn(pe, "dk", dk, 2, norm_vec.done("scaled", "dk"))
        pe.wait_ge(*norm_act.done("gain", "dk", 1))
        turn(pe, "ik", ik2[:, :, :, :].rearrange("p t a d -> p t (a d)"), 1, b2_vec.done("ik2"))
        pe.wait_ge(*norm_act.done("gain", "ik", 0))
        evicted(pe, SLAB["iq"] + 1)
        for t in range(TT):
            K = (t + 1) * P
            if t:
                pe.wait_ge(*b2_act.done("relu", 0))
            for h in range(IH):
                lo, i = (h % 2) * IDIM, h // 2
                ins = mm_(bank[2 + h % 2 + 2 * (i // 2)][:, (i % 2) * T:(i % 2) * T + K],
                          iqT[lo:lo + IDIM, h // 2, t * P:(t + 1) * P], ikT[lo:lo + IDIM, 0:K],
                          start=True, stop=True)
            ins.then_inc(*b2_pe.did("idx", t))
        gate_and_out(0, 2)
        gate_and_out(0, 3)
        pe.wait_ge(*b2_act.done("relu", 1))
        attend(pe, "dsa",
               lambda tt, g: [[(bank[4 + i // (4 // (tt + 1))][:, (i % (4 // (tt + 1))) * (tt + 1) * P:
                                                               (i % (4 // (tt + 1)) + 1) * (tt + 1) * P],
                                [(dqT[:, g * DREP + i, tt * P:(tt + 1) * P], dkT[:, g, 0:(tt + 1) * P])])
                               for i in range(4)]],
               lambda tt, g: [(bank[2][:, :], [(dv[:, kt, g * DD:(g + 1) * DD], probT[:, kt, :, :])
                                               for kt in range(tt + 1)])],
               lambda n: gate_and_out(1, n))

        pe.wait_ge(*b2_act.done("o", "dsa", 1, 1))
        for j in range(4):
            gate_and_out(2, j)
        pe.wait_ge(*b2_vec.done("merged", "dsa", 3))
        slabs(pe, "out2", slab_tokens, mergedT)

        norm_turn(pe, "ffn2")
        pe.wait_ge(*norm_act.done("gain", "ffn2", KT - 1))
        pe.wait_ge(loads["router"], 16 * 3)
        R_ = NGRP + NEXP
        for t in range(TT):
            for k in range(KT):
                ins = mm_(bank[2][:, t * R_:(t + 1) * R_], xT[:, k, t * P:(t + 1) * P], small[:, k, 0:R_],
                          start=(k == 0), stop=(k == KT - 1))
        ins.then_inc(*b2_pe.did("router"))
        def shares():
            pe.wait_ge(*b2_vec.done("comb", 1))
            for e in range(NEXP):
                if e >= 4 and e % 2 == 0:
                    pe.wait_ge(*b2_act.done("comb", e // 2 - 2))
                for t in range(TT):
                    ins = mm_(bank[2 + e // 2 % 2][:, (e % 2) * T + t * P:(e % 2) * T + (t + 1) * P],
                              spread(comb[:, t, e:e + 1], (0, P)), ident[:, :], start=True, stop=True)
                if e % 2:
                    ins.then_inc(*b2_pe.did("comb", e // 2))
            pe.wait_ge(*b2_act.done("comb", 7))

        units_pe(pe, SLAB["moe"], NEXP, FF // SW, shares)


def kernel(**inputs):
    import concourse.bacc as bacc
    from concourse.bass_utils import run_bass_kernel_spmd

    arrays = {name: np.ascontiguousarray(a) for name, a in inputs.items()}
    arrays.update(constants())
    plan = {}
    for _ in range(2):
        nc = bacc.Bacc("TRN2", target_bir_lowering=False, num_devices=1)
        dram = {name: nc.dram_tensor("in_" + name, a.shape, mybir.dt.from_np(a.dtype), kind="ExternalInput").ap()
                for name, a in arrays.items()}
        dram["rev"] = nc.dram_tensor("rev_rows", [NH, REV], F32, kind="Internal").ap()
        dram["rev_copies"] = nc.dram_tensor("rev_copies", [NH, P, REV], F32, kind="Internal").ap()
        out = nc.dram_tensor("out_0", [1, T, D], F32, kind="ExternalOutput").ap()
        program(nc, dram, out, plan)
    r = run_bass_kernel_spmd(nc, [{"in_" + name: a for name, a in arrays.items()}], core_ids=[0])
    return r.results[0]["out_0"]
```
